# Optimizing a Trainium2 kernel written in Bass

```python
import math
import jax, jax.numpy as jnp
from jax import lax
import numpy as np

D_MODEL = 1024
BATCH = 1
SEQ = 1024
DEPTH = 1

GRID_W = 64
CTX_LEN = 256
LRU_WIDTH = 256
LRU_BLOCKS = 4
LRU_BLOCK = LRU_WIDTH // LRU_BLOCKS
CONV_W = 4
RG_C = 8.0
GQA_HEADS = 8
GQA_KV_HEADS = 2
GQA_HEAD_DIM = 64
DIFF_HEADS = 4
DIFF_QK_DIM = 32
DIFF_V_DIM = 64
MIX_WIDTH = LRU_WIDTH + GQA_HEADS * GQA_HEAD_DIM + DIFF_HEADS * DIFF_V_DIM
SPLIT_SIZES = (LRU_WIDTH, LRU_WIDTH, GQA_HEADS * GQA_HEAD_DIM, GQA_KV_HEADS * GQA_HEAD_DIM,
               GQA_KV_HEADS * GQA_HEAD_DIM, DIFF_HEADS * 2 * DIFF_QK_DIM, DIFF_HEADS * 2 * DIFF_QK_DIM,
               DIFF_HEADS * DIFF_V_DIM)
IN_WIDTH = sum(SPLIT_SIZES)
N_EXPERTS = 16
N_GROUPS = 4
EXPERTS_PER_GROUP = N_EXPERTS // N_GROUPS
TOP_K = 2
EXPERT_FF = 512
MOE_BLOCK = 128
Q_BLOCK = 128
ROPE_THETA = 10000.0
EPS = 1e-6
DEEPNORM_ALPHA = (2.0 * DEPTH) ** 0.25
DEEPNORM_BETA = (8.0 * DEPTH) ** -0.25

kernel_name = 'hybrid_diffusion_prefix_trunk'

def layer_norm(x, g, b):
    x32 = x.astype(jnp.float32)
    mu = jnp.mean(x32, axis=-1, keepdims=True)
    var = jnp.mean(jnp.square(x32 - mu), axis=-1, keepdims=True)
    return ((x32 - mu) * lax.rsqrt(var + EPS) * g + b).astype(x.dtype)

def rms_norm(x, g):
    x32 = x.astype(jnp.float32)
    return (x32 * lax.rsqrt(jnp.mean(x32 * x32, axis=-1, keepdims=True) + EPS) * g).astype(x.dtype)

def axial_rope_tables(n_tokens, dim):
    rows = n_tokens // GRID_W
    row = jnp.repeat(jnp.arange(rows, dtype=jnp.float32), GRID_W)
    col = jnp.tile(jnp.arange(GRID_W, dtype=jnp.float32), rows)
    n_freq = dim // 4
    inv = ROPE_THETA ** (-jnp.arange(n_freq, dtype=jnp.float32) / n_freq)
    ang = jnp.concatenate([row[:, None] * inv, col[:, None] * inv], axis=-1)
    return jnp.cos(ang), jnp.sin(ang)

def apply_rope(x, rope):
    cos, sin = rope
    xp = x.reshape(x.shape[:-1] + (x.shape[-1] // 2, 2)).astype(jnp.float32)
    x0, x1 = xp[..., 0], xp[..., 1]
    out = jnp.stack([x0 * cos - x1 * sin, x0 * sin + x1 * cos], axis=-1)
    return out.reshape(x.shape).astype(x.dtype)

def split_heads(z, n_heads, dim):
    b, s, _ = z.shape
    return z.reshape(b, s, n_heads, dim).transpose(0, 2, 1, 3)

def merge_heads(o):
    b, h, s, d = o.shape
    return o.transpose(0, 2, 1, 3).reshape(b, s, h * d)

def centred_dwconv(x, w, b):
    s = x.shape[1]
    left = (CONV_W - 1) // 2
    xp = jnp.pad(x, ((0, 0), (left, CONV_W - 1 - left), (0, 0)))
    y = b
    for k in range(CONV_W):
        y = y + xp[:, k:k + s] * w[k]
    return y

def linear_scan(a, b, h0, reverse):
    if h0 is not None:
        edge = -1 if reverse else 0
        b = b.at[:, edge].add(a[:, edge] * h0)
    def combine(l, r):
        return l[0] * r[0], r[0] * l[1] + r[1]
    _, h = lax.associative_scan(combine, (a, b), axis=1, reverse=reverse)
    return h

def rglru_scan(u, w_a, b_a, w_x, b_x, lam, h0, reverse):
    bsz, s, w = u.shape
    ub = u.reshape(bsz, s, LRU_BLOCKS, LRU_BLOCK)
    r = jax.nn.sigmoid(jnp.einsum('bsnc,ncd->bsnd', ub, w_a).reshape(bsz, s, w) + b_a)
    i = jax.nn.sigmoid(jnp.einsum('bsnc,ncd->bsnd', ub, w_x).reshape(bsz, s, w) + b_x)
    log_a = (-RG_C * r.astype(jnp.float32)) * jax.nn.softplus(-lam.astype(jnp.float32))
    a = jnp.exp(log_a)
    mult = jnp.sqrt(-jnp.expm1(2.0 * log_a))
    return linear_scan(a, mult * (i * u).astype(jnp.float32), h0, reverse)

def gqa_heads(zq, zk, zv, q_g, k_g, rope):
    q = rms_norm(split_heads(zq, GQA_HEADS, GQA_HEAD_DIM), q_g)
    k = rms_norm(split_heads(zk, GQA_KV_HEADS, GQA_HEAD_DIM), k_g)
    v = split_heads(zv, GQA_KV_HEADS, GQA_HEAD_DIM)
    if rope is not None:
        q = apply_rope(q, rope)
        k = apply_rope(k, rope)
    return q, k, v

def gqa_attend(q, k, v):
    bsz, h, sq, dh = q.shape
    kvh = k.shape[1]
    g = h // kvh
    nblk = sq // Q_BLOCK
    qb = jnp.moveaxis(q.reshape(bsz, kvh, g, nblk, Q_BLOCK, dh), 3, 0)
    scale = dh ** -0.5
    def body(qblk):
        s = jnp.einsum('bkgqd,bksd->bkgqs', qblk, k).astype(jnp.float32) * scale
        p = jax.nn.softmax(s, axis=-1).astype(v.dtype)
        return jnp.einsum('bkgqs,bksd->bkgqd', p, v)
    o = lax.map(body, qb)
    return jnp.moveaxis(o, 0, 3).reshape(bsz, h, sq, dh)

def diff_heads(zq, zk, zv, rope):
    bsz, s, _ = zq.shape
    q = zq.reshape(bsz, s, DIFF_HEADS, 2, DIFF_QK_DIM).transpose(0, 2, 3, 1, 4)
    k = zk.reshape(bsz, s, DIFF_HEADS, 2, DIFF_QK_DIM).transpose(0, 2, 3, 1, 4)
    v = split_heads(zv, DIFF_HEADS, DIFF_V_DIM)
    if rope is not None:
        q = apply_rope(q, rope)
        k = apply_rope(k, rope)
    return q, k, v

def diff_attend(q, k, v, lam):
    bsz, h, _, sq, dq = q.shape
    dv = v.shape[-1]
    nblk = sq // Q_BLOCK
    qb = jnp.moveaxis(q.reshape(bsz, h, 2, nblk, Q_BLOCK, dq), 3, 0)
    scale = dq ** -0.5
    def body(qblk):
        s = jnp.einsum('bhmqd,bhmsd->bhmqs', qblk, k).astype(jnp.float32) * scale
        p = jax.nn.softmax(s, axis=-1)
        w = (p[:, :, 0] - lam * p[:, :, 1]).astype(v.dtype)
        return jnp.einsum('bhqs,bhsd->bhqd', w, v)
    o = lax.map(body, qb)
    return jnp.moveaxis(o, 0, 2).reshape(bsz, h, sq, dv)

def token_mixer(h_lat, h_ctx, w_in, conv_w, conv_b, rg_wa, rg_ba, rg_wx, rg_bx, rg_lam,
                q_norm_g, k_norm_g, diff_lambda, diff_subln_g, w_out, rope_g, rope_d, lam_init, need_ctx):
    points = np.cumsum(SPLIT_SIZES)[:-1].tolist()
    ax_l, ag_l, gq_l, gk_l, gv_l, dq_l, dk_l, dv_l = jnp.split(h_lat @ w_in, points, axis=-1)
    ax_c, ag_c, gq_c, gk_c, gv_c, dq_c, dk_c, dv_c = jnp.split(h_ctx @ w_in, points, axis=-1)

    u_l = centred_dwconv(ax_l, conv_w, conv_b)
    u_c = centred_dwconv(ax_c, conv_w, conv_b)
    h_l = jnp.zeros(u_l.shape, jnp.float32)
    h_c = jnp.zeros(u_c.shape, jnp.float32)
    for d, rev in enumerate((False, True)):
        hc = rglru_scan(u_c, rg_wa[d], rg_ba[d], rg_wx[d], rg_bx[d], rg_lam[d], None, rev)
        h0 = hc[:, 0] if rev else hc[:, -1]
        h_l = h_l + rglru_scan(u_l, rg_wa[d], rg_ba[d], rg_wx[d], rg_bx[d], rg_lam[d], h0, rev)
        if need_ctx:
            h_c = h_c + hc
    ya_l = jax.nn.gelu(ag_l) * h_l.astype(ag_l.dtype)

    q_l, k_l, v_l = gqa_heads(gq_l, gk_l, gv_l, q_norm_g, k_norm_g, rope_g)
    q_c, k_c, v_c = gqa_heads(gq_c, gk_c, gv_c, q_norm_g, k_norm_g, None)
    yb_l = merge_heads(gqa_attend(q_l, jnp.concatenate([k_c, k_l], axis=2), jnp.concatenate([v_c, v_l], axis=2)))

    dl = diff_lambda.astype(jnp.float32)
    lam = jnp.exp(jnp.sum(dl[0] * dl[1])) - jnp.exp(jnp.sum(dl[2] * dl[3])) + lam_init
    dq_h, dk_h, dv_h = diff_heads(dq_l, dk_l, dv_l, rope_d)
    cq_h, ck_h, cv_h = diff_heads(dq_c, dk_c, dv_c, None)
    oc_l = diff_attend(dq_h, jnp.concatenate([ck_h, dk_h], axis=3), jnp.concatenate([cv_h, dv_h], axis=2), lam)
    yc_l = merge_heads(rms_norm(oc_l, diff_subln_g) * (1.0 - lam_init))

    out_l = jnp.concatenate([ya_l, yb_l, yc_l], axis=-1) @ w_out
    if not need_ctx:
        return out_l, None
    ya_c = jax.nn.gelu(ag_c) * h_c.astype(ag_c.dtype)
    yb_c = merge_heads(gqa_attend(q_c, k_c, v_c))
    yc_c = merge_heads(rms_norm(diff_attend(cq_h, ck_h, cv_h, lam), diff_subln_g) * (1.0 - lam_init))
    out_c = jnp.concatenate([ya_c, yb_c, yc_c], axis=-1) @ w_out
    return out_l, out_c

def route(h, router_w, router_b):
    t = h.shape[0]
    probs = jax.nn.softmax((h @ router_w).astype(jnp.float32), axis=-1)
    sel = (probs + router_b.astype(jnp.float32)).reshape(t, N_GROUPS, EXPERTS_PER_GROUP)
    grp_score = jnp.sum(lax.top_k(sel, TOP_K)[0], axis=-1)
    g_idx = jnp.argmax(grp_score, axis=-1)
    in_grp = jnp.take_along_axis(sel, g_idx[:, None, None], axis=1)[:, 0]
    _, local = lax.top_k(in_grp, TOP_K)
    experts = g_idx[:, None] * EXPERTS_PER_GROUP + local
    w = jnp.take_along_axis(probs, experts, axis=1)
    return experts, w / jnp.sum(w, axis=-1, keepdims=True)

def moe_ffn(h, router_w, router_b, w_gate, w_up, w_down):
    t, d = h.shape
    experts, gates = route(h, router_w, router_b)
    n_assign = t * TOP_K
    flat_e = experts.reshape(n_assign)
    flat_tok = jnp.repeat(jnp.arange(t, dtype=jnp.int32), TOP_K)
    flat_g = gates.reshape(n_assign)
    order = jnp.argsort(flat_e)
    sorted_e = flat_e[order]
    counts = jnp.bincount(flat_e, length=N_EXPERTS)
    padded = (counts + MOE_BLOCK - 1) // MOE_BLOCK * MOE_BLOCK
    start = jnp.cumsum(counts) - counts
    pend = jnp.cumsum(padded)
    pstart = pend - padded
    dest = pstart[sorted_e] + jnp.arange(n_assign, dtype=jnp.int32) - start[sorted_e]
    n_rows = ((n_assign + MOE_BLOCK - 1) // MOE_BLOCK + N_EXPERTS) * MOE_BLOCK
    n_blk = n_rows // MOE_BLOCK
    row_tok = jnp.zeros((n_rows,), jnp.int32).at[dest].set(flat_tok[order])
    row_gate = jnp.zeros((n_rows,), h.dtype).at[dest].set(flat_g[order].astype(h.dtype))
    blk_expert = jnp.clip(jnp.searchsorted(pend, jnp.arange(n_blk) * MOE_BLOCK, side='right'), 0, N_EXPERTS - 1)
    xs = h[row_tok].reshape(n_blk, MOE_BLOCK, d)
    def expert_block(args):
        xb, e = args
        return (jax.nn.silu(xb @ w_gate[e]) * (xb @ w_up[e])) @ w_down[e]
    ys = lax.map(expert_block, (xs, blk_expert)).reshape(n_rows, d)
    return jnp.zeros_like(h).at[row_tok].add(ys * row_gate[:, None])

def setup_inputs(seed: int = 0) -> dict:
    key = jax.random.key(seed)
    ks = jax.random.split(key, 32)
    f32 = jnp.float32
    D = D_MODEL
    def nrm(k, shape, scale):
        return jax.random.normal(k, shape, f32) * scale
    a0 = jax.random.uniform(ks[14], (DEPTH, 2, LRU_WIDTH), f32, 0.9, 0.999)
    s0 = a0 ** (1.0 / RG_C)
    return {
        'x': nrm(ks[0], (BATCH, SEQ, D), 1.0),
        'c': nrm(ks[1], (BATCH, D), 1.0),
        'ctx': nrm(ks[2], (BATCH, CTX_LEN, D), 1.0),
        'c_ctx': nrm(ks[3], (D,), 1.0),
        'ada_w': nrm(ks[4], (DEPTH, D, 6 * D), D ** -0.5),
        'ada_b': nrm(ks[5], (DEPTH, 6 * D), 0.02),
        'w_in': nrm(ks[6], (DEPTH, D, IN_WIDTH), D ** -0.5),
        'conv_w': nrm(ks[7], (DEPTH, CONV_W, LRU_WIDTH), CONV_W ** -0.5),
        'conv_b': nrm(ks[8], (DEPTH, LRU_WIDTH), 0.02),
        'rg_wa': nrm(ks[9], (DEPTH, 2, LRU_BLOCKS, LRU_BLOCK, LRU_BLOCK), LRU_BLOCK ** -0.5),
        'rg_ba': nrm(ks[10], (DEPTH, 2, LRU_WIDTH), 0.02),
        'rg_wx': nrm(ks[11], (DEPTH, 2, LRU_BLOCKS, LRU_BLOCK, LRU_BLOCK), LRU_BLOCK ** -0.5),
        'rg_bx': nrm(ks[12], (DEPTH, 2, LRU_WIDTH), 0.02),
        'rg_lam': jnp.log(s0) - jnp.log1p(-s0),
        'q_norm_g': 1.0 + nrm(ks[15], (DEPTH, GQA_HEAD_DIM), 0.02),
        'k_norm_g': 1.0 + nrm(ks[16], (DEPTH, GQA_HEAD_DIM), 0.02),
        'diff_lambda': nrm(ks[17], (DEPTH, 4, DIFF_QK_DIM), 0.1),
        'diff_subln_g': 1.0 + nrm(ks[18], (DEPTH, DIFF_V_DIM), 0.02),
        'w_out': nrm(ks[19], (DEPTH, MIX_WIDTH, D), MIX_WIDTH ** -0.5 * DEEPNORM_BETA),
        'ln1_g': 1.0 + nrm(ks[20], (DEPTH, D), 0.02),
        'ln1_b': nrm(ks[21], (DEPTH, D), 0.02),
        'ln2_g': 1.0 + nrm(ks[22], (DEPTH, D), 0.02),
        'ln2_b': nrm(ks[23], (DEPTH, D), 0.02),
        'router_w': nrm(ks[24], (D, N_EXPERTS), D ** -0.5),
        'router_b': nrm(ks[25], (N_EXPERTS,), 0.01),
        'exp_w_gate': nrm(ks[26], (DEPTH, N_EXPERTS, D, EXPERT_FF), D ** -0.5),
        'exp_w_up': nrm(ks[27], (DEPTH, N_EXPERTS, D, EXPERT_FF), D ** -0.5),
        'exp_w_down': nrm(ks[28], (DEPTH, N_EXPERTS, EXPERT_FF, D), EXPERT_FF ** -0.5 * DEEPNORM_BETA),
    }

def reference(x, c, ctx, c_ctx, ada_w, ada_b, w_in, conv_w, conv_b, rg_wa, rg_ba, rg_wx, rg_bx, rg_lam,
              q_norm_g, k_norm_g, diff_lambda, diff_subln_g, w_out, ln1_g, ln1_b, ln2_g, ln2_b,
              router_w, router_b, exp_w_gate, exp_w_up, exp_w_down):
    bsz, s, d = x.shape
    rope_g = axial_rope_tables(s, GQA_HEAD_DIM)
    rope_d = axial_rope_tables(s, DIFF_QK_DIM)
    silu_c = jax.nn.silu(c)
    silu_cc = jax.nn.silu(c_ctx)
    for li in range(DEPTH):
        need_ctx = li < DEPTH - 1
        lam_init = 0.8 - 0.6 * math.exp(-0.3 * li)
        mod_l = (silu_c @ ada_w[li] + ada_b[li])[:, None, :]
        mod_c = silu_cc @ ada_w[li] + ada_b[li]
        sh1, sc1, g1, sh2, sc2, g2 = jnp.split(mod_l, 6, axis=-1)
        csh1, csc1, cg1, csh2, csc2, cg2 = jnp.split(mod_c, 6, axis=-1)

        y_l, y_c = token_mixer(x * (1.0 + sc1) + sh1, ctx * (1.0 + csc1) + csh1, w_in[li], conv_w[li], conv_b[li],
                               rg_wa[li], rg_ba[li], rg_wx[li], rg_bx[li], rg_lam[li], q_norm_g[li], k_norm_g[li],
                               diff_lambda[li], diff_subln_g[li], w_out[li], rope_g, rope_d, lam_init, need_ctx)
        x = layer_norm(DEEPNORM_ALPHA * x + g1 * y_l, ln1_g[li], ln1_b[li])
        h_l = x * (1.0 + sc2) + sh2
        if need_ctx:
            ctx = layer_norm(DEEPNORM_ALPHA * ctx + cg1 * y_c, ln1_g[li], ln1_b[li])
            h_c = ctx * (1.0 + csc2) + csh2
            n_lat = bsz * s
            f = moe_ffn(jnp.concatenate([h_l.reshape(n_lat, d), h_c.reshape(-1, d)], axis=0), router_w, router_b,
                        exp_w_gate[li], exp_w_up[li], exp_w_down[li])
            f_l = f[:n_lat].reshape(bsz, s, d)
            ctx = layer_norm(DEEPNORM_ALPHA * ctx + cg2 * f[n_lat:].reshape(ctx.shape), ln2_g[li], ln2_b[li])
        else:
            f_l = moe_ffn(h_l.reshape(bsz * s, d), router_w, router_b, exp_w_gate[li], exp_w_up[li],
                          exp_w_down[li]).reshape(bsz, s, d)
        x = layer_norm(DEEPNORM_ALPHA * x + g2 * f_l, ln2_g[li], ln2_b[li])
    return x


_drawn_inputs = setup_inputs


def setup_inputs(seed=0):
    import zlib

    import numpy as np

    out = dict(_drawn_inputs(seed))
    spreads = {}
    factors = {'rg_ba': 7.382,
     'rg_bx': 9.698,
     'q_norm_g': 8.0,
     'k_norm_g': 7.724,
     'diff_lambda': 8.0,
     'diff_subln_g': 7.444,
     'ln2_g': 8.331,
     'ln2_b': 8.35}
    for name, (base, spread) in spreads.items():
        noise = np.random.default_rng([zlib.crc32(name.encode()), seed]).standard_normal(out[name].shape)
        drawn = base * np.exp(spread * noise) if base else spread * noise
        out[name] = __import__('jax').numpy.asarray(drawn.astype(out[name].dtype))
    for name, factor in factors.items():
        out[name] = (out[name] * factor).astype(out[name].dtype)
    return out
```

```python
from contextlib import ExitStack

import concourse.bass as bass
from concourse import mybir

F32 = mybir.dt.float32
F32R = mybir.dt.float32r
I32 = mybir.dt.int32
ALU = mybir.AluOpType
ACT = mybir.ActivationFunctionType
AX = mybir.AxisListType

P = 128
D = 1024
KD = D // P
S = 1024
C = 256
T = S + C
ST, CT = S // P, C // P
TT = ST + CT
LRU = 256
LF = LRU // P
GH, GKV, GD = 8, 2, 64
DH, DQ, DV = 4, 32, 64
LAM_INIT = 0.8 - 0.6
EPS = 1e-6
RG_C = 8.0
ALPHA = 2.0 ** 0.25
CONV = 4
PADL = 1 + S + 3 + C + 2
UL = PADL - (CONV - 1)
UC = S + 3
E, G, EG, FF = 16, 4, 4, 512
FK = FF // P
NUNIT = KD + FK
BLK = P
NBLK = 2 * S // BLK + E - 1
MINBLK = 2 * S // BLK
ROWS = (NBLK + 1) * BLK


class Chain:

    def __init__(self, engine, sem):
        self.engine, self.sem, self.base, self.n = engine, sem, 0, 0

    def begin(self, base):
        self.base, self.n = base, 0

    def mark(self, ins):
        self.n += 1
        ins.then_inc(self.sem, 1)

    def wait(self):
        self.engine.wait_ge(self.sem, self.base + self.n)

    def link(self, ins):
        self.mark(ins)
        self.wait()


def wait_apart(engine, sem, value, passed):
    engine.wait_ge(sem, value)
    engine.sem_inc(passed, 1)


def build(nc, A, out):
    def dram(name, shape, dt=F32):
        return nc.dram_tensor(name, shape, dt, kind="Internal").ap()

    q_dram = dram("q_dram", (S, GH * GD))
    k_dram = dram("k_dram", (T, GKV * GD + DH * 2 * DQ))
    dq_dram = dram("dq_dram", (S, DH * 2 * DQ))
    x1_dram, h_dram = dram("x1_dram", (S, D)), dram("h_dram", (S, D))
    g2_dram = dram("g2_dram", (P, D))
    rows_dram = dram("rows_dram", (ROWS, 1), I32)
    y_dram = dram("y_dram", (ROWS, D))

    with ExitStack() as whole:
        def sb(name, shape, dt=F32, at=whole):
            return at.enter_context(nc.sbuf_tensor(name, shape, dt))

        def sem(name):
            return whole.enter_context(nc.semaphore(name))

        ps = whole.enter_context(nc.psum_tensor("ps", [P, 8, 512], F32))
        ident = sb("ident", [P, P])
        dest = sb("dest", [P, 2, ST], I32)
        gates = sb("gates", [P, 2, ST])
        blk_tab = sb("blk_tab", [P, NBLK + 3], I32)
        attn = ExitStack()
        V = sb("V", [P, TT, GKV, GD + 1], F32, attn)
        DVt = sb("DVt", [P, TT, DH, DV + 1], F32, attn)
        ya = sb("ya", [P, LF, S], F32, attn)
        lam = sb("lam", [P, 8], F32, attn)
        silu_c = sb("silu_c", [P, KD, 2], F32, attn)
        cvec = sb("cvec", [P, KD, 2], F32, attn)

        p1 = ExitStack()
        xhi = sb("xhi", [P, KD, T], F32R, p1)
        xlo = sb("xlo", [P, KD, T], F32R, p1)
        whi = sb("whi", [P, KD, 512], F32R, p1)
        wlo = sb("wlo", [P, KD, 512], F32R, p1)
        NWR = 4
        wraw = sb("wraw", [P, NWR, 512], F32, p1)
        ax = sb("ax", [P, LF, PADL], F32, p1)
        rope_q = sb("rope_q", [P, ST, 2, GD], F32, p1)
        rope_k = sb("rope_k", [P, ST, 2, GD], F32, p1)
        rope_d = sb("rope_d", [P, ST, 2, DQ], F32, p1)
        gvec = sb("gvec", [P, 2, 2, GD], F32, p1)
        lvec = sb("lvec", [P, 4, DQ], F32, p1)
        modc = sb("modc", [P, 16, 2], F32, p1)
        adab = sb("adab", [P, 16], F32, p1)
        lruc = sb("lruc", [P, LF, 16], F32, p1)
        nsp = sb("nsp", [P, LF, 2, 2], F32, p1)
        stat = sb("stat", [P, 2, 3, 8], F32, p1)
        wg = sb("wg", [P, 8, P], F32, p1)
        pa = ExitStack()
        NAR = 2
        adar = sb("adar", [P, NAR, 2048], F32, pa)
        xraw = sb("xraw", [P, 2, T], F32, pa)
        pa.close()
        pl = ExitStack()
        U = sb("U", [P, LF, UL], F32, pl)
        TH = sb("TH", [P, UL], F32, pl)
        SQ = sb("SQ", [P, UL], F32, pl)
        H = sb("H", [P, S], F32, pl)
        zst = sb("zst", [P, 2, 512], F32, pl)
        zo = sb("zo", [P, 2, 512], F32, pl)
        pl.close()
        p1.close()
        R = ax[:, 0, 0:UL]
        I = ax[:, 1, 0:UL]

        s = {n: sem(n) for n in (
            "consts", "mod_b", "c_in", "silu", "adar0", "adar1", "ada_used",
            "xraw0", "xraw1", "x_mod", "x_hi", "x_lo",
            "wraw0", "wraw1", "wraw2", "wraw3", "w_hi", "w_lo", "w_used",
            "proj_done", "proj_out", "prep", "wg_zero", "wg_load", "z_sq", "z_rt", "z_fin", "zo_out0", "zo_out1",
            "u_ready", "gate_mm", "gate_sig", "a_rdy", "m_neg", "m_rt",
            "lru_done", "dve_c", "act_c", "sp_rdy", "nsp_rdy")}
        blk = ExitStack()
        block = blk.enter_context(nc.Block())

        units = [("L", f, o, n) for f in range(LF) for o, n in ((0, 512), (512, 512), (S, C))] + \
                [("L", LF + f, o, 512) for f in range(LF) for o in (0, 512)]
        NL = len(units)
        units += [("Q", t) for t in range(ST)] + [("K", t) for t in range(TT)] + [("E", t) for t in range(TT)]
        group = {"L": 0, "Q": 1, "K": 2, "E": 3}
        last_of = [max(i for i, u in enumerate(units) if group[u[0]] == g) for g in range(4)]
        z_units = [i for i, u in enumerate(units) if u[0] in "QK" or (u[0] == "E" and u[1] < ST)]
        z_of = {u: n for n, u in enumerate(z_units)}
        NU, RING = len(units), 4
        combos = [(f, d) for f in range(LF) for d in range(2)]
        gate_at = {NL + 1 + 3 * c + g: (c, g) for c in range(4) for g in range(2)}
        CONSTS = 16 * 7

        def w_free(eng, c):
            g, k = divmod(c, KD)
            if g and k < KD - 1:
                eng.wait_ge(s["w_used"], (g - 1) * (KD - 1) + k + 1)
            elif g:
                eng.wait_ge(s["proj_done"], last_of[g - 1] + 1)

        @block.sync
        def _(sp):
            sp.dma_start(cvec[:, :, :], A["cvec"]).then_inc(s["c_in"], 16)
            sp.dma_start(adab[:, :], A["adab_cols"]).then_inc(s["mod_b"], 16)
            for k in range(KD):
                if k >= NAR:
                    sp.wait_ge(s["ada_used"], k - NAR + 1)
                sp.dma_start(adar[:, k % NAR, :], A["ada_w"][k * P:(k + 1) * P, 0:2048]).then_inc(s[f"adar{k % NAR}"], 16)

            def load_w(c):
                g, k = divmod(c, KD)
                if c >= NWR:
                    sp.wait_ge(s["w_lo"], c - NWR + 1)
                sp.dma_start(wraw[:, c % NWR, :], A["w_in"][k * P:(k + 1) * P, g * 512:(g + 1) * 512])\
                    .then_inc(s[f"wraw{c % NWR}"], 16)

            for k in range(KD):
                if k >= 2:
                    sp.wait_ge(s["x_lo"], k - 1)
                sp.dma_start(xraw[:, k % 2, :], A["xT"][k * P:(k + 1) * P, :]).then_inc(s[f"xraw{k % 2}"], 16)
                load_w(k)
            for dst, name in ((ident[:, :], "ident"), (rope_q[:, :, :, :], "rope_g"), (rope_k[:, :, :, :], "rope_g"),
                              (rope_d[:, :, :, :], "rope_d"), (gvec[:, :, :, :], "gvec"), (lvec[:, :, :], "lvec"),
                              (lruc[:, :, :], "lruc")):
                sp.dma_start(dst, A[name]).then_inc(s["consts"], 16)
            sp.wait_ge(s["wg_zero"], 1)
            for b in range(2):
                sp.dma_start(wg[b * 64:(b + 1) * 64, :, b * 64:(b + 1) * 64], A["wg"][b]).then_inc(s["wg_load"], 16)

            def store_z(i):
                n, (kind, t) = z_of[i], units[i]
                rows = slice(t * P, (t + 1) * P)
                dst, lo = {"Q": (q_dram, 0), "K": (k_dram, 128), "E": (dq_dram, 256)}[kind]
                sp.wait_ge(s["z_fin"], n + 1)
                sp.dma_start(dst[rows, :], zo[:, n % 2, lo:512]).then_inc(s[f"zo_out{n % 2}"], 16)

            for c in range(KD, 2 * KD):
                load_w(c)
            for g in range(1, 4):
                mine = [i for i in z_units if group[units[i][0]] == g]
                for c in range((g + 1) * KD, (g + 1) * KD + NWR if g < 3 else 0):
                    load_w(c)
                for i in mine[:-1]:
                    store_z(i)
                for c in range((g + 1) * KD + NWR, (g + 2) * KD if g < 3 else 0):
                    load_w(c)
                store_z(mine[-1])
            for b in range(2):
                sp.wait_ge(s[f"zo_out{b}"], 16 * len(z_units[b::2]))

        @block.gpsimd
        def _(pool):
            pool.memset(V[:, :, :, GD:GD + 1], 1.0)
            pool.memset(DVt[:, :, :, DV:DV + 1], 1.0)
            pool.memset(ax[:, :, :], 0.0).then_inc(s["prep"], 1)
            pool.memset(wg[:, :, :], 0.0).then_inc(s["wg_zero"], 1)
            for c in range(4 * KD):
                pool.wait_ge(s["w_hi"], c + 1)
                pool.tensor_tensor(wlo[:, c % KD, :], wraw[:, c % NWR, :], whi[:, c % KD, :].bitcast(F32), ALU.subtract)\
                    .then_inc(s["w_lo"], 1)

        @block.scalar
        def _(act):
            ch = Chain(act, s["act_c"])
            act.wait_ge(s["c_in"], 16)
            act.activation(silu_c[:, :, :], cvec[:, :, :], ACT.Silu).then_inc(s["silu"], 1)

            def w_hi(c):
                act.wait_ge(s[f"wraw{c % NWR}"], 16 * (c // NWR + 1))
                w_free(act, c)
                act.activation(whi[:, c % KD, :], wraw[:, c % NWR, :], ACT.Copy).then_inc(s["w_hi"], 1)

            for k in range(KD):
                act.wait_ge(s["x_mod"], k + 1)
                act.activation(xhi[:, k, :], xraw[:, k % 2, :], ACT.Copy).then_inc(s["x_hi"], 1)
                w_hi(k)

            def sqrt_rms(i):
                n, nh = z_of[i], {"Q": GH, "K": GKV}[units[i][0]]
                act.wait_ge(s["z_sq"], n + 1)
                act.activation(stat[:, n % 2, 1, 0:nh], stat[:, n % 2, 0, 0:nh], ACT.Sqrt).then_inc(s["z_rt"], 1)

            def lru_gate(c, g):
                f, d = combos[c]
                act.wait_ge(s["gate_mm"], 2 * c + g + 1)
                if g == 0 and c:
                    act.wait_ge(s["lru_done"], c)
                act.activation(R if g == 0 else I, ps[:, 0:3, :].rearrange("p a b -> p (a b)")[:, 0:UL], ACT.Sigmoid,
                               bias=lruc[:, f, 5 + 2 * g + d:6 + 2 * g + d]).then_inc(s["gate_sig"], 1)
                if g == 1:
                    act.wait_ge(s["gate_sig"], 2 * c + 2)
                    act.wait_ge(s["nsp_rdy"], 1)
                    ch.link(act.activation(TH[:, :], R, ACT.Tanh, scale=nsp[:, f, d:d + 1, 0]))
                    act.activation(R, R, ACT.Exp, scale=nsp[:, f, d:d + 1, 0]).then_inc(s["a_rdy"], 1)

            def lru_root(c):
                act.wait_ge(s["m_neg"], c + 1)
                act.activation(TH[:, :], TH[:, :], ACT.Sqrt, scale=-1.0).then_inc(s["m_rt"], 1)

            for i, u in enumerate(units):
                if i in last_of and i != NU - 1:
                    for k in range(KD):
                        w_hi((group[u[0]] + 1) * KD + k)
                act.wait_ge(s["proj_done"], i + 1)
                src = ps[:, 4 + i % RING, :]
                if i == 0:
                    act.wait_ge(s["prep"], 1)
                if i == NL:
                    act.wait_ge(s["consts"], CONSTS)
                    for f in range(LF):
                        ch.link(act.activation(nsp[:, f, :, 1], lruc[:, f, 9:11], ACT.Exp, scale=-1.0))
                        ins = act.activation(nsp[:, f, :, 0], nsp[:, f, :, 1], ACT.Ln, bias=1.0)
                    ins.then_inc(s["sp_rdy"], 1)
                if u[0] == "L":
                    _, f, o, n = u
                    if f < LF:
                        at = 1 + o if o < S else UC + 1
                        last = act.activation(ax[:, f, at:at + n], src[:, 0:n], ACT.Copy)
                    else:
                        last = act.activation(ya[:, f - LF, o:o + n], src[:, 0:n], ACT.Gelu_apprx_tanh)
                else:
                    t, n = u[1], z_of.get(i)
                    if n is not None and n >= 2:
                        act.wait_ge(s["z_fin"], n - 1)
                    if u[0] == "K":
                        act.activation(V[:, t, :, 0:GD], src[:, 0:128].rearrange("p (h d) -> p h d", h=GKV), ACT.Copy)
                    if u[0] == "E":
                        last = act.activation(DVt[:, t, :, 0:DV], src[:, 0:256].rearrange("p (h d) -> p h d", h=DH), ACT.Copy)
                    lo = {"Q": 0, "K": 128, "E": 256}[u[0]]
                    if n is not None:
                        last = act.activation(zst[:, n % 2, lo:512], src[:, lo:512], ACT.Copy)
                last.then_inc(s["proj_out"], 1)
                if u[0] in "QK":
                    sqrt_rms(i)
                if i - 1 in gate_at and gate_at[i - 1][1] == 1:
                    lru_root(gate_at[i - 1][0])
                if i in gate_at:
                    lru_gate(*gate_at[i])

        @block.vector
        def _(dve):
            ch = Chain(dve, s["dve_c"])
            dve.wait_ge(s["ada_used"], KD)
            dve.wait_ge(s["mod_b"], 16)
            for j in range(2):
                ins = dve.tensor_tensor(modc[:, :, j], ps[:, 0, 0:32].rearrange("p (n j) -> p n j", j=2)[:, :, j],
                                        adab[:, :], ALU.add)
            ch.link(ins)
            ch.link(dve.tensor_scalar(modc[:, 8:16, :], modc[:, 8:16, :], 1.0, None, ALU.add))

            def modulate(k):
                dve.wait_ge(s[f"xraw{k % 2}"], 16 * (k // 2 + 1))
                x = xraw[:, k % 2, :]
                dve.tensor_scalar(x[:, 0:S], x[:, 0:S], modc[:, 8 + k, 0:1], modc[:, k, 0:1], ALU.mult, ALU.add)
                dve.tensor_scalar(x[:, S:T], x[:, S:T], modc[:, 8 + k, 1:2], modc[:, k, 1:2], ALU.mult, ALU.add)\
                    .then_inc(s["x_mod"], 1)

            modulate(0)
            for k in range(KD):
                if k + 1 < KD:
                    modulate(k + 1)
                dve.wait_ge(s["x_hi"], k + 1)
                dve.tensor_tensor(xlo[:, k, :], xraw[:, k % 2, :], xhi[:, k, :].bitcast(F32), ALU.subtract)\
                    .then_inc(s["x_lo"], 1)

            dve.wait_ge(s["consts"], CONSTS)
            for tab, j in ((rope_q, 0), (rope_k, 1)):
                for h in range(2):
                    dve.tensor_tensor(tab[:, :, h, :], tab[:, :, h, :],
                                      gvec[:, j, h, :].unsqueeze(1).broadcast_to([P, ST, GD]), ALU.mult)
            for j in range(2):
                ch.link(dve.tensor_tensor(lvec[:, 2 * j, :], lvec[:, 2 * j, :], lvec[:, 2 * j + 1, :], ALU.mult))
                ch.link(dve.tensor_reduce(lam[:, j:j + 1], lvec[:, 2 * j, :], AX.X, ALU.add))

            dve.wait_ge(s["proj_out"], 3 * LF)
            for f in range(LF):
                ch.link(dve.tensor_scalar(U[:, f, :], ax[:, f, 0:UL], lruc[:, f, 0:1], lruc[:, f, 4:5], ALU.mult, ALU.add))
                for k in range(1, CONV):
                    ins = dve.scalar_tensor_tensor(out=U[:, f, :], in0=ax[:, f, k:k + UL], scalar=lruc[:, f, k:k + 1],
                                                   in1=U[:, f, :], op0=ALU.mult, op1=ALU.add)
                    if f == LF - 1 and k == CONV - 1:
                        ins.then_inc(s["u_ready"], 1)
                    else:
                        ch.link(ins)
            dve.wait_ge(s["sp_rdy"], 1)
            dve.tensor_scalar(nsp[:, :, :, 0], nsp[:, :, :, 0], -RG_C, None, ALU.mult).then_inc(s["nsp_rdy"], 1)

            def rms(n, lo, nh, w):
                z = zst[:, n % 2, lo:lo + nh * w].rearrange("p (h d) -> p h d", h=nh)
                o = zo[:, n % 2, lo:lo + nh * w].rearrange("p (h d) -> p h d", h=nh)
                st = stat[:, n % 2]
                ch.link(dve.tensor_tensor(o, z, z, ALU.mult))
                ch.link(dve.tensor_reduce(st[:, 0, 0:nh], o, AX.X, ALU.add))
                dve.tensor_scalar(st[:, 0, 0:nh], st[:, 0, 0:nh], 1.0 / w, EPS, ALU.mult, ALU.add).then_inc(s["z_sq"], 1)
                dve.wait_ge(s["z_rt"], n + 1)
                ch.link(dve.reciprocal(st[:, 2, 0:nh], st[:, 1, 0:nh]))
                ch.link(dve.tensor_tensor(z, z, st[:, 2, 0:nh].unsqueeze(2).broadcast_to([P, nh, w]), ALU.mult))

            def rotate(n, lo, tab, t, nh, w):
                z, o = zst[:, n % 2, lo:lo + nh * w], zo[:, n % 2, lo:lo + nh * w]
                swapped = z.rearrange("p (h c two) -> p h c two", h=nh, two=2)[:, :, :, ::-1]
                sines = tab[:, t, 1, :].rearrange("p (c two) -> p c two", two=2).unsqueeze(1).broadcast_to([P, nh, w // 2, 2])
                zh = z.rearrange("p (h d) -> p h d", h=nh)
                ch.link(dve.tensor_tensor(o.rearrange("p (h c two) -> p h c two", h=nh, two=2), swapped, sines, ALU.mult))
                ch.link(dve.tensor_tensor(zh, zh, tab[:, t, 0, :].unsqueeze(1).broadcast_to([P, nh, w]), ALU.mult))
                return dve.tensor_tensor(o, o, z, ALU.add)

            def heads(i):
                (kind, t), n = units[i], z_of[i]
                dve.wait_ge(s["proj_out"], i + 1)
                if n >= 2:
                    dve.wait_ge(s[f"zo_out{n % 2}"], 16 * (n // 2))
                if kind == "Q":
                    rms(n, 0, GH, GD)
                    last = rotate(n, 0, rope_q, t, GH, GD)
                elif kind == "E":
                    last = rotate(n, 256, rope_d, t, 2 * DH, DQ)
                else:
                    rms(n, 128, GKV, GD)
                    if t < ST:
                        ch.mark(rotate(n, 128, rope_k, t, GKV, GD))
                        last = rotate(n, 256, rope_d, t, 2 * DH, DQ)
                    else:
                        dve.tensor_tensor(zo[:, n % 2, 128:256].rearrange("p (h d) -> p h d", h=GKV),
                                          zst[:, n % 2, 128:256].rearrange("p (h d) -> p h d", h=GKV),
                                          gvec[:, 1, 0, :].unsqueeze(1).broadcast_to([P, GKV, GD]), ALU.mult)
                        last = dve.tensor_copy(zo[:, n % 2, 256:512], zst[:, n % 2, 256:512])
                last.then_inc(s["z_fin"], 1)

            def lru_mult(c):
                f, d = combos[c]
                dve.wait_ge(s["gate_sig"], 2 * c + 2)
                dve.tensor_tensor(I, I, U[:, f, :], ALU.mult)
                dve.wait_ge(s["a_rdy"], c + 1)
                ch.link(dve.tensor_tensor(SQ[:, :], R, R, ALU.mult))
                dve.scalar_tensor_tensor(out=TH[:, :], in0=SQ[:, :], scalar=1.0, in1=TH[:, :], op0=ALU.add, op1=ALU.mult)\
                    .then_inc(s["m_neg"], 1)

            def lru_scan(c):
                f, d = combos[c]
                dve.wait_ge(s["m_rt"], c + 1)
                ch.link(dve.tensor_tensor(I, I, TH[:, :], ALU.mult))
                rv = slice(None, None, -1) if d else slice(None)
                cx, lx = slice(UC, UC + C), slice(0, S)
                ch.link(dve.tensor_tensor_scan(I[:, cx][:, rv], R[:, cx][:, rv], I[:, cx][:, rv], 0.0, ALU.mult, ALU.add))
                h0 = I[:, UC:UC + 1] if d else I[:, UC + C - 1:UC + C]
                dst = I[:, lx] if d else H[:, :]
                scan = dve.tensor_tensor_scan(dst[:, rv], R[:, lx][:, rv], I[:, lx][:, rv], h0, ALU.mult, ALU.add)
                if d == 0:
                    scan.then_inc(s["lru_done"], 1)
                else:
                    ch.link(scan)
                    ch.link(dve.tensor_tensor(H[:, :], H[:, :], I[:, lx], ALU.add))
                    dve.wait_ge(s["proj_out"], NL)
                    dve.tensor_tensor(ya[:, f, :], ya[:, f, :], H[:, :], ALU.mult).then_inc(s["lru_done"], 1)

            for i, u in enumerate(units):
                if i in z_of:
                    heads(i)
                if i - 1 in gate_at and gate_at[i - 1][1] == 1:
                    lru_scan(gate_at[i - 1][0])
                if i in gate_at and gate_at[i][1] == 1:
                    lru_mult(gate_at[i][0])

        @block.tensor
        def _(pe):
            pe.wait_ge(s["silu"], 1)
            for k in range(KD):
                pe.wait_ge(s[f"adar{k % NAR}"], 16 * (k // NAR + 1))
                for n in range(16):
                    mm = pe.matmul(ps[:, 0, 2 * n:2 * n + 2], adar[:, k % NAR, n * P:(n + 1) * P], silu_c[:, k, :],
                                   start=(k == 0 and n == 0), stop=(k == KD - 1), skip_group_check=True)
                mm.then_inc(s["ada_used"], 1)

            def product(dst, a, b, k, n_k):
                for j, (x, y) in enumerate(((a[0], b[0]), (a[1], b[0]), (a[0], b[1]))):
                    mm = pe.matmul(dst, x, y, start=(k == 0 and j == 0), stop=(k == n_k - 1 and j == 2))
                return mm

            def gates(c, g):
                f, d = combos[c]
                pe.wait_ge(s["u_ready"], 1)
                pe.wait_ge(s["wg_load"], 32)
                if 2 * c + g:
                    pe.wait_ge(s["gate_sig"], 2 * c + g)
                for o, n, b in ((0, 512, 0), (512, 512, 1), (1024, UL - 1024, 2)):
                    mm = pe.matmul(ps[:, b, 0:n], wg[:, (f * 2 + d) * 2 + g, :], U[:, f, o:o + n], start=True, stop=True)
                mm.then_inc(s["gate_mm"], 1)

            for i, u in enumerate(units):
                g = group[u[0]]
                if i >= RING:
                    pe.wait_ge(s["proj_out"], i - RING + 1)
                for k in range(KD):
                    pe.wait_ge(s["w_lo"], g * KD + k + 1)
                    if g == 0:
                        pe.wait_ge(s["x_lo"], k + 1)
                    if u[0] == "L":
                        _, f, o, n = u
                        cols = slice(f * P, (f + 1) * P)
                        a, b = (whi[:, k, cols], wlo[:, k, cols]), (xhi[:, k, o:o + n], xlo[:, k, o:o + n])
                    else:
                        n = 256 if u[0] == "E" and u[1] >= ST else 512
                        cols = slice(u[1] * P, (u[1] + 1) * P)
                        a, b = (xhi[:, k, cols], xlo[:, k, cols]), (whi[:, k, 0:n], wlo[:, k, 0:n])
                    mm = product(ps[:, 4 + i % RING, 0:n], a, b, k, KD)
                    if i in last_of and k < KD - 1:
                        mm.then_inc(s["w_used"], 1)
                mm.then_inc(s["proj_done"], 1)
                if i in gate_at:
                    gates(*gate_at[i])

        blk.close()

        mrow = sb("mrow", [P, 4, D], F32, attn)
        p2 = ExitStack()
        woh = sb("woh", [P, KD, D], F32R, attn)
        wol = sb("wol", [P, KD, D], F32R, attn)
        ysm = sb("ysm", [P, ST, GH * GD + DH * DV], F32, attn)
        ring = sb("ring", [P, 2, 2048], F32, p2)
        pr = ExitStack()
        sbc = sb("sbc", [P, KD, P], F32, pr)
        pr.close()
        Q1 = sb("Q1", [P, 2, S], F32R, p2)
        Q2 = sb("Q2", [P, 2, S], F32R, p2)
        K1 = sb("K1", [P, 2, T], F32R, p2)
        K2 = sb("K2", [P, 2, T], F32R, p2)
        qr = sb("qr", [P, ST, GD], F32, p2)
        kr = sb("kr", [P, TT, GD], F32, p2)
        qs = sb("qs", [P, ST, P], F32, p2)
        ks = sb("ks", [P, TT, P], F32, p2)
        pT = sb("pT", [P, 2, 512], F32, p2)
        OT = ring[:, 0, 0:S]
        MX = sb("MX", [P, ST], F32, p2)
        MM = sb("MM", [P, ST, 2], F32R, p2)
        rec = sb("rec", [P, ST], F32, p2)
        od = sb("od", [P, 2, ST, DV], F32, p2)
        Vs = sb("Vs", [P, 2, TT, GD + 1], F32, p2)
        subg = sb("subg", [P, DV], F32, p2)
        rst = sb("rst", [P, 2, ST * DH], F32, p2)
        p2.close()

        a2 = {n: sem(n) for n in (
            "passed2", "mrow_in", "ring0", "ring1", "row_mm", "row_out", "wo_hi", "wo_lo", "bc_rdy", "m_hi", "head_d", "rec_d", "subg_in", "lam_e",
            "qr_in", "kr_in", "dup", "tr_mm", "hi_d", "lo_d", "k2_cp", "max_mm", "max_red", "m_rdy", "mt_mm", "mt_cp",
            "s_mm", "exp_d", "pv_d", "o_out", "acc_free", "ot_mm", "ones_d", "vs_d", "dve2_c", "act2_c", "sub_sq", "sub_rt")}
        NROW = 8
        MAPS = GH + 2 * DH
        GROUP_HEADS = GH // GKV
        rounds = [(0, 0, 4), (0, 4, 4), (1, 0, 4), (1, 4, 4), (1, 8, 2)]
        NR = len(rounds)
        NS = 2 * TT
        chunks = [(0, 512), (512, 512), (1024, 256)]

        class Kind:
            def __init__(self, w, rep, rows, scale):
                self.w, self.rep, self.rows, self.scale = w, rep, rows, scale

        gqa = Kind(GD, 2, 128, GD ** -0.5)
        dif = Kind(DQ, 3, 96, DQ ** -0.5)

        block = blk.enter_context(nc.Block())

        @block.sync
        def _(sp):
            sp.dma_start(mrow[:, :, :], A["adab_rows"]).then_inc(a2["mrow_in"], 16)
            sp.dma_start(subg[:, :], A["subg"]).then_inc(a2["subg_in"], 16)
            for i in range(2 * NROW + 4):
                if i >= 2:
                    if i - 2 < 2 * NROW:
                        sp.wait_ge(a2["row_mm"], i - 1)
                    else:
                        sp.wait_ge(a2["wo_lo"], 2 * (i - 2 - 2 * NROW) + 2)
                if i < 2 * NROW:
                    n, kh = divmod(i, 2)
                    src = A["ada_w"][kh * 512:(kh + 1) * 512, 2048 + n * 512:2048 + (n + 1) * 512]
                    dst = ring[:, i % 2, :].rearrange("p (k n) -> p k n", k=4)
                else:
                    j = i - 2 * NROW
                    src = A["w_out"][j * 256:(j + 1) * 256, :]
                    dst = ring[:, i % 2, :].rearrange("p (k n) -> p k n", k=2)
                sp.dma_start(dst, src.rearrange("(k p) n -> p k n", p=P)).then_inc(a2[f"ring{i % 2}"], 16)

            def load(G, q_src, k_src):
                sp.wait_ge(a2["dup"], 2 * G + 1)
                sp.dma_start(qr[:, :, :], q_src).then_inc(a2["qr_in"], 16)
                sp.dma_start(kr[:, :, :], k_src).then_inc(a2["kr_in"], 16)

            q_v = q_dram.rearrange("(t p) (h d) -> h p t d", p=P, d=GD)
            k_v = k_dram.rearrange("(t p) (h d) -> h p t d", p=P, d=GD)
            dq_v = dq_dram.rearrange("(t p) (h d) -> h p t d", p=P, d=GD)
            one = lambda v, i: v[bass.ds(i, 1)].rearrange("o p t d -> (o p) t d")
            with sp.Fori(0, GKV) as kv:
                with sp.Fori(0, GROUP_HEADS) as j:
                    load(kv * GROUP_HEADS + j, one(q_v, kv * GROUP_HEADS + j), one(k_v, kv))
            with sp.Fori(0, DH) as h:
                for m in range(2):
                    load(GH + 2 * h + m, one(dq_v, h), one(k_v, GKV + h))

        @block.gpsimd
        def _(pool):
            pool.memset(K2[64:66, :, :].bitcast(F32), 1.0).then_inc(a2["dup"], 1)
            pool.wait_ge(a2["dup"], 1)
            for k in range(KD):
                i = 2 * NROW + k // 2
                pool.wait_ge(a2["wo_hi"], k + 1)
                pool.tensor_tensor(wol[:, k, :], ring[:, i % 2, (k % 2) * D:(k % 2 + 1) * D], woh[:, k, :].bitcast(F32), ALU.subtract)\
                    .then_inc(a2["wo_lo"], 1)

            def repeat(kind, G, par, m, vh, first=False, ones=False):
                if not first and kind is gqa:
                    wait_apart(pool, a2["k2_cp"], G * 3, a2["passed2"])
                if not first:
                    wait_apart(pool, a2["lo_d"], G * NR, a2["passed2"])
                for raw, dst, n, got in ((qr, qs, ST, "qr_in"), (kr, ks, TT, "kr_in")):
                    wait_apart(pool, a2[got], G * 16 + 16, a2["passed2"])
                    pool.tensor_copy(dst[:, :, 0:kind.rep * kind.w].rearrange("p t (r w) -> p t r w", w=kind.w),
                                     raw[:, :, m * kind.w:(m + 1) * kind.w].unsqueeze(2).broadcast_to([P, n, kind.rep, kind.w]))\
                        .then_inc(a2["dup"], 1)
                wait_apart(pool, a2["tr_mm"], G * NR + 1, a2["passed2"])
                src = (V if kind is gqa else DVt)[:, :, bass.ds(vh, 1), :].rearrange("p t o d -> p (t o) d")
                pool.tensor_copy(Vs[:, par, :, :], src).then_inc(a2["vs_d"], 1)
                if kind is gqa:
                    for r, (is_k, t0, nt) in enumerate(rounds):
                        if is_k:
                            if r == 2:
                                wait_apart(pool, a2["vs_d"], G + 1, a2["passed2"])
                            else:
                                wait_apart(pool, a2["k2_cp"], G * 3 + r - 2, a2["passed2"])
                            wait_apart(pool, a2["hi_d"], G * NR + r + 1, a2["passed2"])
                            cols = slice(t0 * P, (t0 + nt) * P)
                            pool.tensor_copy(K2[0:64, par, cols], K1[0:64, par, cols].bitcast(F32)).then_inc(a2["k2_cp"], 1)
                if ones:
                    wait_apart(pool, a2["vs_d"], G + 1, a2["passed2"])
                    pool.memset(K1[96:98, par, :].bitcast(F32), 1.0).then_inc(a2["ones_d"], 1)
                    pool.wait_ge(a2["ones_d"], par + 1)

            repeat(gqa, 0, 0, 0, 0, first=True)
            repeat(gqa, 1, 1, 0, 0)
            repeat(gqa, 2, 0, 0, 0)
            repeat(gqa, 3, 1, 0, 0)
            with pool.Fori(GROUP_HEADS // 2, GH // 2) as it:
                for par in range(2):
                    repeat(gqa, it * 2 + par, par, 0, 1)
            pool.wait_ge(a2["k2_cp"], GH * 3)
            for m in range(2):
                if m == 1:
                    pool.wait_ge(a2["dup"], GH * 2 + 3)
                repeat(dif, GH + m, m, m, 0, ones=True)
            with pool.Fori(1, DH) as it:
                for par in range(2):
                    repeat(dif, it * 2 + (GH + par), par, par, it)

        @block.scalar
        def _(act):
            ch = Chain(act, a2["act2_c"])
            act.activation(lam[:, 2:4], lam[:, 0:2], ACT.Exp).then_inc(a2["lam_e"], 1)
            for k in range(KD):
                i = 2 * NROW + k // 2
                act.wait_ge(a2[f"ring{i % 2}"], 16 * (i // 2 + 1))
                act.activation(woh[:, k, :], ring[:, i % 2, (k % 2) * D:(k % 2 + 1) * D], ACT.Copy).then_inc(a2["wo_hi"], 1)

            def hi(kind, G, par, r):
                is_k, t0, nt = rounds[r]
                dst = (K1 if is_k else Q1)[0:kind.rows, par, t0 * P:(t0 + nt) * P]
                act.wait_ge(a2["tr_mm"], G * NR + r + 1)
                act.activation(dst, ps[0:kind.rows, 7, 0:nt * P], ACT.Copy).then_inc(a2["hi_d"], 1)

            def soft(kind, G, par, nxt, Gn):
                for u in range(NS):
                    act.wait_ge(a2["s_mm"], G * NS + u + 1)
                    act.activation(pT[:, u % 2, :], ps[:, u % 2, :], ACT.Exp, scale=kind.scale).then_inc(a2["exp_d"], 1)
                    if nxt and u < NR:
                        hi(nxt, Gn, 1 - par, u)

            for r in range(NR):
                hi(gqa, 0, 0, r)
            for kind, G0, after in ((gqa, 0, dif), (dif, GH, None)):
                with act.Fori(0, 3) as it:
                    for par in range(2):
                        soft(kind, it * 2 + (G0 + par), par, kind, it * 2 + (G0 + par + 1))
                soft(kind, G0 + 6, 0, kind, G0 + 7)
                soft(kind, G0 + 7, 1, after, G0 + 8)
            act.wait_ge(a2["sub_sq"], 1)
            act.activation(rst[:, 1, :], rst[:, 0, :], ACT.Sqrt).then_inc(a2["sub_rt"], 1)

        @block.vector
        def _(dve):
            ch = Chain(dve, a2["dve2_c"])
            for k in range(KD):
                ins = dve.tensor_copy(sbc[:, k, :], silu_c[:, k, 0:1].broadcast_to([P, P]))
            ins.then_inc(a2["bc_rdy"], 1)
            dve.wait_ge(a2["lam_e"], 1)
            ch.link(dve.tensor_tensor(lam[:, 4:5], lam[:, 3:4], lam[:, 2:3], ALU.subtract))
            dve.tensor_scalar(lam[:, 5:6], lam[:, 4:5], LAM_INIT, None, ALU.subtract).then_inc(a2["o_out"], 1)
            dve.wait_ge(a2["mrow_in"], 16)
            for n in range(NROW):
                dve.wait_ge(a2["row_mm"], 2 * n + 2)
                m = mrow[:, n // 2, (n % 2) * 512:(n % 2 + 1) * 512]
                ins = dve.tensor_tensor(m, m, ps[:, n % 2, :], ALU.add)
                ins.then_inc(a2["row_out"], 1)
            dve.wait_ge(a2["row_out"], NROW)
            dve.tensor_scalar(mrow[:, 2, :], mrow[:, 2, :], 1.0, None, ALU.add).then_inc(a2["acc_free"], 1)

            def lo(kind, G, par, r):
                is_k, t0, nt = rounds[r]
                cols = slice(t0 * P, (t0 + nt) * P)
                dve.wait_ge(a2["hi_d"], G * NR + r + 1)
                if kind is gqa:
                    rows = slice(64, 128) if is_k else slice(0, 64)
                    hi_part = (K1 if is_k else Q1)[rows, par, cols]
                    dst = (K1 if is_k else Q2)[rows, par, cols]
                else:
                    rows = slice(32, 64) if is_k else slice(64, 96)
                    hi_part = dst = (K1 if is_k else Q1)[rows, par, cols]
                dve.tensor_tensor(dst, ps[rows, 7, 0:nt * P], hi_part.bitcast(F32), ALU.subtract).then_inc(a2["lo_d"], 1)

            def maxima(G, j):
                dve.wait_ge(a2["max_mm"], G * ST + j + 1)
                dve.tensor_reduce(MX[:, j:j + 1], ps[:, 4:7, :].rearrange("p a b -> p (a b)")[:, 0:T], AX.X, ALU.max, negate=True)\
                    .then_inc(a2["max_red"], 1)

            def max_parts(G):
                dve.wait_ge(a2["max_red"], G * ST + ST)
                dve.tensor_copy(MM[:, :, 0], MX[:, :]).then_inc(a2["m_hi"], 1)
                dve.wait_ge(a2["m_hi"], G + 1)
                dve.tensor_tensor(MM[:, :, 1], MX[:, :], MM[:, :, 0].bitcast(F32), ALU.subtract).then_inc(a2["m_rdy"], 1)

            def max_rows(kind, G, par, b):
                dve.wait_ge(a2["mt_mm"], G * 2 + b + 1)
                dst = Q2[64:66, par, b * 512:(b + 1) * 512] if kind is gqa else Q1[96:98, par, b * 512:(b + 1) * 512]
                dve.tensor_copy(dst, ps[0:2, 7, :]).then_inc(a2["mt_cp"], 1)

            def output(kind, G, par, col):
                dve.wait_ge(a2["pv_d"], G + 1)
                dve.tensor_copy(OT[0:GD + 1, :].rearrange("p (b n) -> p b n", b=2), ps[0:GD + 1, 2:4, :]).then_inc(a2["acc_free"], 1)
                for b in range(2):
                    acc = ps[:, 7, 0:4 * (GD + 1)].rearrange("p (j d) -> p j d", j=4)
                    js = slice(4 * b, 4 * b + 4)
                    dve.wait_ge(a2["ot_mm"], 2 * G + b + 1)
                    dve.reciprocal(rec[:, js], acc[:, :, GD]).then_inc(a2["rec_d"], 1)
                    dve.wait_ge(a2["rec_d"], 2 * G + b + 1)
                    dst = ysm[:, js, bass.ds(col, GD)] if kind is gqa else od[:, par, js, :]
                    dve.tensor_tensor(dst, acc[:, :, 0:GD], rec[:, js].unsqueeze(2).broadcast_to([P, 4, GD]), ALU.mult)\
                        .then_inc(a2["o_out"], 1)
                if kind is dif and par:
                    dve.wait_ge(a2["o_out"], 2 * G + 3)
                    dve.scalar_tensor_tensor(out=ysm[:, :, bass.ds(col, DV)], in0=od[:, 1, :, :], scalar=lam[:, 5:6], in1=od[:, 0, :, :],
                                             op0=ALU.mult, op1=ALU.add).then_inc(a2["head_d"], 1)

            def ahead(kind, G, par):
                for r in range(NR):
                    lo(kind, G, par, r)
                if kind is dif:
                    pass
                for j in range(ST):
                    maxima(G, j)
                max_parts(G)
                for b in range(2):
                    max_rows(kind, G, par, b)

            def step(kind, G, par, col, nxt, Gn):
                if nxt:
                    ahead(nxt, Gn, 1 - par)
                output(kind, G, par, col)

            ahead(gqa, 0, 0)
            for kind, G0, after in ((gqa, 0, dif), (dif, GH, None)):
                def col(it, par):
                    return it * (2 * GD) + par * GD if kind is gqa else it * DV + GH * GD
                with dve.Fori(0, 3) as it:
                    for par in range(2):
                        step(kind, it * 2 + (G0 + par), par, col(it, par), kind, it * 2 + (G0 + par + 1))
                step(kind, G0 + 6, 0, col(3, 0), kind, G0 + 7)
                step(kind, G0 + 7, 1, col(3, 1), after, G0 + 8)

            dve.wait_ge(a2["subg_in"], 16)
            dve.wait_ge(a2["head_d"], DH)
            sq = ring[:, 0, :].rearrange("p (t h d) -> p (t h) d", t=ST, h=DH)
            y3 = ysm[:, :, GH * GD:GH * GD + DH * DV]
            ch.link(dve.tensor_copy(ring[:, 0, :].rearrange("p (t c) -> p t c", t=ST), y3))
            ch.link(dve.tensor_tensor(ring[:, 1, :], ring[:, 0, :], ring[:, 0, :], ALU.mult))
            ch.link(dve.tensor_reduce(rst[:, 0, :], ring[:, 1, :].rearrange("p (g d) -> p g d", d=DV), AX.X, ALU.add))
            dve.tensor_scalar(rst[:, 0, :], rst[:, 0, :], 1.0 / DV, EPS, ALU.mult, ALU.add).then_inc(a2["sub_sq"], 1)
            dve.wait_ge(a2["sub_rt"], 1)
            ch.link(dve.reciprocal(rst[:, 0, :], rst[:, 1, :]))
            ch.link(dve.tensor_scalar(rst[:, 0, :], rst[:, 0, :], 1.0 - LAM_INIT, None, ALU.mult))
            ch.link(dve.tensor_tensor(sq, sq, rst[:, 0, :].unsqueeze(2).broadcast_to([P, ST * DH, DV]), ALU.mult))
            ch.link(dve.tensor_tensor(sq, sq, subg[:, :].unsqueeze(1).broadcast_to([P, ST * DH, DV]), ALU.mult))
            ch.link(dve.tensor_copy(y3, ring[:, 0, :].rearrange("p (t c) -> p t c", t=ST)))

        @block.tensor
        def _(pe):
            pe.wait_ge(a2["bc_rdy"], 1)
            for n in range(NROW):
                if n >= 2:
                    pe.wait_ge(a2["row_out"], n - 1)
                for k in range(KD):
                    i = 2 * n + k // 4
                    if k % 4 == 0:
                        pe.wait_ge(a2[f"ring{i % 2}"], 16 * (i // 2 + 1))
                    mm = pe.matmul(ps[:, n % 2, :], sbc[:, k, :], ring[:, i % 2, (k % 4) * 512:(k % 4 + 1) * 512],
                                   start=(k == 0), stop=(k == KD - 1))
                    if k % 4 == 3:
                        mm.then_inc(a2["row_mm"], 1)

            def transposes(kind, G, r, first):
                is_k, t0, nt = rounds[r]
                src = ks if is_k else qs
                if r == 0:
                    pe.wait_ge(a2["dup"], G * 2 + 2)
                    if not first:
                        pe.wait_ge(a2["o_out"], G * 2 - 1)
                else:
                    pe.wait_ge(a2["lo_d"], G * NR + r)
                if r == 2:
                    pe.wait_ge(a2["dup"], G * 2 + 3)
                for j in range(nt):
                    mm = pe.transpose(ps[0:kind.rows, 7, j * P:(j + 1) * P], src[:, t0 + j, 0:kind.rows], ident[:, :])
                mm.then_inc(a2["tr_mm"], 1)

            def max_tile(kind, G, par, j):
                if j == 0:
                    pe.wait_ge(a2["lo_d"], G * NR + NR)
                    if kind is gqa:
                        pe.wait_ge(a2["k2_cp"], G * 3 + 3)
                else:
                    pe.wait_ge(a2["max_red"], G * ST + j)
                cols = slice(j * P, (j + 1) * P)
                for b, (o, n) in enumerate(chunks):
                    mm = pe.matmul(ps[:, 4 + b, 0:n], Q1[0:kind.rows, par, cols], K1[0:kind.rows, par, o:o + n],
                                   start=True, stop=kind is dif)
                    if kind is gqa:
                        mm = pe.matmul(ps[:, 4 + b, 0:n], Q2[0:64, par, cols], K2[0:64, par, o:o + n], start=False, stop=True)
                mm.then_inc(a2["max_mm"], 1)

            def max_turn(G, b):
                if b == 0:
                    pe.wait_ge(a2["m_rdy"], G + 1)
                else:
                    pe.wait_ge(a2["mt_cp"], G * 2 + 1)
                for j in range(4):
                    mm = pe.transpose(ps[0:2, 7, j * P:(j + 1) * P], MM[:, b * 4 + j, :].bitcast(F32), ident[:, :])
                mm.then_inc(a2["mt_mm"], 1)

            def scores(kind, G, par, u):
                kt, qh = divmod(u, 2)
                if u == 0:
                    pe.wait_ge(a2["mt_cp"], G * 2 + 2)
                    if kind is dif:
                        pe.wait_ge(a2["ones_d"], par + 1)
                if u >= 2:
                    pe.wait_ge(a2["exp_d"], G * NS + (u - 1))
                keys, qrs = slice(kt * P, (kt + 1) * P), slice(qh * 512, (qh + 1) * 512)
                rows = 128 if kind is gqa else 98
                mm = pe.matmul(ps[:, u % 2, :], K1[0:rows, par, keys], Q1[0:rows, par, qrs], start=True, stop=kind is dif)
                if kind is gqa:
                    mm = pe.matmul(ps[:, u % 2, :], K2[0:66, par, keys], Q2[0:66, par, qrs], start=False, stop=True)
                mm.then_inc(a2["s_mm"], 1)

            def values(kind, G, par, u):
                kt, qh = divmod(u, 2)
                if u == 0:
                    pe.wait_ge(a2["vs_d"], G + 1)
                    pe.wait_ge(a2["acc_free"], G + 1)
                pe.wait_ge(a2["exp_d"], G * NS + (u + 1))
                mm = pe.matmul(ps[0:GD + 1, 2 + qh, :], Vs[:, par, kt, :], pT[:, u % 2, :], start=(kt == 0), stop=(kt == TT - 1))
                if u == NS - 1:
                    mm.then_inc(a2["pv_d"], 1)

            def turn_back(G, b):
                if b == 0:
                    pe.wait_ge(a2["acc_free"], G + 2)
                else:
                    pe.wait_ge(a2["o_out"], 2 * G + 2)
                for j in range(4):
                    mm = pe.transpose(ps[:, 7, j * (GD + 1):(j + 1) * (GD + 1)], OT[0:GD + 1, (4 * b + j) * P:(4 * b + j + 1) * P],
                                      ident[0:GD + 1, 0:GD + 1])
                mm.then_inc(a2["ot_mm"], 1)

            def ahead(kind, G, par, u, first=False):
                if u < NR:
                    transposes(kind, G, u, first)
                elif NR < u <= NR + ST:
                    max_tile(kind, G, par, u - NR - 1)
                elif NR + ST + 2 <= u < NR + ST + 4:
                    max_turn(G, u - NR - ST - 2)

            def step(kind, G, par, nxt, Gn):
                for u in range(NS):
                    if 1 <= u < NS - 1:
                        scores(kind, G, par, u + 1)
                    if nxt:
                        ahead(nxt, Gn, 1 - par, u)
                    values(kind, G, par, u)
                if nxt:
                    for u in range(2):
                        scores(nxt, Gn, 1 - par, u)
                for b in range(2):
                    turn_back(G, b)

            pe.wait_ge(a2["acc_free"], 1)
            for u in range(NS):
                ahead(gqa, 0, 0, u, first=True)
            for u in range(2):
                scores(gqa, 0, 0, u)
            for kind, G0, after in ((gqa, 0, dif), (dif, GH, None)):
                with pe.Fori(0, 3) as it:
                    for m in range(2):
                        step(kind, it * 2 + (G0 + m), m, kind, it * 2 + (G0 + m + 1))
                step(kind, G0 + 6, 0, kind, G0 + 7)
                step(kind, G0 + 7, 1, after, G0 + 8)
        blk.close()

        p3 = ExitStack()
        yTh = sb("yTh", [P, 2, KD, P], F32R, p3)
        yTl = sb("yTl", [P, 2, KD, P], F32R, p3)
        xt = sb("xt", [P, 2, D], F32, p3)
        ln1 = sb("ln1", [P, 2, D], F32, p3)
        res = sb("res", [P, D], F32, p3)
        x1 = sb("x1", [P, 2, D], F32, p3)
        hh = sb("hh", [P, 2, D], F32, p3)
        hT = sb("hT", [P, KD, P], F32, p3)
        rw = sb("rw", [P, KD, E], F32, p3)
        rb = sb("rb", [P, E], F32, p3)
        st3 = sb("st3", [P, 2, 16], F32, p3)
        tri = sb("tri", [P, 2, P], F32, p3)
        kc = sb("kc", [P, 8 + NBLK + 2], F32, p3)
        rt = sb("rt", [P, 12, ST * E], F32, p3)
        rsm = sb("rsm", [P, 16, ST], F32, p3)
        ecmp = sb("ecmp", [P, E * (NBLK + 2)], F32, p3)
        zrow = sb("zrow", [P, (NBLK + 1)], I32, p3)
        zeros = sb("zeros", [P, D], F32, p3)
        tokid = sb("tokid", [P, ST], I32, p3)
        p3.close()

        a3 = {n: sem(n) for n in (
            "c3_in", "g2_out", "y_zero", "xt0", "xt1", "yt_mm", "yt_hi", "yt_lo", "ya_lo", "y_mm", "y_ev", "ln_sq", "ln_rt", "x1g", "x1_done",
            "h_mul", "h_done", "x1_out0", "x1_out1", "h_out0", "h_out1", "ht_mm", "ht_cp", "lg_mm", "dve3_c", "sm_in",
            "sm_ex", "mask_d", "cnt_mm", "z_in", "z_out", "dest_d", "tok_d", "scat")}
        block = blk.enter_context(nc.Block())

        @block.sync
        def _(sp):
            for dst, name in ((ln1[:, :, :], "ln1"), (rw[:, :, :], "rw"), (rb[:, :], "rb"), (tri[:, :, :], "tri"), (kc[:, :], "kc")):
                sp.dma_start(dst, A[name]).then_inc(a3["c3_in"], 16)
            def load_x(t):
                sp.dma_start(xt[:, t % 2, :], A["x"][t * P:(t + 1) * P, :]).then_inc(a3[f"xt{t % 2}"], 16)

            load_x(0)
            load_x(1)
            sp.dma_start(g2_dram, mrow[:, 3, :]).then_inc(a3["g2_out"], 16)
            sp.wait_ge(a3["z_in"], 1)
            sp.dma_start(rows_dram.rearrange("(p n) o -> p (n o)", p=P), zrow[:, :]).then_inc(a3["z_out"], 16)
            for t in range(ST):
                if t + 2 < ST:
                    sp.wait_ge(a3["y_ev"], t + 1)
                    load_x(t + 2)
                for b in range(MINBLK + 2 * t, min(MINBLK + 2 * t + 2, NBLK + 1)):
                    sp.dma_start(y_dram[b * BLK:(b + 1) * BLK, :], zeros[:, :]).then_inc(a3["y_zero"], 16)
                sp.wait_ge(a3["x1_done"], t + 1)
                sp.dma_start(x1_dram[t * P:(t + 1) * P, :], x1[:, t % 2, :]).then_inc(a3[f"x1_out{t % 2}"], 16)
                sp.wait_ge(a3["h_done"], t + 1)
                sp.dma_start(h_dram[t * P:(t + 1) * P, :], hh[:, t % 2, :]).then_inc(a3[f"h_out{t % 2}"], 16)
            sp.wait_ge(a3["g2_out"], 16)
            sp.wait_ge(a3["y_zero"], 16 * (NBLK + 1 - MINBLK))
            for b in range(2):
                sp.wait_ge(a3[f"x1_out{b}"], 16 * ST // 2)
                sp.wait_ge(a3[f"h_out{b}"], 16 * ST // 2)

        @block.gpsimd
        def _(pool):
            pool.memset(zrow[:, :], 0)
            pool.memset(zeros[:, :], 0.0).then_inc(a3["z_in"], 1)
            pool.iota(tokid[:, :], [[P, ST]], base=0, channel_multiplier=1).then_inc(a3["tok_d"], 1)
            pool.wait_ge(a3["c3_in"], 16 * 5)

            def ya_part(t):
                pool.wait_ge(a3["yt_hi"], t + 1)
                if t >= 2:
                    pool.wait_ge(a3["y_mm"], t - 1)
                pool.tensor_tensor(yTl[:, t % 2, 0:LF, :], ya[:, :, t * P:(t + 1) * P], yTh[:, t % 2, 0:LF, :].bitcast(F32), ALU.subtract)\
                    .then_inc(a3["ya_lo"], 1)

            ya_part(0)
            for t in range(ST):
                if t + 1 < ST:
                    ya_part(t + 1)
                pool.wait_ge(a3["x1g"], t + 1)
                pool.tensor_tensor(x1[:, t % 2, :], x1[:, t % 2, :], ln1[:, 1, :], ALU.add).then_inc(a3["x1_done"], 1)
                pool.wait_ge(a3["x1_done"], t + 1)
                if t >= 2:
                    pool.wait_ge(a3[f"h_out{t % 2}"], 16 * (t // 2))
                    pool.wait_ge(a3["ht_mm"], t - 1)
                pool.tensor_tensor(hh[:, t % 2, :], x1[:, t % 2, :], mrow[:, 2, :], ALU.mult).then_inc(a3["h_mul"], 1)
            pool.wait_ge(a3["z_out"], 16)
            pool.wait_ge(a3["dest_d"], 1)
            pool.wait_ge(a3["tok_d"], 1)
            for t in range(ST):
                for c in range(2):
                    pool.indirect_dma_start(rows_dram, bass.IndirectOffsetOnAxis(ap=dest[:, c, t:t + 1], axis=0), tokid[:, t:t + 1], None)\
                        .then_inc(a3["scat"], 16)
            pool.wait_ge(a3["scat"], 16 * 2 * ST)

        @block.scalar
        def _(act):
            def hi_parts(t):
                act.wait_ge(a3["yt_mm"], t + 1)
                if t >= 2:
                    act.wait_ge(a3["y_mm"], t - 1)
                act.activation(yTh[:, t % 2, LF:KD, :].rearrange("p k m -> p (k m)"), ps[:, 0:2, :].rearrange("p a b -> p (a b)")[:, 0:(KD - LF) * P], ACT.Copy)
                act.activation(yTh[:, t % 2, 0:LF, :], ya[:, :, t * P:(t + 1) * P], ACT.Copy).then_inc(a3["yt_hi"], 1)

            def h_copy(t):
                act.wait_ge(a3["ht_mm"], t + 1)
                if t >= 1:
                    act.wait_ge(a3["lg_mm"], t)
                act.activation(hT[:, :, :].rearrange("p k m -> p (k m)"), ps[:, 6:8, :].rearrange("p a b -> p (a b)"), ACT.Copy).then_inc(a3["ht_cp"], 1)

            hi_parts(0)
            for t in range(ST):
                if t + 1 < ST:
                    hi_parts(t + 1)
                act.wait_ge(a3["ln_sq"], t + 1)
                act.activation(st3[:, t % 2, 14:15], st3[:, t % 2, 13:14], ACT.Sqrt).then_inc(a3["ln_rt"], 1)
                if t:
                    h_copy(t - 1)
            h_copy(ST - 1)
            act.wait_ge(a3["sm_in"], 1)
            act.activation(rt[:, 1, :], rt[:, 0, :], ACT.Exp).then_inc(a3["sm_ex"], 1)

        @block.vector
        def _(dve):
            ch = Chain(dve, a3["dve3_c"])
            dve.wait_ge(a3["c3_in"], 16 * 5)

            def lo_part(t):
                dve.wait_ge(a3["yt_hi"], t + 1)
                dve.tensor_tensor(yTl[:, t % 2, LF:KD, :].rearrange("p k m -> p (k m)"), ps[:, 0:2, :].rearrange("p a b -> p (a b)")[:, 0:(KD - LF) * P],
                                  yTh[:, t % 2, LF:KD, :].rearrange("p k m -> p (k m)").bitcast(F32), ALU.subtract).then_inc(a3["yt_lo"], 1)

            def shift_h(t):
                dve.wait_ge(a3["h_mul"], t + 1)
                dve.tensor_tensor(hh[:, t % 2, :], hh[:, t % 2, :], mrow[:, 1, :], ALU.add).then_inc(a3["h_done"], 1)

            lo_part(0)
            for t in range(ST):
                if t + 1 < ST:
                    lo_part(t + 1)
                s_ = st3[:, t % 2, :]
                dve.wait_ge(a3["y_mm"], t + 1)
                ch.link(dve.tensor_tensor(res[:, :].rearrange("p (a b) -> p a b", a=2), ps[:, 2:4, :],
                                          mrow[:, 0, :].rearrange("p (a b) -> p a b", a=2), ALU.mult))
                dve.wait_ge(a3[f"xt{t % 2}"], 16 * (t // 2 + 1))
                dve.scalar_tensor_tensor(out=res[:, :], in0=xt[:, t % 2, :], scalar=ALPHA, in1=res[:, :], op0=ALU.mult, op1=ALU.add)\
                    .then_inc(a3["y_ev"], 1)
                dve.wait_ge(a3["y_ev"], t + 1)
                for b in range(2):
                    ins = dve.bn_stats(s_[:, 6 * b:6 * b + 6], res[:, b * 512:(b + 1) * 512])
                ch.link(ins)
                ch.link(dve.bn_aggr(s_[:, 12:14], s_[:, 0:12]))
                dve.tensor_scalar(s_[:, 13:14], s_[:, 13:14], EPS, None, ALU.add).then_inc(a3["ln_sq"], 1)
                if t:
                    shift_h(t - 1)
                dve.wait_ge(a3["ln_rt"], t + 1)
                ch.link(dve.reciprocal(s_[:, 15:16], s_[:, 14:15]))
                ch.link(dve.tensor_scalar(res[:, :], res[:, :], s_[:, 12:13], s_[:, 15:16], ALU.subtract, ALU.mult))
                if t >= 2:
                    dve.wait_ge(a3[f"x1_out{t % 2}"], 16 * (t // 2))
                    dve.wait_ge(a3["h_mul"], t - 1)
                dve.tensor_tensor(x1[:, t % 2, :], res[:, :], ln1[:, 0, :], ALU.mult).then_inc(a3["x1g"], 1)
                dve.wait_ge(a3["x1g"], t + 1)
            shift_h(ST - 1)

            def v(i, pat="p (t e) -> p t e", **k):
                return rt[:, i, :].rearrange(pat, **(k or dict(t=ST)))

            TG = ST * G
            dve.wait_ge(a3["lg_mm"], ST)
            lg = ps[:, 4, 0:ST * E].rearrange("p (t e) -> p t e", t=ST)
            ch.link(dve.tensor_reduce(rsm[:, 0, :], lg, AX.X, ALU.max))
            dve.tensor_tensor(v(0), lg, rsm[:, 0, :].unsqueeze(2).broadcast_to([P, ST, E]), ALU.subtract).then_inc(a3["sm_in"], 1)
            dve.wait_ge(a3["sm_ex"], 1)
            ch.link(dve.tensor_reduce(rsm[:, 1, :], v(1), AX.X, ALU.add))
            ch.link(dve.reciprocal(rsm[:, 2, :], rsm[:, 1, :]))
            ch.link(dve.tensor_tensor(v(1), v(1), rsm[:, 2, :].unsqueeze(2).broadcast_to([P, ST, E]), ALU.mult))
            ch.link(dve.tensor_tensor(v(2), v(1), rb[:, :].unsqueeze(1).broadcast_to([P, ST, E]), ALU.add))

            def ranks(score, rank, tmp, n, w):
                for i in range(w):
                    ins = dve.memset(rank[:, :, i:i + 1], float(w - 1 - i))
                ch.link(ins)
                for d in range(1, w):
                    t_ = tmp[:, :, 0:w - d]
                    ch.link(dve.tensor_tensor(t_, score[:, :, 0:w - d], score[:, :, d:w], ALU.is_ge))
                    ch.link(dve.tensor_tensor(rank[:, :, d:w], rank[:, :, d:w], t_, ALU.add))
                    ch.link(dve.tensor_tensor(rank[:, :, 0:w - d], rank[:, :, 0:w - d], t_, ALU.subtract))

            g4 = lambda i: rt[:, i, :].rearrange("p (g c) -> p g c", c=EG)
            ranks(g4(2), g4(3), g4(4), TG, EG)
            ch.link(dve.tensor_scalar(rt[:, 3, :], rt[:, 3, :], 1.5, None, ALU.is_lt))
            ch.link(dve.tensor_tensor(rt[:, 4, :], rt[:, 2, :], rt[:, 3, :], ALU.mult))
            ch.link(dve.tensor_reduce(rt[:, 5, 0:TG], g4(4), AX.X, ALU.add))
            gg = lambda i: rt[:, i, 0:TG].rearrange("p (t g) -> p t g", g=G)
            ranks(gg(5), gg(6), gg(7), ST, G)
            ch.link(dve.tensor_scalar(rt[:, 6, 0:TG], rt[:, 6, 0:TG], 0.5, None, ALU.is_lt))
            dve.tensor_tensor(g4(3), g4(3), rt[:, 6, 0:TG].unsqueeze(2).broadcast_to([P, TG, EG]), ALU.mult).then_inc(a3["mask_d"], 1)
            dve.wait_ge(a3["mask_d"], 1)
            ch.link(dve.tensor_tensor(rt[:, 1, :], rt[:, 1, :], rt[:, 3, :], ALU.mult))
            ch.link(dve.tensor_reduce(rsm[:, 3, :], v(1), AX.X, ALU.add))
            ch.link(dve.reciprocal(rsm[:, 4, :], rsm[:, 3, :]))
            ch.link(dve.tensor_tensor(v(1), v(1), rsm[:, 4, :].unsqueeze(2).broadcast_to([P, ST, E]), ALU.mult))
            dve.wait_ge(a3["cnt_mm"], 1)
            ch.link(dve.tensor_copy(rt[:, 8, :], ps[:, 6, 0:ST * E]))
            ch.link(dve.memset(rt[:, 9, 0:E], 0.0))
            for t in range(ST):
                dst = rt[:, 9, (t + 1) * E:(t + 2) * E] if t + 1 < ST else rt[:, 10, 0:E]
                ch.link(dve.tensor_tensor(dst, rt[:, 9, t * E:(t + 1) * E], rt[:, 8, t * E:(t + 1) * E], ALU.add))
            ch.link(dve.tensor_tensor(ecmp[:, 0:E * 8].rearrange("p (e j) -> p e j", j=8), rt[:, 10, 0:E].unsqueeze(2).broadcast_to([P, E, 8]),
                                      kc[:, 0:8].unsqueeze(1).broadcast_to([P, E, 8]), ALU.is_gt))
            ch.link(dve.tensor_reduce(rt[:, 10, 16:32], ecmp[:, 0:E * 8].rearrange("p (e j) -> p e j", j=8), AX.X, ALU.add))
            ch.link(dve.memset(rt[:, 10, 32:48], 1.0))
            ch.link(dve.tensor_tensor_scan(rt[:, 10, 48:64], rt[:, 10, 32:48], rt[:, 10, 16:32], 0.0, ALU.mult, ALU.add))
            ch.link(dve.tensor_tensor(rt[:, 10, 64:80], rt[:, 10, 48:64], rt[:, 10, 16:32], ALU.subtract))
            ch.link(dve.tensor_scalar(rt[:, 10, 64:80], rt[:, 10, 64:80], float(BLK), None, ALU.mult))
            nb = NBLK + 2
            ch.link(dve.tensor_tensor(ecmp[:, 0:nb * E].rearrange("p (b e) -> p b e", e=E), rt[:, 10, 48:64].unsqueeze(1).broadcast_to([P, nb, E]),
                                      kc[:, 8:8 + nb].unsqueeze(2).broadcast_to([P, nb, E]), ALU.is_le))
            ch.link(dve.tensor_reduce(rt[:, 11, 0:nb], ecmp[:, 0:nb * E].rearrange("p (b e) -> p b e", e=E), AX.X, ALU.add))
            ch.link(dve.tensor_scalar(rt[:, 11, 0:nb], rt[:, 11, 0:nb], float(E - 1), None, ALU.min))
            ch.link(dve.tensor_copy(blk_tab[:, 0:nb], rt[:, 11, 0:nb]))
            ch.link(dve.tensor_copy(blk_tab[:, nb:nb + 1], rt[:, 10, 63:64]))
            ch.link(dve.tensor_tensor(v(9), v(9), rt[:, 10, 64:80].unsqueeze(1).broadcast_to([P, ST, E]), ALU.add))
            dve.wait_ge(a3["cnt_mm"], 2)
            ch.link(dve.tensor_tensor(rt[:, 9, :], rt[:, 9, :], ps[:, 7, 0:ST * E], ALU.add))
            ch.link(dve.tensor_tensor(rt[:, 9, :], rt[:, 9, :], rt[:, 3, :], ALU.mult))
            ch.link(dve.tensor_reduce(rsm[:, 5, :], v(9), AX.X, ALU.max))
            ch.link(dve.tensor_reduce(rsm[:, 6, :], v(9), AX.X, ALU.add))
            ch.link(dve.tensor_tensor(rsm[:, 6, :], rsm[:, 6, :], rsm[:, 5, :], ALU.subtract))
            ch.link(dve.tensor_tensor(v(8), v(9), rsm[:, 5, :].unsqueeze(2).broadcast_to([P, ST, E]), ALU.is_equal))
            ch.link(dve.tensor_tensor(rt[:, 8, :], rt[:, 8, :], rt[:, 1, :], ALU.mult))
            ch.link(dve.tensor_reduce(gates[:, 0, :], v(8), AX.X, ALU.add))
            ch.link(dve.tensor_tensor(rt[:, 1, :], rt[:, 1, :], rt[:, 8, :], ALU.subtract))
            ch.link(dve.tensor_reduce(gates[:, 1, :], v(1), AX.X, ALU.add))
            ch.link(dve.tensor_copy(dest[:, 0, :], rsm[:, 5, :]))
            dve.tensor_copy(dest[:, 1, :], rsm[:, 6, :]).then_inc(a3["dest_d"], 1)

        @block.tensor
        def _(pe):
            def turn_y(t):
                if t:
                    pe.wait_ge(a3["yt_lo"], t)
                for j in range(KD - LF):
                    mm = pe.transpose(ps[:, j // 4, (j % 4) * P:(j % 4 + 1) * P], ysm[:, t, j * P:(j + 1) * P], ident[:, :])
                mm.then_inc(a3["yt_mm"], 1)

            def project(t):
                pe.wait_ge(a3["yt_lo"], t + 1)
                pe.wait_ge(a3["ya_lo"], t + 1)
                if t:
                    pe.wait_ge(a3["y_ev"], t)
                for b in range(2):
                    cols = slice(b * 512, (b + 1) * 512)
                    for k in range(KD):
                        for j, (x, y) in enumerate(((yTh, woh), (yTl, woh), (yTh, wol))):
                            mm = pe.matmul(ps[:, 2 + b, :], x[:, t % 2, k, :], y[:, k, cols], start=(k == 0 and j == 0), stop=(k == KD - 1 and j == 2))
                mm.then_inc(a3["y_mm"], 1)

            def turn_h(t):
                pe.wait_ge(a3["h_done"], t + 1)
                if t:
                    pe.wait_ge(a3["ht_cp"], t)
                for k in range(KD):
                    mm = pe.transpose(ps[:, 6 + k // 4, (k % 4) * P:(k % 4 + 1) * P], hh[:, t % 2, k * P:(k + 1) * P], ident[:, :])
                mm.then_inc(a3["ht_mm"], 1)

            def route(t):
                pe.wait_ge(a3["ht_cp"], t + 1)
                pe.wait_ge(a3["c3_in"], 16 * 5)
                for k in range(KD):
                    mm = pe.matmul(ps[:, 4, t * E:(t + 1) * E], hT[:, k, :], rw[:, k, :], start=(k == 0), stop=(k == KD - 1))
                mm.then_inc(a3["lg_mm"], 1)

            turn_y(0)
            for t in range(ST):
                if t + 1 < ST:
                    turn_y(t + 1)
                project(t)
                if t:
                    turn_h(t - 1)
                    route(t - 1)
            turn_h(ST - 1)
            route(ST - 1)
            pe.wait_ge(a3["mask_d"], 1)
            for j, b in ((1, 6), (0, 7)):
                pe.matmul(ps[:, b, 0:ST * E], tri[:, j, :], rt[:, 3, :], start=True, stop=True).then_inc(a3["cnt_mm"], 1)
        blk.close()
        attn.close()

        p4 = ExitStack()
        wraw4 = sb("wraw4", [P, NUNIT, D], F32, p4)
        whi4 = sb("whi4", [P, NUNIT, D], F32R, p4)
        wlo4 = sb("wlo4", [P, NUNIT, D], F32R, p4)
        xg = sb("xg", [P, D], F32, p4)
        xTh = sb("xTh", [P, KD, P], F32R, p4)
        xTl = sb("xTl", [P, KD, P], F32R, p4)
        hs = sb("hs", [P, FF], F32, p4)
        hTh = sb("hTh", [P, FK, P], F32R, p4)
        hTl = sb("hTl", [P, FK, P], F32R, p4)
        ys = sb("ys", [P, D], F32, p4)
        row_all = sb("row_all", [P, NBLK + 1], I32, p4)
        row_ix = sb("row_ix", [P, 2], I32, p4)
        tok4 = sb("tok4", [P, 2], F32, p4)
        p4.close()
        a4 = {n: sem(n) for n in (
            *(f"raw{p}" for p in range(NUNIT // 2)), "rows_in", "passed4", "passed4_sp", "whi_d", "wlo_d", "wlo_p", "used", "xg_in", "ix_d", "xt_mm", "xt_hi", "xt_lo",
            "silu_d", "mul_d", "ht_mm4", "ht_hi4", "ht_lo4", "y_ev4", "y_free")}
        block = blk.enter_context(nc.Block())
        POOL_UNITS = (1, 4, 7, 10)
        DVE_UNITS = tuple(u for u in range(NUNIT) if u not in POOL_UNITS)

        def lo_ready(eng, b, u, passed=None):
            name, mine = ("wlo_p", POOL_UNITS) if u in POOL_UNITS else ("wlo_d", DVE_UNITS)
            count = b * len(mine) + (mine.index(u) + 1)
            if passed:
                wait_apart(eng, a4[name], count, passed)
            else:
                eng.wait_ge(a4[name], count)

        def block_count(eng):
            return eng.value_load(blk_tab[0:1, NBLK + 2:NBLK + 3], min_val=1, max_val=NBLK)

        def lo_unit(eng, name, b, u):
            eng.wait_ge(a4["whi_d"], b * NUNIT + (u + 1))
            eng.tensor_tensor(wlo4[:, u, :], wraw4[:, u, :], whi4[:, u, :].bitcast(F32), ALU.subtract).then_inc(a4[name], 1)

        @block.sync
        def _(sp):
            def load(b, p):
                e = sp.value_load(blk_tab[0:1, bass.ds(b, 1)], min_val=0, max_val=E - 1)
                sp.dma_start(wraw4[:, 2 * p:2 * p + 2, :], A["wexp"][bass.ds(e, 1), :, 2 * p:2 * p + 2, :].rearrange("o p u n -> p (o u) n"))\
                    .then_inc(a4[f"raw{p}"], 16)

            sp.dma_start(row_all[:, :], rows_dram.rearrange("(b p) o -> p (b o)", p=P), allow_slow_non_contiguous=True).then_inc(a4["rows_in"], 16)
            for p in range(NUNIT // 2):
                load(0, p)
            for p in range(NUNIT // 2):
                lo_ready(sp, 0, 2 * p)
                lo_ready(sp, 0, 2 * p + 1)
                load(1, p)
            nb = block_count(sp)
            with sp.Fori(0, NBLK) as b:
                with sp.If(b < nb):
                    for p in range(NUNIT // 2):
                        lo_ready(sp, b + 1, 2 * p, a4["passed4_sp"])
                        lo_ready(sp, b + 1, 2 * p + 1, a4["passed4_sp"])
                        load(b + 2, p)
                    sp.wait_ge(a4["y_ev4"], b + 2)
                    sp.dma_start(y_dram[bass.ds(b * BLK, BLK), :], ys[:, :]).then_inc(a4["y_free"], 16)
            wait_apart(sp, a4["y_free"], nb * 16 + 16, a4["passed4_sp"])
            for p in range(NUNIT // 2):
                wait_apart(sp, a4[f"raw{p}"], nb * 16 + 32, a4["passed4_sp"])

        @block.gpsimd
        def _(pool):
            def gather(b, col):
                pool.tensor_copy(row_ix[:, 0:1], col).then_inc(a4["ix_d"], 1)
                wait_apart(pool, a4["ix_d"], b + 1, a4["passed4"])
                pool.indirect_dma_start(xg[:, :], None, h_dram, bass.IndirectOffsetOnAxis(ap=row_ix[:, 0:1], axis=0)).then_inc(a4["xg_in"], 16)

            pool.wait_ge(a4["rows_in"], 16)
            gather(0, row_all[:, 0:1])
            for u in POOL_UNITS:
                lo_unit(pool, "wlo_p", 0, u)
            nb = block_count(pool)
            with pool.Fori(0, NBLK) as b:
                with pool.If(b < nb):
                    wait_apart(pool, a4["xt_mm"], b + 1, a4["passed4"])
                    gather(b + 1, row_all[:, bass.ds(b + 1, 1)])
                    for u in POOL_UNITS:
                        lo_unit(pool, "wlo_p", b + 1, u)

        @block.scalar
        def _(act):
            def hi_unit(b, u, first=False):
                act.wait_ge(a4[f"raw{u // 2}"], b * 16 + 16)
                if not first:
                    act.wait_ge(a4["used"], (b - 1) * NUNIT + (u + 1))
                act.activation(whi4[:, u, :], wraw4[:, u, :], ACT.Copy).then_inc(a4["whi_d"], 1)

            def xt_hi(b):
                act.wait_ge(a4["xt_mm"], b + 1)
                act.activation(xTh[:, :, :].rearrange("p k m -> p (k m)"), ps[:, 2:4, :].rearrange("p a b -> p (a b)"), ACT.Copy)\
                    .then_inc(a4["xt_hi"], 1)

            for u in range(NUNIT):
                hi_unit(0, u, first=True)
                if u == 3:
                    xt_hi(0)
            nb = block_count(act)
            with act.Fori(0, NBLK) as b:
                with act.If(b < nb):
                    for u in range(KD - 1):
                        hi_unit(b + 1, u)
                    act.wait_ge(a4["used"], b * NUNIT + KD)
                    act.activation(hs[:, :], ps[:, 0, :], ACT.Silu).then_inc(a4["silu_d"], 1)
                    hi_unit(b + 1, KD - 1)
                    act.wait_ge(a4["ht_mm4"], b + 1)
                    act.activation(hTh[:, :, :].rearrange("p k m -> p (k m)"), ps[:, 4, :], ACT.Copy).then_inc(a4["ht_hi4"], 1)
                    xt_hi(b + 1)
                    for u in range(KD, NUNIT):
                        hi_unit(b + 1, u)

        @block.vector
        def _(dve):
            def xt_lo(b):
                dve.wait_ge(a4["xt_hi"], b + 1)
                dve.tensor_tensor(xTl[:, :, :].rearrange("p k m -> p (k m)"), ps[:, 2:4, :].rearrange("p a b -> p (a b)"),
                                  xTh[:, :, :].rearrange("p k m -> p (k m)").bitcast(F32), ALU.subtract).then_inc(a4["xt_lo"], 1)

            dve.memset(tok4[:, 0:1], 0.0).then_inc(a4["y_ev4"], 1)
            dve.memset(tok4[:, 1:2], 0.0).then_inc(a4["y_free"], 16)
            for u in DVE_UNITS:
                lo_unit(dve, "wlo_d", 0, u)
                if u == 3:
                    xt_lo(0)
            nb = block_count(dve)
            with dve.Fori(0, NBLK) as b:
                with dve.If(b < nb):
                    for u in DVE_UNITS:
                        if u == KD:
                            dve.wait_ge(a4["silu_d"], b + 1)
                            dve.tensor_tensor(hs[:, :], hs[:, :], ps[:, 1, :], ALU.mult).then_inc(a4["mul_d"], 1)
                            dve.wait_ge(a4["ht_hi4"], b + 1)
                            dve.tensor_tensor(hTl[:, :, :].rearrange("p k m -> p (k m)"), ps[:, 4, :],
                                              hTh[:, :, :].rearrange("p k m -> p (k m)").bitcast(F32), ALU.subtract).then_inc(a4["ht_lo4"], 1)
                            xt_lo(b + 1)
                        lo_unit(dve, "wlo_d", b + 1, u)
                    dve.wait_ge(a4["used"], b * NUNIT + NUNIT)
                    dve.wait_ge(a4["y_free"], b * 16 + 16)
                    dve.tensor_copy(ys[:, :].rearrange("p (a b) -> p a b", a=2), ps[:, 5:7, :]).then_inc(a4["y_ev4"], 1)

        @block.tensor
        def _(pe):
            def turn_x(b, first=False):
                pe.wait_ge(a4["xg_in"], b * 16 + 16)
                if not first:
                    pe.wait_ge(a4["xt_lo"], b)
                for k in range(KD):
                    mm = pe.transpose(ps[:, 2 + k // 4, (k % 4) * P:(k % 4 + 1) * P], xg[:, k * P:(k + 1) * P], ident[:, :])
                mm.then_inc(a4["xt_mm"], 1)

            def product(b, u, lhs_hi, lhs_lo, bank, first, last):
                lo_ready(pe, b, u)
                for half in range(2):
                    cols = slice(half * 512, (half + 1) * 512)
                    for j, (x, y) in enumerate(((lhs_hi, whi4), (lhs_lo, whi4), (lhs_hi, wlo4))):
                        mm = pe.matmul(ps[:, bank + half, :], x, y[:, u, cols], start=first and j == 0, stop=last and j == 2)
                mm.then_inc(a4["used"], 1)

            turn_x(0, first=True)
            nb = block_count(pe)
            with pe.Fori(0, NBLK) as b:
                with pe.If(b < nb):
                    pe.wait_ge(a4["xt_lo"], b + 1)
                    for k in range(KD):
                        product(b, k, xTh[:, k, :], xTl[:, k, :], 0, k == 0, k == KD - 1)
                    turn_x(b + 1)
                    pe.wait_ge(a4["mul_d"], b + 1)
                    for k in range(FK):
                        mm = pe.transpose(ps[:, 4, k * P:(k + 1) * P], hs[:, k * P:(k + 1) * P], ident[:, :])
                    mm.then_inc(a4["ht_mm4"], 1)
                    pe.wait_ge(a4["ht_lo4"], b + 1)
                    pe.wait_ge(a4["y_ev4"], b + 1)
                    for k in range(FK):
                        product(b, KD + k, hTh[:, k, :], hTl[:, k, :], 5, k == 0, k == FK - 1)
        blk.close()

        p5 = ExitStack()
        yg = sb("yg", [P, 3, 2, D], F32, p5)
        x1t = sb("x1t", [P, 3, D], F32, p5)
        r5 = sb("r5", [P, 2, D], F32, p5)
        o5 = sb("o5", [P, 2, D], F32, p5)
        g2row = sb("g2row", [P, D], F32, p5)
        ln2 = sb("ln2", [P, 2, D], F32, p5)
        st5 = sb("st5", [P, 2, 16], F32, p5)
        p5.close()
        a5 = {n: sem(n) for n in ("c5_in", "yg0", "yg1", "yg2", "x1t0", "x1t1", "x1t2", "y_sum", "var_d", "root_d", "norm_d", "gain_d", "fin_d",
                                  "fin_out0", "fin_out1", "dve5_c")}
        block = blk.enter_context(nc.Block())

        @block.sync
        def _(sp):
            sp.dma_start(g2row[:, :], g2_dram).then_inc(a5["c5_in"], 16)
            sp.dma_start(ln2[:, :, :], A["ln2"]).then_inc(a5["c5_in"], 16)

            def load_x1(t):
                sp.dma_start(x1t[:, t % 3, :], x1_dram[t * P:(t + 1) * P, :]).then_inc(a5[f"x1t{t % 3}"], 16)

            for t in range(3):
                load_x1(t)
            for t in range(ST):
                if t + 3 < ST:
                    sp.wait_ge(a5["y_sum"], t + 1)
                    load_x1(t + 3)
                sp.wait_ge(a5["fin_d"], t + 1)
                sp.dma_start(out[0, t * P:(t + 1) * P, :], o5[:, t % 2, :]).then_inc(a5[f"fin_out{t % 2}"], 16)
            for b in range(2):
                sp.wait_ge(a5[f"fin_out{b}"], 16 * (ST // 2))

        @block.gpsimd
        def _(pool):
            def gather(t):
                if t >= 3:
                    pool.wait_ge(a5["y_sum"], t - 2)
                for c in range(2):
                    pool.indirect_dma_start(yg[:, t % 3, c, :], None, y_dram, bass.IndirectOffsetOnAxis(ap=dest[:, c, t:t + 1], axis=0))\
                        .then_inc(a5[f"yg{t % 3}"], 16)

            for t in range(2):
                gather(t)
            pool.wait_ge(a5["c5_in"], 32)
            for t in range(ST):
                if t + 2 < ST:
                    gather(t + 2)
                pool.wait_ge(a5["norm_d"], t + 1)
                if t >= 2:
                    pool.wait_ge(a5[f"fin_out{t % 2}"], 16 * (t // 2))
                pool.tensor_tensor(o5[:, t % 2, :], r5[:, t % 2, :], ln2[:, 0, :], ALU.mult).then_inc(a5["gain_d"], 1)

        @block.scalar
        def _(act):
            for t in range(ST):
                act.wait_ge(a5["var_d"], t + 1)
                act.activation(st5[:, t % 2, 14:15], st5[:, t % 2, 13:14], ACT.Sqrt).then_inc(a5["root_d"], 1)

        @block.vector
        def _(dve):
            ch = Chain(dve, a5["dve5_c"])
            dve.wait_ge(a5["c5_in"], 32)

            def shift(t):
                dve.wait_ge(a5["gain_d"], t + 1)
                dve.tensor_tensor(o5[:, t % 2, :], o5[:, t % 2, :], ln2[:, 1, :], ALU.add).then_inc(a5["fin_d"], 1)

            for t in range(ST):
                s_, r = st5[:, t % 2, :], r5[:, t % 2, :]
                dve.wait_ge(a5[f"yg{t % 3}"], 32 * (t // 3 + 1))
                if t >= 2:
                    dve.wait_ge(a5["gain_d"], t - 1)
                ch.link(dve.tensor_scalar(r, yg[:, t % 3, 0, :], gates[:, 0, t:t + 1], None, ALU.mult))
                ch.link(dve.scalar_tensor_tensor(out=r, in0=yg[:, t % 3, 1, :], scalar=gates[:, 1, t:t + 1], in1=r, op0=ALU.mult, op1=ALU.add))
                ch.link(dve.tensor_tensor(r, r, g2row[:, :], ALU.mult))
                dve.wait_ge(a5[f"x1t{t % 3}"], 16 * (t // 3 + 1))
                dve.scalar_tensor_tensor(out=r, in0=x1t[:, t % 3, :], scalar=ALPHA, in1=r, op0=ALU.mult, op1=ALU.add).then_inc(a5["y_sum"], 1)
                dve.wait_ge(a5["y_sum"], t + 1)
                for b in range(2):
                    ins = dve.bn_stats(s_[:, 6 * b:6 * b + 6], r5[:, t % 2, b * 512:(b + 1) * 512])
                ch.link(ins)
                ch.link(dve.bn_aggr(s_[:, 12:14], s_[:, 0:12]))
                dve.tensor_scalar(s_[:, 13:14], s_[:, 13:14], EPS, None, ALU.add).then_inc(a5["var_d"], 1)
                if t:
                    shift(t - 1)
                dve.wait_ge(a5["root_d"], t + 1)
                ch.link(dve.reciprocal(s_[:, 15:16], s_[:, 14:15]))
                dve.tensor_scalar(r, r, s_[:, 12:13], s_[:, 15:16], ALU.subtract, ALU.mult).then_inc(a5["norm_d"], 1)
            shift(ST - 1)
        blk.close()


def layouts(inputs):
    import numpy as np
    a = {k: np.asarray(v) for k, v in inputs.items()}
    o = {}
    o["xT"] = np.concatenate([a["x"][0], a["ctx"][0]], 0).T
    o["x"] = a["x"][0]
    o["cvec"] = np.stack([a["c"][0], a["c_ctx"]], -1).reshape(KD, P, 2).transpose(1, 0, 2)
    o["ada_w"] = a["ada_w"][0]
    o["adab_cols"] = a["ada_b"][0][0:2048].reshape(16, P).T
    o["adab_rows"] = np.broadcast_to(a["ada_b"][0][2048:], (P, 4096)).reshape(P, 4, D)
    w = a["w_in"][0]
    ax_, ag, gq, gk, gv, dq, dk, dv = np.split(w, np.cumsum([256, 256, 512, 128, 128, 256, 256]).tolist(), axis=1)
    o["w_in"] = np.concatenate([ax_, ag, gq, gv, gk, dk, dv, dq], 1)
    o["ident"] = np.eye(P, dtype=np.float32)

    def rope(dim):
        t = np.arange(S)
        n = dim // 4
        inv = np.float32(10000.0) ** (-np.arange(n, dtype=np.float32) / np.float32(n))
        ang = np.concatenate([(t // 64).astype(np.float32)[:, None] * inv, (t % 64).astype(np.float32)[:, None] * inv], -1)
        c, s_ = np.cos(ang), np.sin(ang)
        tab = np.stack([np.stack([c, c], -1).reshape(S, dim), np.stack([-s_, s_], -1).reshape(S, dim)], 1)
        return tab.reshape(ST, P, 2, dim).transpose(1, 0, 2, 3).astype(np.float32)

    o["rope_g"], o["rope_d"] = rope(GD), rope(DQ)
    swap = np.arange(GD).reshape(-1, 2)[:, ::-1].reshape(-1)
    o["gvec"] = np.broadcast_to(np.stack([np.stack([g[0], g[0][swap]]) for g in (a["q_norm_g"], a["k_norm_g"])]), (P, 2, 2, GD))
    o["lvec"] = np.broadcast_to(a["diff_lambda"][0], (P, 4, DQ))
    cols = [a["conv_w"][0][k] for k in range(4)] + [a["conv_b"][0]] + [a[n][0][d] for n in ("rg_ba", "rg_bx", "rg_lam") for d in range(2)]
    cols += [cols[0]] * 5
    o["lruc"] = np.stack(cols, -1).reshape(LF, P, 16).transpose(1, 0, 2)
    g = np.stack([a["rg_wa"][0], a["rg_wx"][0]], 1)
    g = g.reshape(2, 2, LF, 2, 64, 64)
    o["wg"] = g.transpose(3, 4, 2, 0, 1, 5).reshape(2, 64, 8, 64)
    o["subg"] = np.broadcast_to(a["diff_subln_g"][0], (P, DV))
    o["w_out"] = a["w_out"][0]
    o["ln1"] = np.broadcast_to(np.stack([a["ln1_g"][0], a["ln1_b"][0]]), (P, 2, D))
    o["rw"] = a["router_w"].reshape(KD, P, E).transpose(1, 0, 2)
    o["rb"] = np.broadcast_to(a["router_b"], (P, E))
    o["tri"] = np.stack([np.triu(np.ones((P, P), np.float32), 1), np.ones((P, P), np.float32)], 1)
    o["kc"] = np.broadcast_to(np.concatenate([np.arange(8) * BLK, np.arange(NBLK + 2)]).astype(np.float32), (P, 8 + NBLK + 2))
    gu = np.concatenate([a["exp_w_gate"][0], a["exp_w_up"][0]], -1).reshape(E, KD, P, D)
    o["wexp"] = np.concatenate([gu, a["exp_w_down"][0].reshape(E, FK, P, D)], 1).transpose(0, 2, 1, 3)
    o["ln2"] = np.broadcast_to(np.stack([a["ln2_g"][0], a["ln2_b"][0]]), (P, 2, D))
    return {k: np.ascontiguousarray(v) for k, v in o.items()}


def kernel(**inputs):
    import concourse.bacc as bacc
    from concourse.bass_utils import run_bass_kernel_spmd
    nc = bacc.Bacc("TRN2", target_bir_lowering=False, num_devices=1)
    arrays = layouts(inputs)
    A = {n: nc.dram_tensor(f"in_{n}", v.shape, mybir.dt.from_np(v.dtype), kind="ExternalInput").ap() for n, v in arrays.items()}
    out = nc.dram_tensor("out", (1, S, D), F32, kind="ExternalOutput").ap()
    build(nc, A, out)
    r = run_bass_kernel_spmd(nc, [{f"in_{n}": v for n, v in arrays.items()}], core_ids=[0])
    return r.results[0]["out"]
```

```python
from contextlib import ExitStack

import concourse.bass as bass
from concourse import mybir

F32 = mybir.dt.float32
F32R = mybir.dt.float32r
I32 = mybir.dt.int32
ALU = mybir.AluOpType
ACT = mybir.ActivationFunctionType
AX = mybir.AxisListType

P = 128
D = 1024
KD = D // P
S = 1024
C = 256
T = S + C
ST, CT = S // P, C // P
TT = ST + CT
LRU = 256
LF = LRU // P
GH, GKV, GD = 8, 2, 64
DH, DQ, DV = 4, 32, 64
LAM_INIT = 0.8 - 0.6
EPS = 1e-6
RG_C = 8.0
ALPHA = 2.0 ** 0.25
CONV = 4
PADL = 1 + S + 3 + C + 2
UL = PADL - (CONV - 1)
UC = S + 3
E, G, EG, FF = 16, 4, 4, 512
FK = FF // P
NUNIT = KD + FK
BLK = P
NBLK = 2 * S // BLK + E - 1
MINBLK = 2 * S // BLK
ROWS = (NBLK + 1) * BLK


class Chain:

    def __init__(self, engine, sem):
        self.engine, self.sem, self.base, self.n = engine, sem, 0, 0

    def begin(self, base):
        self.base, self.n = base, 0

    def mark(self, ins):
        self.n += 1
        ins.then_inc(self.sem, 1)

    def wait(self):
        self.engine.wait_ge(self.sem, self.base + self.n)

    def link(self, ins):
        self.mark(ins)
        self.wait()


def wait_apart(engine, sem, value, passed):
    engine.wait_ge(sem, value)
    engine.sem_inc(passed, 1)


def build(nc, A, out):
    def dram(name, shape, dt=F32):
        return nc.dram_tensor(name, shape, dt, kind="Internal").ap()

    q_dram = dram("q_dram", (S, GH * GD))
    k_dram = dram("k_dram", (T, GKV * GD + DH * 2 * DQ))
    dq_dram = dram("dq_dram", (S, DH * 2 * DQ))
    x1_dram, h_dram = dram("x1_dram", (S, D)), dram("h_dram", (S, D))
    g2_dram = dram("g2_dram", (P, D))
    rows_dram = dram("rows_dram", (ROWS, 1), I32)
    y_dram = dram("y_dram", (ROWS, D))

    with ExitStack() as whole:
        def sb(name, shape, dt=F32, at=whole):
            return at.enter_context(nc.sbuf_tensor(name, shape, dt))

        def sem(name):
            return whole.enter_context(nc.semaphore(name))

        ps = whole.enter_context(nc.psum_tensor("ps", [P, 8, 512], F32))
        ident = sb("ident", [P, P])
        dest = sb("dest", [P, 2, ST], I32)
        gates = sb("gates", [P, 2, ST])
        blk_tab = sb("blk_tab", [P, NBLK + 3], I32)
        attn = ExitStack()
        V = sb("V", [P, TT, GKV, GD + 1], F32, attn)
        DVt = sb("DVt", [P, TT, DH, DV + 1], F32, attn)
        ya = sb("ya", [P, LF, S], F32, attn)
        lam = sb("lam", [P, 8], F32, attn)
        silu_c = sb("silu_c", [P, KD, 2], F32, attn)

        p1 = ExitStack()
        cvec = sb("cvec", [P, KD, 2], F32, p1)
        xhi = sb("xhi", [P, KD, T], F32R, p1)
        xlo = sb("xlo", [P, KD, T], F32R, p1)
        whi = sb("whi", [P, KD, 512], F32R, p1)
        wlo = sb("wlo", [P, KD, 512], F32R, p1)
        NWR = 4
        wraw = sb("wraw", [P, NWR, 512], F32, p1)
        ax = sb("ax", [P, LF, PADL], F32, p1)
        rope_q = sb("rope_q", [P, ST, 2, GD], F32, p1)
        rope_k = sb("rope_k", [P, ST, 2, GD], F32, p1)
        rope_d = sb("rope_d", [P, ST, 2, DQ], F32, p1)
        gvec = sb("gvec", [P, 2, 2, GD], F32, p1)
        lvec = sb("lvec", [P, 4, DQ], F32, p1)
        modc = sb("modc", [P, 16, 2], F32, p1)
        adab = sb("adab", [P, 16], F32, p1)
        lruc = sb("lruc", [P, LF, 16], F32, p1)
        nsp = sb("nsp", [P, LF, 2, 2], F32, p1)
        stat = sb("stat", [P, 2, 3, 8], F32, p1)
        wg = sb("wg", [P, 8, P], F32, p1)
        pa = ExitStack()
        NAR = 2
        adar = sb("adar", [P, NAR, 2048], F32, pa)
        xraw = sb("xraw", [P, 2, T], F32, pa)
        pa.close()
        pl = ExitStack()
        U = sb("U", [P, LF, UL], F32, pl)
        TH = sb("TH", [P, UL], F32, pl)
        SQ = sb("SQ", [P, UL], F32, pl)
        H = sb("H", [P, S], F32, pl)
        zst = sb("zst", [P, 2, 512], F32, pl)
        zo = sb("zo", [P, 2, 512], F32, pl)
        pl.close()
        p1.close()
        R = ax[:, 0, 0:UL]
        I = ax[:, 1, 0:UL]

        passed = sem("passed")
        s = {n: sem(n) for n in (
            "consts", "mod_b", "c_in", "silu", "adar0", "adar1", "ada_used",
            "xraw0", "xraw1", "x_mod", "x_hi", "x_lo",
            "wraw0", "wraw1", "wraw2", "wraw3", "w_hi", "w_lo", "w_used",
            "proj_done", "proj_out", "prep", "wg_zero", "wg_load", "z_sq", "z_rt", "z_fin", "zo_out0", "zo_out1",
            "u_ready", "gate_mm", "gate_sig", "a_rdy", "m_neg", "m_rt",
            "lru_done", "dve_c", "act_c", "sp_rdy", "nsp_rdy")}
        blk = ExitStack()
        block = blk.enter_context(nc.Block())

        units = [("L", f, o, n) for f in range(LF) for o, n in ((0, 512), (512, 512), (S, C))] + \
                [("L", LF + f, o, 512) for f in range(LF) for o in (0, 512)]
        NL = len(units)
        units += [("Q", t) for t in range(ST)] + [("K", t) for t in range(TT)] + [("E", t) for t in range(TT)]
        group = {"L": 0, "Q": 1, "K": 2, "E": 3}
        last_of = [max(i for i, u in enumerate(units) if group[u[0]] == g) for g in range(4)]
        z_units = [i for i, u in enumerate(units) if u[0] in "QK" or (u[0] == "E" and u[1] < ST)]
        z_of = {u: n for n, u in enumerate(z_units)}
        NU, RING = len(units), 4
        combos = [(f, d) for f in range(LF) for d in range(2)]
        gate_at = {NL + 1 + 3 * c + g: (c, g) for c in range(4) for g in range(2)}
        CONSTS = 16 * 7

        def w_free(eng, c):
            g, k = divmod(c, KD)
            if g and k < KD - 1:
                eng.wait_ge(s["w_used"], (g - 1) * (KD - 1) + k + 1)
            elif g:
                eng.wait_ge(s["proj_done"], last_of[g - 1] + 1)

        @block.sync
        def _(sp):
            sp.dma_start(cvec[:, :, :], A["cvec"]).then_inc(s["c_in"], 16)
            sp.dma_start(adab[:, :], A["adab_cols"]).then_inc(s["mod_b"], 16)
            for k in range(KD):
                if k >= NAR:
                    sp.wait_ge(s["ada_used"], k - NAR + 1)
                sp.dma_start(adar[:, k % NAR, :], A["ada_w"][k * P:(k + 1) * P, 0:2048]).then_inc(s[f"adar{k % NAR}"], 16)

            def load_w(c):
                g, k = divmod(c, KD)
                if c >= NWR:
                    sp.wait_ge(s["w_lo"], c - NWR + 1)
                sp.dma_start(wraw[:, c % NWR, :], A["w_in"][k * P:(k + 1) * P, g * 512:(g + 1) * 512])\
                    .then_inc(s[f"wraw{c % NWR}"], 16)

            for k in range(KD):
                if k >= 2:
                    sp.wait_ge(s["x_lo"], k - 1)
                sp.dma_start(xraw[:, k % 2, :], A["xT"][k * P:(k + 1) * P, :]).then_inc(s[f"xraw{k % 2}"], 16)
                load_w(k)
            for dst, name in ((ident[:, :], "ident"), (rope_q[:, :, :, :], "rope_g"), (rope_k[:, :, :, :], "rope_g"),
                              (rope_d[:, :, :, :], "rope_d"), (gvec[:, :, :, :], "gvec"), (lvec[:, :, :], "lvec"),
                              (lruc[:, :, :], "lruc")):
                sp.dma_start(dst, A[name]).then_inc(s["consts"], 16)
            sp.wait_ge(s["wg_zero"], 1)
            for b in range(2):
                sp.dma_start(wg[b * 64:(b + 1) * 64, :, b * 64:(b + 1) * 64], A["wg"][b]).then_inc(s["wg_load"], 16)

            def store_z(i):
                n, (kind, t) = z_of[i], units[i]
                rows = slice(t * P, (t + 1) * P)
                dst, lo = {"Q": (q_dram, 0), "K": (k_dram, 128), "E": (dq_dram, 256)}[kind]
                sp.wait_ge(s["z_fin"], n + 1)
                sp.dma_start(dst[rows, :], zo[:, n % 2, lo:512]).then_inc(s[f"zo_out{n % 2}"], 16)

            for c in range(KD, 2 * KD):
                load_w(c)
            for g in range(1, 4):
                mine = [i for i in z_units if group[units[i][0]] == g]
                for c in range((g + 1) * KD, (g + 1) * KD + NWR if g < 3 else 0):
                    load_w(c)
                for i in mine[:-1]:
                    store_z(i)
                for c in range((g + 1) * KD + NWR, (g + 2) * KD if g < 3 else 0):
                    load_w(c)
                store_z(mine[-1])
            for b in range(2):
                sp.wait_ge(s[f"zo_out{b}"], 16 * len(z_units[b::2]))

        @block.gpsimd
        def _(pool):
            pool.memset(V[:, :, :, GD:GD + 1], 1.0)
            pool.memset(DVt[:, :, :, DV:DV + 1], 1.0)
            pool.memset(ax[:, :, :], 0.0).then_inc(s["prep"], 1)
            pool.memset(wg[:, :, :], 0.0).then_inc(s["wg_zero"], 1)
            for c in range(4 * KD):
                pool.wait_ge(s["w_hi"], c + 1)
                pool.tensor_tensor(wlo[:, c % KD, :], wraw[:, c % NWR, :], whi[:, c % KD, :].bitcast(F32), ALU.subtract)\
                    .then_inc(s["w_lo"], 1)

        @block.scalar
        def _(act):
            ch = Chain(act, s["act_c"])
            act.wait_ge(s["c_in"], 16)
            act.activation(silu_c[:, :, :], cvec[:, :, :], ACT.Silu).then_inc(s["silu"], 1)

            def w_hi(c):
                act.wait_ge(s[f"wraw{c % NWR}"], 16 * (c // NWR + 1))
                w_free(act, c)
                act.activation(whi[:, c % KD, :], wraw[:, c % NWR, :], ACT.Copy).then_inc(s["w_hi"], 1)

            for k in range(KD):
                act.wait_ge(s["x_mod"], k + 1)
                act.activation(xhi[:, k, :], xraw[:, k % 2, :], ACT.Copy).then_inc(s["x_hi"], 1)
                w_hi(k)

            def sqrt_rms(i):
                n, nh = z_of[i], {"Q": GH, "K": GKV}[units[i][0]]
                act.wait_ge(s["z_sq"], n + 1)
                act.activation(stat[:, n % 2, 1, 0:nh], stat[:, n % 2, 0, 0:nh], ACT.Sqrt).then_inc(s["z_rt"], 1)

            def lru_gate(c, g):
                f, d = combos[c]
                act.wait_ge(s["gate_mm"], 2 * c + g + 1)
                if g == 0 and c:
                    act.wait_ge(s["lru_done"], c)
                act.activation(R if g == 0 else I, ps[:, 0:3, :].rearrange("p a b -> p (a b)")[:, 0:UL], ACT.Sigmoid,
                               bias=lruc[:, f, 5 + 2 * g + d:6 + 2 * g + d]).then_inc(s["gate_sig"], 1)
                if g == 1:
                    act.wait_ge(s["gate_sig"], 2 * c + 2)
                    act.wait_ge(s["nsp_rdy"], 1)
                    ch.link(act.activation(TH[:, :], R, ACT.Tanh, scale=nsp[:, f, d:d + 1, 0]))
                    act.activation(R, R, ACT.Exp, scale=nsp[:, f, d:d + 1, 0]).then_inc(s["a_rdy"], 1)

            def lru_root(c):
                act.wait_ge(s["m_neg"], c + 1)
                act.activation(TH[:, :], TH[:, :], ACT.Sqrt, scale=-1.0).then_inc(s["m_rt"], 1)

            for i, u in enumerate(units):
                if i in last_of and i != NU - 1:
                    for k in range(KD):
                        w_hi((group[u[0]] + 1) * KD + k)
                act.wait_ge(s["proj_done"], i + 1)
                src = ps[:, 4 + i % RING, :]
                if i == 0:
                    act.wait_ge(s["prep"], 1)
                if i == NL:
                    act.wait_ge(s["consts"], CONSTS)
                    for f in range(LF):
                        ch.link(act.activation(nsp[:, f, :, 1], lruc[:, f, 9:11], ACT.Exp, scale=-1.0))
                        ins = act.activation(nsp[:, f, :, 0], nsp[:, f, :, 1], ACT.Ln, bias=1.0)
                    ins.then_inc(s["sp_rdy"], 1)
                if u[0] == "L":
                    _, f, o, n = u
                    if f < LF:
                        at = 1 + o if o < S else UC + 1
                        last = act.activation(ax[:, f, at:at + n], src[:, 0:n], ACT.Copy)
                    else:
                        last = act.activation(ya[:, f - LF, o:o + n], src[:, 0:n], ACT.Gelu_apprx_tanh)
                else:
                    t, n = u[1], z_of.get(i)
                    if n is not None and n >= 2:
                        act.wait_ge(s["z_fin"], n - 1)
                    if u[0] == "K":
                        act.activation(V[:, t, :, 0:GD], src[:, 0:128].rearrange("p (h d) -> p h d", h=GKV), ACT.Copy)
                    if u[0] == "E":
                        last = act.activation(DVt[:, t, :, 0:DV], src[:, 0:256].rearrange("p (h d) -> p h d", h=DH), ACT.Copy)
                    lo = {"Q": 0, "K": 128, "E": 256}[u[0]]
                    if n is not None:
                        last = act.activation(zst[:, n % 2, lo:512], src[:, lo:512], ACT.Copy)
                last.then_inc(s["proj_out"], 1)
                if u[0] in "QK":
                    sqrt_rms(i)
                if i - 1 in gate_at and gate_at[i - 1][1] == 1:
                    lru_root(gate_at[i - 1][0])
                if i in gate_at:
                    lru_gate(*gate_at[i])

        @block.vector
        def _(dve):
            ch = Chain(dve, s["dve_c"])
            dve.wait_ge(s["ada_used"], KD)
            dve.wait_ge(s["mod_b"], 16)
            for j in range(2):
                ins = dve.tensor_tensor(modc[:, :, j], ps[:, 0, 0:32].rearrange("p (n j) -> p n j", j=2)[:, :, j],
                                        adab[:, :], ALU.add)
            ch.link(ins)
            ch.link(dve.tensor_scalar(modc[:, 8:16, :], modc[:, 8:16, :], 1.0, None, ALU.add))

            def modulate(k):
                dve.wait_ge(s[f"xraw{k % 2}"], 16 * (k // 2 + 1))
                x = xraw[:, k % 2, :]
                dve.tensor_scalar(x[:, 0:S], x[:, 0:S], modc[:, 8 + k, 0:1], modc[:, k, 0:1], ALU.mult, ALU.add)
                dve.tensor_scalar(x[:, S:T], x[:, S:T], modc[:, 8 + k, 1:2], modc[:, k, 1:2], ALU.mult, ALU.add)\
                    .then_inc(s["x_mod"], 1)

            modulate(0)
            for k in range(KD):
                if k + 1 < KD:
                    modulate(k + 1)
                dve.wait_ge(s["x_hi"], k + 1)
                dve.tensor_tensor(xlo[:, k, :], xraw[:, k % 2, :], xhi[:, k, :].bitcast(F32), ALU.subtract)\
                    .then_inc(s["x_lo"], 1)

            dve.wait_ge(s["consts"], CONSTS)
            for tab, j in ((rope_q, 0), (rope_k, 1)):
                for h in range(2):
                    dve.tensor_tensor(tab[:, :, h, :], tab[:, :, h, :],
                                      gvec[:, j, h, :].unsqueeze(1).broadcast_to([P, ST, GD]), ALU.mult)
            for j in range(2):
                ch.link(dve.tensor_tensor(lvec[:, 2 * j, :], lvec[:, 2 * j, :], lvec[:, 2 * j + 1, :], ALU.mult))
                ch.link(dve.tensor_reduce(lam[:, j:j + 1], lvec[:, 2 * j, :], AX.X, ALU.add))

            dve.wait_ge(s["proj_out"], 3 * LF)
            for f in range(LF):
                ch.link(dve.tensor_scalar(U[:, f, :], ax[:, f, 0:UL], lruc[:, f, 0:1], lruc[:, f, 4:5], ALU.mult, ALU.add))
                for k in range(1, CONV):
                    ins = dve.scalar_tensor_tensor(out=U[:, f, :], in0=ax[:, f, k:k + UL], scalar=lruc[:, f, k:k + 1],
                                                   in1=U[:, f, :], op0=ALU.mult, op1=ALU.add)
                    if f == LF - 1 and k == CONV - 1:
                        ins.then_inc(s["u_ready"], 1)
                    else:
                        ch.link(ins)
            dve.wait_ge(s["sp_rdy"], 1)
            dve.tensor_scalar(nsp[:, :, :, 0], nsp[:, :, :, 0], -RG_C, None, ALU.mult).then_inc(s["nsp_rdy"], 1)

            def rms(n, lo, nh, w):
                z = zst[:, n % 2, lo:lo + nh * w].rearrange("p (h d) -> p h d", h=nh)
                o = zo[:, n % 2, lo:lo + nh * w].rearrange("p (h d) -> p h d", h=nh)
                st = stat[:, n % 2]
                ch.link(dve.tensor_tensor(o, z, z, ALU.mult))
                ch.link(dve.tensor_reduce(st[:, 0, 0:nh], o, AX.X, ALU.add))
                dve.tensor_scalar(st[:, 0, 0:nh], st[:, 0, 0:nh], 1.0 / w, EPS, ALU.mult, ALU.add).then_inc(s["z_sq"], 1)
                dve.wait_ge(s["z_rt"], n + 1)
                ch.link(dve.reciprocal(st[:, 2, 0:nh], st[:, 1, 0:nh]))
                ch.link(dve.tensor_tensor(z, z, st[:, 2, 0:nh].unsqueeze(2).broadcast_to([P, nh, w]), ALU.mult))

            def rotate(n, lo, tab, t, nh, w):
                z, o = zst[:, n % 2, lo:lo + nh * w], zo[:, n % 2, lo:lo + nh * w]
                swapped = z.rearrange("p (h c two) -> p h c two", h=nh, two=2)[:, :, :, ::-1]
                sines = tab[:, t, 1, :].rearrange("p (c two) -> p c two", two=2).unsqueeze(1).broadcast_to([P, nh, w // 2, 2])
                zh = z.rearrange("p (h d) -> p h d", h=nh)
                ch.link(dve.tensor_tensor(o.rearrange("p (h c two) -> p h c two", h=nh, two=2), swapped, sines, ALU.mult))
                ch.link(dve.tensor_tensor(zh, zh, tab[:, t, 0, :].unsqueeze(1).broadcast_to([P, nh, w]), ALU.mult))
                return dve.tensor_tensor(o, o, z, ALU.add)

            def heads(i):
                (kind, t), n = units[i], z_of[i]
                dve.wait_ge(s["proj_out"], i + 1)
                if n >= 2:
                    dve.wait_ge(s[f"zo_out{n % 2}"], 16 * (n // 2))
                if kind == "Q":
                    rms(n, 0, GH, GD)
                    last = rotate(n, 0, rope_q, t, GH, GD)
                elif kind == "E":
                    last = rotate(n, 256, rope_d, t, 2 * DH, DQ)
                else:
                    rms(n, 128, GKV, GD)
                    if t < ST:
                        ch.mark(rotate(n, 128, rope_k, t, GKV, GD))
                        last = rotate(n, 256, rope_d, t, 2 * DH, DQ)
                    else:
                        dve.tensor_tensor(zo[:, n % 2, 128:256].rearrange("p (h d) -> p h d", h=GKV),
                                          zst[:, n % 2, 128:256].rearrange("p (h d) -> p h d", h=GKV),
                                          gvec[:, 1, 0, :].unsqueeze(1).broadcast_to([P, GKV, GD]), ALU.mult)
                        last = dve.tensor_copy(zo[:, n % 2, 256:512], zst[:, n % 2, 256:512])
                last.then_inc(s["z_fin"], 1)

            def lru_mult(c):
                f, d = combos[c]
                dve.wait_ge(s["gate_sig"], 2 * c + 2)
                dve.tensor_tensor(I, I, U[:, f, :], ALU.mult)
                dve.wait_ge(s["a_rdy"], c + 1)
                ch.link(dve.tensor_tensor(SQ[:, :], R, R, ALU.mult))
                dve.scalar_tensor_tensor(out=TH[:, :], in0=SQ[:, :], scalar=1.0, in1=TH[:, :], op0=ALU.add, op1=ALU.mult)\
                    .then_inc(s["m_neg"], 1)

            def lru_scan(c):
                f, d = combos[c]
                dve.wait_ge(s["m_rt"], c + 1)
                ch.link(dve.tensor_tensor(I, I, TH[:, :], ALU.mult))
                rv = slice(None, None, -1) if d else slice(None)
                cx, lx = slice(UC, UC + C), slice(0, S)
                ch.link(dve.tensor_tensor_scan(I[:, cx][:, rv], R[:, cx][:, rv], I[:, cx][:, rv], 0.0, ALU.mult, ALU.add))
                h0 = I[:, UC:UC + 1] if d else I[:, UC + C - 1:UC + C]
                dst = I[:, lx] if d else H[:, :]
                scan = dve.tensor_tensor_scan(dst[:, rv], R[:, lx][:, rv], I[:, lx][:, rv], h0, ALU.mult, ALU.add)
                if d == 0:
                    scan.then_inc(s["lru_done"], 1)
                else:
                    ch.link(scan)
                    ch.link(dve.tensor_tensor(H[:, :], H[:, :], I[:, lx], ALU.add))
                    dve.wait_ge(s["proj_out"], NL)
                    dve.tensor_tensor(ya[:, f, :], ya[:, f, :], H[:, :], ALU.mult).then_inc(s["lru_done"], 1)

            for i, u in enumerate(units):
                if i in z_of:
                    heads(i)
                if i - 1 in gate_at and gate_at[i - 1][1] == 1:
                    lru_scan(gate_at[i - 1][0])
                if i in gate_at and gate_at[i][1] == 1:
                    lru_mult(gate_at[i][0])

        @block.tensor
        def _(pe):
            pe.wait_ge(s["silu"], 1)
            for k in range(KD):
                pe.wait_ge(s[f"adar{k % NAR}"], 16 * (k // NAR + 1))
                for n in range(16):
                    mm = pe.matmul(ps[:, 0, 2 * n:2 * n + 2], adar[:, k % NAR, n * P:(n + 1) * P], silu_c[:, k, :],
                                   start=(k == 0 and n == 0), stop=(k == KD - 1), skip_group_check=True)
                mm.then_inc(s["ada_used"], 1)

            def product(dst, a, b, k, n_k):
                for j, (x, y) in enumerate(((a[0], b[0]), (a[1], b[0]), (a[0], b[1]))):
                    mm = pe.matmul(dst, x, y, start=(k == 0 and j == 0), stop=(k == n_k - 1 and j == 2))
                return mm

            def gates(c, g):
                f, d = combos[c]
                pe.wait_ge(s["u_ready"], 1)
                pe.wait_ge(s["wg_load"], 32)
                if 2 * c + g:
                    pe.wait_ge(s["gate_sig"], 2 * c + g)
                for o, n, b in ((0, 512, 0), (512, 512, 1), (1024, UL - 1024, 2)):
                    mm = pe.matmul(ps[:, b, 0:n], wg[:, (f * 2 + d) * 2 + g, :], U[:, f, o:o + n], start=True, stop=True)
                mm.then_inc(s["gate_mm"], 1)

            for i, u in enumerate(units):
                g = group[u[0]]
                if i >= RING:
                    pe.wait_ge(s["proj_out"], i - RING + 1)
                for k in range(KD):
                    pe.wait_ge(s["w_lo"], g * KD + k + 1)
                    if g == 0:
                        pe.wait_ge(s["x_lo"], k + 1)
                    if u[0] == "L":
                        _, f, o, n = u
                        cols = slice(f * P, (f + 1) * P)
                        a, b = (whi[:, k, cols], wlo[:, k, cols]), (xhi[:, k, o:o + n], xlo[:, k, o:o + n])
                    else:
                        n = 256 if u[0] == "E" and u[1] >= ST else 512
                        cols = slice(u[1] * P, (u[1] + 1) * P)
                        a, b = (xhi[:, k, cols], xlo[:, k, cols]), (whi[:, k, 0:n], wlo[:, k, 0:n])
                    mm = product(ps[:, 4 + i % RING, 0:n], a, b, k, KD)
                    if i in last_of and k < KD - 1:
                        mm.then_inc(s["w_used"], 1)
                mm.then_inc(s["proj_done"], 1)
                if i in gate_at:
                    gates(*gate_at[i])

        blk.close()

        mrow = sb("mrow", [P, 3, D], F32, attn)
        p2 = ExitStack()
        woh = sb("woh", [P, KD, D], F32R, attn)
        wol = sb("wol", [P, KD, D], F32R, attn)
        ysm = sb("ysm", [P, ST, GH * GD + DH * DV], F32, attn)
        pw = ExitStack()
        ring = sb("ring", [P, 2, 2048], F32, pw)
        pw.close()
        py = ExitStack()
        sub = sb("sub", [P, 2, ST * DH * DV], F32, py)
        subg = sb("subg", [P, DV], F32, py)
        rst = sb("rst", [P, 2, ST * DH], F32, py)
        py.close()
        pT = sb("pT", [P, 2, 512], F32, p2)
        pH = sb("pH", [P, 2, 512], F32R, p2)
        pL = sb("pL", [P, 2, 512], F32R, p2)
        OT = sb("OT", [P, S], F32, p2)
        pr = ExitStack()
        sbc = sb("sbc", [P, KD, P], F32, pr)
        pr.close()
        Q1 = sb("Q1", [P, 2, S], F32R, p2)
        Q2 = sb("Q2", [P, 2, S], F32R, p2)
        K1 = sb("K1", [P, 2, T], F32R, p2)
        K2 = sb("K2", [P, 2, T], F32R, p2)
        qr = sb("qr", [P, ST, GD], F32, p2)
        kr = sb("kr", [P, TT, GD], F32, p2)
        qs = sb("qs", [P, ST, P], F32, p2)
        ks = sb("ks", [P, TT, P], F32, p2)
        MX = sb("MX", [P, ST], F32, p2)
        MX3 = sb("MX3", [P, ST, 3], F32, p2)
        MM = sb("MM", [P, ST, 2], F32R, p2)
        rec = sb("rec", [P, ST], F32, p2)
        pz = ExitStack()
        g2t = sb("g2t", [P, D], F32, pz)
        pz.close()
        od = sb("od", [P, 2, ST, DV], F32, p2)
        Vh = sb("Vh", [P, 2, TT, GD + 1], F32R, p2)
        Vl = sb("Vl", [P, 2, TT, GD], F32R, p2)
        p2.close()

        a2 = {n: sem(n) for n in (
            "g2_out", "phi_d", "plo_d", "plo_p", "vh_d", "mrow_in", "ring0", "ring1", "row_mm", "row_out", "wo_hi", "wo_lo", "bc_rdy", "m_part", "head_d", "rec_d", "subg_in", "lam_e",
            "qr_in", "kr_in", "dup", "tr_mm", "hi_d", "lo_d", "k2_cp", "max_mm", "max_red", "m_rdy", "mt_mm", "mt_cp",
            "s_mm", "exp_d", "pv_mm", "o_out", "acc_free", "ot_mm", "ones_d", "vs_d", "dve2_c", "act2_c", "sub_sq", "sub_rt")}
        NROW = 8
        MAPS = GH + 2 * DH
        GROUP_HEADS = GH // GKV
        rounds = [(0, 0, 4), (0, 4, 4), (1, 0, 4), (1, 4, 4), (1, 8, 2)]
        NR = len(rounds)
        NS = 2 * TT
        chunks = [(0, 512), (512, 512), (1024, 256)]
        POOL_SOFT = (10, 12, 14, 16, 18)
        DVE_SOFT = tuple(u for u in range(NS) if u not in POOL_SOFT)

        class Kind:
            def __init__(self, w, rep, rows, scale):
                self.w, self.rep, self.rows, self.scale = w, rep, rows, scale

        gqa = Kind(GD, 2, 128, GD ** -0.5)
        dif = Kind(DQ, 3, 96, DQ ** -0.5)

        block = blk.enter_context(nc.Block())

        def soft_lo_ready(eng, G, u):
            name, mine = ("plo_p", POOL_SOFT) if u in POOL_SOFT else ("plo_d", DVE_SOFT)
            eng.wait_ge(a2[name], G * len(mine) + (mine.index(u) + 1))

        def soft_lo(eng, name, G, u):
            eng.wait_ge(a2["phi_d"], G * NS + (u + 1))
            eng.tensor_tensor(pL[:, u % 2, :], pT[:, u % 2, :], pH[:, u % 2, :].bitcast(F32), ALU.subtract).then_inc(a2[name], 1)

        @block.sync
        def _(sp):
            sp.dma_start(mrow[:, :, :], A["adab_rows"][:, 0:3, :]).then_inc(a2["mrow_in"], 16)
            sp.dma_start(g2t[:, :], A["adab_rows"][:, 3, :]).then_inc(a2["mrow_in"], 16)
            for i in range(2 * NROW + 4):
                if i >= 2:
                    if i - 2 < 2 * NROW:
                        sp.wait_ge(a2["row_mm"], i - 1)
                    else:
                        sp.wait_ge(a2["wo_lo"], 2 * (i - 2 - 2 * NROW) + 2)
                if i < 2 * NROW:
                    n, kh = divmod(i, 2)
                    src = A["ada_w"][kh * 512:(kh + 1) * 512, 2048 + n * 512:2048 + (n + 1) * 512]
                    dst = ring[:, i % 2, :].rearrange("p (k n) -> p k n", k=4)
                else:
                    j = i - 2 * NROW
                    src = A["w_out"][j * 256:(j + 1) * 256, :]
                    dst = ring[:, i % 2, :].rearrange("p (k n) -> p k n", k=2)
                sp.dma_start(dst, src.rearrange("(k p) n -> p k n", p=P)).then_inc(a2[f"ring{i % 2}"], 16)

            sp.wait_ge(a2["row_out"], NROW)
            sp.dma_start(g2_dram, g2t[:, :]).then_inc(a2["g2_out"], 16)

            def load(G, q_src, k_src):
                sp.wait_ge(a2["dup"], 2 * G + 1)
                sp.dma_start(qr[:, :, :], q_src).then_inc(a2["qr_in"], 16)
                sp.dma_start(kr[:, :, :], k_src).then_inc(a2["kr_in"], 16)

            q_v = q_dram.rearrange("(t p) (h d) -> h p t d", p=P, d=GD)
            k_v = k_dram.rearrange("(t p) (h d) -> h p t d", p=P, d=GD)
            dq_v = dq_dram.rearrange("(t p) (h d) -> h p t d", p=P, d=GD)
            one = lambda v, i: v[bass.ds(i, 1)].rearrange("o p t d -> (o p) t d")
            with sp.Fori(0, GKV) as kv:
                with sp.Fori(0, GROUP_HEADS) as j:
                    load(kv * GROUP_HEADS + j, one(q_v, kv * GROUP_HEADS + j), one(k_v, kv))
            with sp.Fori(0, DH) as h:
                for m in range(2):
                    load(GH + 2 * h + m, one(dq_v, h), one(k_v, GKV + h))
            sp.wait_ge(a2["head_d"], DH)
            sp.dma_start(subg[:, :], A["subg"]).then_inc(a2["subg_in"], 16)

        @block.gpsimd
        def _(pool):
            pool.memset(K2[64:66, :, :].bitcast(F32), 1.0).then_inc(a2["dup"], 1)
            pool.wait_ge(a2["dup"], 1)
            for k in range(KD):
                i = 2 * NROW + k // 2
                pool.wait_ge(a2["wo_hi"], k + 1)
                pool.tensor_tensor(wol[:, k, :], ring[:, i % 2, (k % 2) * D:(k % 2 + 1) * D], woh[:, k, :].bitcast(F32), ALU.subtract)\
                    .then_inc(a2["wo_lo"], 1)

            def repeat(kind, G, m, first=False):
                if not first:
                    if kind is gqa:
                        wait_apart(pool, a2["k2_cp"], G * 3, passed)
                    wait_apart(pool, a2["lo_d"], G * NR, passed)
                for raw, dst, n, got in ((qr, qs, ST, "qr_in"), (kr, ks, TT, "kr_in")):
                    wait_apart(pool, a2[got], G * 16 + 16, passed)
                    pool.tensor_copy(dst[:, :, 0:kind.rep * kind.w].rearrange("p t (r w) -> p t r w", w=kind.w),
                                     raw[:, :, m * kind.w:(m + 1) * kind.w].unsqueeze(2).broadcast_to([P, n, kind.rep, kind.w]))\
                        .then_inc(a2["dup"], 1)

            def split_values(kind, G, par, vh, ones=False):
                wait_apart(pool, a2["tr_mm"], G * NR + 1, passed)
                src = (V if kind is gqa else DVt)[:, :, bass.ds(vh, 1), :].rearrange("p t o d -> p (t o) d")
                pool.tensor_copy(Vh[:, par, :, :], src).then_inc(a2["vh_d"], 1)
                wait_apart(pool, a2["vh_d"], G + 1, passed)
                pool.tensor_tensor(Vl[:, par, :, :], src[:, :, 0:GD], Vh[:, par, :, 0:GD].bitcast(F32), ALU.subtract).then_inc(a2["vs_d"], 1)
                if kind is gqa:
                    for r, (is_k, t0, nt) in enumerate(rounds):
                        if is_k:
                            if r == 2:
                                wait_apart(pool, a2["vs_d"], G + 1, passed)
                            else:
                                wait_apart(pool, a2["k2_cp"], G * 3 + r - 2, passed)
                            wait_apart(pool, a2["hi_d"], G * NR + r + 1, passed)
                            cols = slice(t0 * P, (t0 + nt) * P)
                            pool.tensor_copy(K2[0:64, par, cols], K1[0:64, par, cols].bitcast(F32)).then_inc(a2["k2_cp"], 1)
                if ones:
                    wait_apart(pool, a2["vs_d"], G + 1, passed)
                    pool.memset(K1[96:98, par, :].bitcast(F32), 1.0).then_inc(a2["ones_d"], 1)
                    pool.wait_ge(a2["ones_d"], par + 1)

            def soft_parts(G):
                for u in POOL_SOFT:
                    soft_lo(pool, "plo_p", G, u)

            repeat(gqa, 0, 0, first=True)
            split_values(gqa, 0, 0, 0)
            repeat(gqa, 1, 0)
            with pool.Fori(0, 3) as it:
                for par in range(2):
                    G = it * 2 + par
                    split_values(gqa, G + 1, 1 - par, (it + par) // 2)
                    repeat(gqa, G + 2, 0)
                    soft_parts(G)
            split_values(gqa, 7, 1, 1)
            pool.wait_ge(a2["k2_cp"], GH * 3)
            repeat(dif, GH, 0)
            soft_parts(6)
            split_values(dif, GH, 0, 0, ones=True)
            repeat(dif, GH + 1, 1)
            soft_parts(7)
            split_values(dif, GH + 1, 1, 0, ones=True)
            repeat(dif, GH + 2, 0)
            soft_parts(GH)
            split_values(dif, GH + 2, 0, 1)
            repeat(dif, GH + 3, 1)
            soft_parts(GH + 1)
            with pool.Fori(1, 3) as it:
                for par in range(2):
                    G = it * 2 + (GH + par)
                    split_values(dif, G + 1, 1 - par, it + par)
                    repeat(dif, G + 2, par)
                    soft_parts(G)
            split_values(dif, MAPS - 1, 1, DH - 1)
            soft_parts(MAPS - 2)
            soft_parts(MAPS - 1)

        @block.scalar
        def _(act):
            ch = Chain(act, a2["act2_c"])
            act.activation(lam[:, 2:4], lam[:, 0:2], ACT.Exp).then_inc(a2["lam_e"], 1)
            for k in range(KD):
                i = 2 * NROW + k // 2
                act.wait_ge(a2[f"ring{i % 2}"], 16 * (i // 2 + 1))
                act.activation(woh[:, k, :], ring[:, i % 2, (k % 2) * D:(k % 2 + 1) * D], ACT.Copy).then_inc(a2["wo_hi"], 1)

            def hi(kind, G, par, r):
                is_k, t0, nt = rounds[r]
                dst = (K1 if is_k else Q1)[0:kind.rows, par, t0 * P:(t0 + nt) * P]
                act.wait_ge(a2["tr_mm"], G * NR + r + 1)
                act.activation(dst, ps[0:kind.rows, 4 + r % 3, 0:nt * P], ACT.Copy).then_inc(a2["hi_d"], 1)

            def soft(kind, G, nxt, Gn, par, first=False):
                for u in range(NS):
                    act.wait_ge(a2["s_mm"], G * NS + u + 1)
                    if u >= 2 or not first:
                        soft_lo_ready(act, G if u >= 2 else G - 1, (u - 2) % NS)
                    act.activation(pT[:, u % 2, :], ps[:, u % 2, :], ACT.Exp, scale=kind.scale).then_inc(a2["exp_d"], 1)
                    if nxt and 1 <= u <= NR:
                        hi(nxt, Gn, 1 - par, u - 1)
                    act.wait_ge(a2["exp_d"], G * NS + (u + 1))
                    if u >= 2 or not first:
                        act.wait_ge(a2["pv_mm"], G * NS + (u - 1))
                    act.activation(pH[:, u % 2, :], pT[:, u % 2, :], ACT.Copy).then_inc(a2["phi_d"], 1)

            for r in range(NR):
                hi(gqa, 0, 0, r)
            for kind, G0, after in ((gqa, 0, dif), (dif, GH, None)):
                for par in range(2):
                    soft(kind, G0 + par, kind, G0 + par + 1, par, first=(G0 + par == 0))
                with act.Fori(1, 3) as it:
                    for par in range(2):
                        soft(kind, it * 2 + (G0 + par), kind, it * 2 + (G0 + par + 1), par)
                soft(kind, G0 + 6, kind, G0 + 7, 0)
                soft(kind, G0 + 7, after, G0 + 8, 1)
            act.wait_ge(a2["sub_sq"], 1)
            act.activation(rst[:, 1, :], rst[:, 0, :], ACT.Sqrt).then_inc(a2["sub_rt"], 1)

        @block.vector
        def _(dve):
            ch = Chain(dve, a2["dve2_c"])
            for k in range(KD):
                ins = dve.tensor_copy(sbc[:, k, :], silu_c[:, k, 0:1].broadcast_to([P, P]))
            ins.then_inc(a2["bc_rdy"], 1)
            dve.wait_ge(a2["lam_e"], 1)
            ch.link(dve.tensor_tensor(lam[:, 4:5], lam[:, 3:4], lam[:, 2:3], ALU.subtract))
            dve.tensor_scalar(lam[:, 5:6], lam[:, 4:5], LAM_INIT, None, ALU.subtract).then_inc(a2["o_out"], 1)
            dve.wait_ge(a2["mrow_in"], 32)
            for n in range(NROW):
                dve.wait_ge(a2["row_mm"], 2 * n + 2)
                m = (mrow[:, n // 2, :] if n < 6 else g2t[:, :])[:, (n % 2) * 512:(n % 2 + 1) * 512]
                ins = dve.tensor_tensor(m, m, ps[:, n % 2, :], ALU.add)
                ins.then_inc(a2["row_out"], 1)
            dve.wait_ge(a2["row_out"], NROW)
            dve.tensor_scalar(mrow[:, 2, :], mrow[:, 2, :], 1.0, None, ALU.add).then_inc(a2["acc_free"], 2)

            def lo(kind, G, par, r):
                is_k, t0, nt = rounds[r]
                cols = slice(t0 * P, (t0 + nt) * P)
                dve.wait_ge(a2["hi_d"], G * NR + r + 1)
                if kind is gqa:
                    rows = slice(64, 128) if is_k else slice(0, 64)
                    hi_part = (K1 if is_k else Q1)[rows, par, cols]
                    dst = (K1 if is_k else Q2)[rows, par, cols]
                else:
                    rows = slice(32, 64) if is_k else slice(64, 96)
                    hi_part = dst = (K1 if is_k else Q1)[rows, par, cols]
                dve.tensor_tensor(dst, ps[rows, 4 + r % 3, 0:nt * P], hi_part.bitcast(F32), ALU.subtract).then_inc(a2["lo_d"], 1)

            def maxima(G, j):
                for b, (o, n) in enumerate(chunks):
                    dve.wait_ge(a2["max_mm"], G * (3 * ST) + (3 * j + b + 1))
                    dve.tensor_reduce(MX3[:, j, b:b + 1], ps[:, 4 + b, 0:n], AX.X, ALU.max, negate=True).then_inc(a2["max_red"], 1)

            def max_parts(G):
                dve.wait_ge(a2["max_red"], G * (3 * ST) + 3 * ST)
                dve.tensor_reduce(MX[:, :], MX3[:, :, :], AX.X, ALU.min).then_inc(a2["m_part"], 1)
                dve.wait_ge(a2["m_part"], 2 * G + 1)
                dve.tensor_copy(MM[:, :, 0], MX[:, :]).then_inc(a2["m_part"], 1)
                dve.wait_ge(a2["m_part"], 2 * G + 2)
                dve.tensor_tensor(MM[:, :, 1], MX[:, :], MM[:, :, 0].bitcast(F32), ALU.subtract).then_inc(a2["m_rdy"], 1)

            def max_rows(kind, G, par, b):
                dve.wait_ge(a2["mt_mm"], G * 2 + b + 1)
                dst = Q2[64:66, par, b * 512:(b + 1) * 512] if kind is gqa else Q1[96:98, par, b * 512:(b + 1) * 512]
                dve.tensor_copy(dst, ps[0:2, 7, :]).then_inc(a2["mt_cp"], 1)

            def take(G, b):
                dve.wait_ge(a2["pv_mm"], G * NS + (NS - 1 + b))
                dve.tensor_copy(OT[0:GD + 1, b * 512:(b + 1) * 512], ps[0:GD + 1, 2 + b, :]).then_inc(a2["acc_free"], 1)

            def output(kind, G, par, col, b):
                acc = ps[:, 7, 0:4 * (GD + 1)].rearrange("p (j d) -> p j d", j=4)
                js = slice(4 * b, 4 * b + 4)
                dve.wait_ge(a2["ot_mm"], 2 * G + b + 1)
                dve.reciprocal(rec[:, js], acc[:, :, GD]).then_inc(a2["rec_d"], 1)
                dve.wait_ge(a2["rec_d"], 2 * G + b + 1)
                dst = ysm[:, js, bass.ds(col, GD)] if kind is gqa else od[:, par, js, :]
                dve.tensor_tensor(dst, acc[:, :, 0:GD], rec[:, js].unsqueeze(2).broadcast_to([P, 4, GD]), ALU.mult)\
                    .then_inc(a2["o_out"], 1)
                if kind is dif and par and b:
                    dve.wait_ge(a2["o_out"], 2 * G + 3)
                    dve.scalar_tensor_tensor(out=ysm[:, :, bass.ds(col, DV)], in0=od[:, 1, :, :], scalar=lam[:, 5:6], in1=od[:, 0, :, :],
                                             op0=ALU.mult, op1=ALU.add).then_inc(a2["head_d"], 1)

            def ahead(kind, G, par, u):
                if 1 <= u <= NR:
                    lo(kind, G, par, u - 1)
                elif NR < u <= NR + ST:
                    maxima(G, u - NR - 1)
                    if u == NR + ST:
                        max_parts(G)
                elif NR + ST + 2 <= u < NR + ST + 4:
                    max_rows(kind, G, par, u - NR - ST - 2)

            def step(kind, G, par, nxt, Gn, prev, prev_col):
                for u in range(NS):
                    if u in DVE_SOFT:
                        soft_lo(dve, "plo_d", G, u)
                    if nxt:
                        ahead(nxt, Gn, 1 - par, u)
                    if prev and u in (1, 3):
                        output(prev, G - 1, 1 - par, prev_col, u // 2)
                for b in range(2):
                    take(G, b)

            for u in range(NS):
                ahead(gqa, 0, 0, u)
            dve.wait_ge(a2["g2_out"], 16)
            for kind, G0, before, after in ((gqa, 0, None, dif), (dif, GH, gqa, None)):
                wide = 2 * GD if kind is gqa else DV
                base = 0 if kind is gqa else GH * GD
                back = GD if kind is gqa else DV
                step(kind, G0, 0, kind, G0 + 1, before, (GH - 1) * GD)
                step(kind, G0 + 1, 1, kind, G0 + 2, kind, base)
                with dve.Fori(1, 3) as it:
                    for par in range(2):
                        step(kind, it * 2 + (G0 + par), par, kind, it * 2 + (G0 + par + 1), kind, it * wide + (base if par else base - back))
                step(kind, G0 + 6, 0, kind, G0 + 7, kind, 3 * wide + base - back)
                step(kind, G0 + 7, 1, after, G0 + 8, kind, 3 * wide + base)
            for b in range(2):
                output(dif, MAPS - 1, 1, GH * GD + (DH - 1) * DV, b)

            dve.wait_ge(a2["subg_in"], 16)
            dve.wait_ge(a2["head_d"], DH)
            sq = sub[:, 0, :].rearrange("p (t h d) -> p (t h) d", t=ST, h=DH)
            y3 = ysm[:, :, GH * GD:GH * GD + DH * DV]
            ch.link(dve.tensor_copy(sub[:, 0, :].rearrange("p (t c) -> p t c", t=ST), y3))
            ch.link(dve.tensor_tensor(sub[:, 1, :], sub[:, 0, :], sub[:, 0, :], ALU.mult))
            ch.link(dve.tensor_reduce(rst[:, 0, :], sub[:, 1, :].rearrange("p (g d) -> p g d", d=DV), AX.X, ALU.add))
            dve.tensor_scalar(rst[:, 0, :], rst[:, 0, :], 1.0 / DV, EPS, ALU.mult, ALU.add).then_inc(a2["sub_sq"], 1)
            dve.wait_ge(a2["sub_rt"], 1)
            ch.link(dve.reciprocal(rst[:, 0, :], rst[:, 1, :]))
            ch.link(dve.tensor_scalar(rst[:, 0, :], rst[:, 0, :], 1.0 - LAM_INIT, None, ALU.mult))
            ch.link(dve.tensor_tensor(sq, sq, rst[:, 0, :].unsqueeze(2).broadcast_to([P, ST * DH, DV]), ALU.mult))
            ch.link(dve.tensor_tensor(sq, sq, subg[:, :].unsqueeze(1).broadcast_to([P, ST * DH, DV]), ALU.mult))
            ch.link(dve.tensor_copy(y3, sub[:, 0, :].rearrange("p (t c) -> p t c", t=ST)))

        @block.tensor
        def _(pe):
            pe.wait_ge(a2["bc_rdy"], 1)
            for n in range(NROW):
                if n >= 2:
                    pe.wait_ge(a2["row_out"], n - 1)
                for k in range(KD):
                    i = 2 * n + k // 4
                    if k % 4 == 0:
                        pe.wait_ge(a2[f"ring{i % 2}"], 16 * (i // 2 + 1))
                    mm = pe.matmul(ps[:, n % 2, :], sbc[:, k, :], ring[:, i % 2, (k % 4) * 512:(k % 4 + 1) * 512],
                                   start=(k == 0), stop=(k == KD - 1))
                    if k % 4 == 3:
                        mm.then_inc(a2["row_mm"], 1)

            def transposes(kind, G, r):
                is_k, t0, nt = rounds[r]
                src = ks if is_k else qs
                if r == 0:
                    pe.wait_ge(a2["dup"], G * 2 + 2)
                if r == 2:
                    pe.wait_ge(a2["dup"], G * 2 + 3)
                if r >= 3:
                    pe.wait_ge(a2["lo_d"], G * NR + r - 2)
                for j in range(nt):
                    mm = pe.transpose(ps[0:kind.rows, 4 + r % 3, j * P:(j + 1) * P], src[:, t0 + j, 0:kind.rows], ident[:, :])
                mm.then_inc(a2["tr_mm"], 1)

            def max_tile(kind, G, par, j):
                if j == 0:
                    pe.wait_ge(a2["lo_d"], G * NR + NR)
                    if kind is gqa:
                        pe.wait_ge(a2["k2_cp"], G * 3 + 3)
                cols = slice(j * P, (j + 1) * P)
                for b, (o, n) in enumerate(chunks):
                    if j:
                        pe.wait_ge(a2["max_red"], G * (3 * ST) + (3 * j - 2 + b))
                    mm = pe.matmul(ps[:, 4 + b, 0:n], Q1[0:kind.rows, par, cols], K1[0:kind.rows, par, o:o + n],
                                   start=True, stop=kind is dif)
                    if kind is gqa:
                        mm = pe.matmul(ps[:, 4 + b, 0:n], Q2[0:64, par, cols], K2[0:64, par, o:o + n], start=False, stop=True)
                    mm.then_inc(a2["max_mm"], 1)

            def max_turn(G, b, first):
                if b == 0:
                    pe.wait_ge(a2["m_rdy"], G + 1)
                    if not first:
                        pe.wait_ge(a2["o_out"], G * 2 - 1)
                else:
                    pe.wait_ge(a2["mt_cp"], G * 2 + 1)
                for j in range(4):
                    mm = pe.transpose(ps[0:2, 7, j * P:(j + 1) * P], MM[:, b * 4 + j, :].bitcast(F32), ident[:, :])
                mm.then_inc(a2["mt_mm"], 1)

            def scores(kind, G, par, u, first=False):
                kt, qh = divmod(u, 2)
                if u == 0:
                    pe.wait_ge(a2["mt_cp"], G * 2 + 2)
                    if kind is dif:
                        pe.wait_ge(a2["ones_d"], par + 1)
                if u >= 2 or not first:
                    pe.wait_ge(a2["exp_d"], G * NS + (u - 1))
                keys, qrs = slice(kt * P, (kt + 1) * P), slice(qh * 512, (qh + 1) * 512)
                rows = 128 if kind is gqa else 98
                mm = pe.matmul(ps[:, u % 2, :], K1[0:rows, par, keys], Q1[0:rows, par, qrs], start=True, stop=kind is dif)
                if kind is gqa:
                    mm = pe.matmul(ps[:, u % 2, :], K2[0:66, par, keys], Q2[0:66, par, qrs], start=False, stop=True)
                mm.then_inc(a2["s_mm"], 1)

            def values(G, par, u, part):
                kt, qh = divmod(u, 2)
                if part == 0:
                    if u == 0:
                        pe.wait_ge(a2["vs_d"], G + 1)
                    if u < 2:
                        pe.wait_ge(a2["acc_free"], 2 * G + (1 + u))
                    pe.wait_ge(a2["phi_d"], G * NS + (u + 1))
                    pe.matmul(ps[0:GD + 1, 2 + qh, :], Vh[:, par, kt, :], pH[:, u % 2, :], start=kt == 0, stop=False)
                    pe.matmul(ps[0:GD, 2 + qh, :], Vl[:, par, kt, :], pH[:, u % 2, :], start=False, stop=False)
                else:
                    soft_lo_ready(pe, G, u)
                    pe.matmul(ps[0:GD + 1, 2 + qh, :], Vh[:, par, kt, :], pL[:, u % 2, :], start=False, stop=kt == TT - 1).then_inc(a2["pv_mm"], 1)

            def turn_back(G, b):
                pe.wait_ge(a2["acc_free"], 2 * G + (3 + b))
                if b == 1:
                    pe.wait_ge(a2["o_out"], 2 * G + 2)
                for j in range(4):
                    mm = pe.transpose(ps[:, 7, j * (GD + 1):(j + 1) * (GD + 1)], OT[0:GD + 1, (4 * b + j) * P:(4 * b + j + 1) * P],
                                      ident[0:GD + 1, 0:GD + 1])
                mm.then_inc(a2["ot_mm"], 1)

            def ahead(kind, G, par, u, first=False):
                if u < NR:
                    transposes(kind, G, u)
                elif NR < u <= NR + ST:
                    max_tile(kind, G, par, u - NR - 1)
                elif NR + ST + 2 <= u < NR + ST + 4:
                    max_turn(G, u - NR - ST - 2, first)

            def step(kind, G, par, nxt, Gn, prev):
                for u in range(NS):
                    if u:
                        values(G, par, u - 1, 1)
                    elif prev:
                        values(G - 1, 1 - par, NS - 1, 1)
                    if u + 2 < NS:
                        scores(kind, G, par, u + 2)
                    elif nxt:
                        scores(nxt, Gn, 1 - par, u + 2 - NS)
                    if nxt:
                        ahead(nxt, Gn, 1 - par, u)
                    values(G, par, u, 0)
                    if prev and u in (1, 3):
                        turn_back(G - 1, u // 2)

            pe.wait_ge(a2["acc_free"], 2)
            for u in range(NS):
                ahead(gqa, 0, 0, u, first=True)
            for u in range(2):
                scores(gqa, 0, 0, u, first=True)
            for kind, G0, after in ((gqa, 0, dif), (dif, GH, None)):
                for par in range(2):
                    step(kind, G0 + par, par, kind, G0 + par + 1, G0 + par > 0)
                with pe.Fori(1, 3) as it:
                    for par in range(2):
                        step(kind, it * 2 + (G0 + par), par, kind, it * 2 + (G0 + par + 1), True)
                step(kind, G0 + 6, 0, kind, G0 + 7, True)
                step(kind, G0 + 7, 1, after, G0 + 8, True)
            values(MAPS - 1, 1, NS - 1, 1)
            for b in range(2):
                turn_back(MAPS - 1, b)
        blk.close()

        p3 = ExitStack()
        yTh = sb("yTh", [P, 2, KD, P], F32R, p3)
        yTl = sb("yTl", [P, 2, KD, P], F32R, p3)
        xt = sb("xt", [P, 2, D], F32, p3)
        ln1 = sb("ln1", [P, 2, D], F32, p3)
        res = sb("res", [P, D], F32, p3)
        x1 = sb("x1", [P, 2, D], F32, p3)
        hh = sb("hh", [P, 2, D], F32, p3)
        hT = sb("hT", [P, KD, P], F32, p3)
        rw = sb("rw", [P, KD, E], F32, p3)
        rb = sb("rb", [P, E], F32, p3)
        st3 = sb("st3", [P, 2, 16], F32, p3)
        tri = sb("tri", [P, 2, P], F32, p3)
        kc = sb("kc", [P, 8 + NBLK + 2], F32, p3)
        rt = sb("rt", [P, 12, ST * E], F32, p3)
        rsm = sb("rsm", [P, 16, ST], F32, p3)
        ecmp = sb("ecmp", [P, E * (NBLK + 2)], F32, p3)
        zrow = sb("zrow", [P, (NBLK + 1)], I32, p3)
        zeros = sb("zeros", [P, D], F32, p3)
        tokid = sb("tokid", [P, ST], I32, p3)
        p3.close()

        a3 = {n: sem(n) for n in (
            "c3_in", "y_zero", "xt0", "xt1", "yt_mm", "yt_hi", "yt_lo", "ya_lo", "y_mm", "y_ev", "ln_sq", "ln_rt", "x1g", "x1_done",
            "h_mul", "h_done", "x1_out0", "x1_out1", "h_out0", "h_out1", "ht_mm", "ht_cp", "lg_mm", "dve3_c", "sm_in",
            "sm_ex", "mask_d", "cnt_mm", "z_in", "z_out", "dest_d", "tok_d", "scat")}
        block = blk.enter_context(nc.Block())

        @block.sync
        def _(sp):
            for dst, name in ((ln1[:, :, :], "ln1"), (rw[:, :, :], "rw"), (rb[:, :], "rb"), (tri[:, :, :], "tri"), (kc[:, :], "kc")):
                sp.dma_start(dst, A[name]).then_inc(a3["c3_in"], 16)
            def load_x(t):
                sp.dma_start(xt[:, t % 2, :], A["x"][t * P:(t + 1) * P, :]).then_inc(a3[f"xt{t % 2}"], 16)

            load_x(0)
            load_x(1)
            sp.wait_ge(a3["z_in"], 1)
            sp.dma_start(rows_dram.rearrange("(p n) o -> p (n o)", p=P), zrow[:, :]).then_inc(a3["z_out"], 16)
            for t in range(ST):
                if t + 2 < ST:
                    sp.wait_ge(a3["y_ev"], t + 1)
                    load_x(t + 2)
                for b in range(MINBLK + 2 * t, min(MINBLK + 2 * t + 2, NBLK + 1)):
                    sp.dma_start(y_dram[b * BLK:(b + 1) * BLK, :], zeros[:, :]).then_inc(a3["y_zero"], 16)
                sp.wait_ge(a3["x1_done"], t + 1)
                sp.dma_start(x1_dram[t * P:(t + 1) * P, :], x1[:, t % 2, :]).then_inc(a3[f"x1_out{t % 2}"], 16)
                sp.wait_ge(a3["h_done"], t + 1)
                sp.dma_start(h_dram[t * P:(t + 1) * P, :], hh[:, t % 2, :]).then_inc(a3[f"h_out{t % 2}"], 16)
            sp.wait_ge(a3["y_zero"], 16 * (NBLK + 1 - MINBLK))
            for b in range(2):
                sp.wait_ge(a3[f"x1_out{b}"], 16 * ST // 2)
                sp.wait_ge(a3[f"h_out{b}"], 16 * ST // 2)

        @block.gpsimd
        def _(pool):
            pool.memset(zrow[:, :], 0)
            pool.memset(zeros[:, :], 0.0).then_inc(a3["z_in"], 1)
            pool.iota(tokid[:, :], [[P, ST]], base=0, channel_multiplier=1).then_inc(a3["tok_d"], 1)
            pool.wait_ge(a3["c3_in"], 16 * 5)

            def ya_part(t):
                pool.wait_ge(a3["yt_hi"], t + 1)
                if t >= 2:
                    pool.wait_ge(a3["y_mm"], t - 1)
                pool.tensor_tensor(yTl[:, t % 2, 0:LF, :], ya[:, :, t * P:(t + 1) * P], yTh[:, t % 2, 0:LF, :].bitcast(F32), ALU.subtract)\
                    .then_inc(a3["ya_lo"], 1)

            ya_part(0)
            for t in range(ST):
                if t + 1 < ST:
                    ya_part(t + 1)
                pool.wait_ge(a3["x1g"], t + 1)
                pool.tensor_tensor(x1[:, t % 2, :], x1[:, t % 2, :], ln1[:, 1, :], ALU.add).then_inc(a3["x1_done"], 1)
                pool.wait_ge(a3["x1_done"], t + 1)
                if t >= 2:
                    pool.wait_ge(a3[f"h_out{t % 2}"], 16 * (t // 2))
                    pool.wait_ge(a3["ht_mm"], t - 1)
                pool.tensor_tensor(hh[:, t % 2, :], x1[:, t % 2, :], mrow[:, 2, :], ALU.mult).then_inc(a3["h_mul"], 1)
            pool.wait_ge(a3["z_out"], 16)
            pool.wait_ge(a3["dest_d"], 1)
            pool.wait_ge(a3["tok_d"], 1)
            for t in range(ST):
                for c in range(2):
                    pool.indirect_dma_start(rows_dram, bass.IndirectOffsetOnAxis(ap=dest[:, c, t:t + 1], axis=0), tokid[:, t:t + 1], None)\
                        .then_inc(a3["scat"], 16)
            pool.wait_ge(a3["scat"], 16 * 2 * ST)

        @block.scalar
        def _(act):
            def hi_parts(t):
                act.wait_ge(a3["yt_mm"], t + 1)
                if t >= 2:
                    act.wait_ge(a3["y_mm"], t - 1)
                act.activation(yTh[:, t % 2, LF:KD, :].rearrange("p k m -> p (k m)"), ps[:, 0:2, :].rearrange("p a b -> p (a b)")[:, 0:(KD - LF) * P], ACT.Copy)
                act.activation(yTh[:, t % 2, 0:LF, :], ya[:, :, t * P:(t + 1) * P], ACT.Copy).then_inc(a3["yt_hi"], 1)

            def h_copy(t):
                act.wait_ge(a3["ht_mm"], t + 1)
                if t >= 1:
                    act.wait_ge(a3["lg_mm"], t)
                act.activation(hT[:, :, :].rearrange("p k m -> p (k m)"), ps[:, 6:8, :].rearrange("p a b -> p (a b)"), ACT.Copy).then_inc(a3["ht_cp"], 1)

            hi_parts(0)
            for t in range(ST):
                if t + 1 < ST:
                    hi_parts(t + 1)
                act.wait_ge(a3["ln_sq"], t + 1)
                act.activation(st3[:, t % 2, 14:15], st3[:, t % 2, 13:14], ACT.Sqrt).then_inc(a3["ln_rt"], 1)
                if t:
                    h_copy(t - 1)
            h_copy(ST - 1)
            act.wait_ge(a3["sm_in"], 1)
            act.activation(rt[:, 1, :], rt[:, 0, :], ACT.Exp).then_inc(a3["sm_ex"], 1)

        @block.vector
        def _(dve):
            ch = Chain(dve, a3["dve3_c"])
            dve.wait_ge(a3["c3_in"], 16 * 5)

            def lo_part(t):
                dve.wait_ge(a3["yt_hi"], t + 1)
                dve.tensor_tensor(yTl[:, t % 2, LF:KD, :].rearrange("p k m -> p (k m)"), ps[:, 0:2, :].rearrange("p a b -> p (a b)")[:, 0:(KD - LF) * P],
                                  yTh[:, t % 2, LF:KD, :].rearrange("p k m -> p (k m)").bitcast(F32), ALU.subtract).then_inc(a3["yt_lo"], 1)

            def shift_h(t):
                dve.wait_ge(a3["h_mul"], t + 1)
                dve.tensor_tensor(hh[:, t % 2, :], hh[:, t % 2, :], mrow[:, 1, :], ALU.add).then_inc(a3["h_done"], 1)

            lo_part(0)
            for t in range(ST):
                if t + 1 < ST:
                    lo_part(t + 1)
                s_ = st3[:, t % 2, :]
                dve.wait_ge(a3["y_mm"], t + 1)
                ch.link(dve.tensor_tensor(res[:, :].rearrange("p (a b) -> p a b", a=2), ps[:, 2:4, :],
                                          mrow[:, 0, :].rearrange("p (a b) -> p a b", a=2), ALU.mult))
                dve.wait_ge(a3[f"xt{t % 2}"], 16 * (t // 2 + 1))
                dve.scalar_tensor_tensor(out=res[:, :], in0=xt[:, t % 2, :], scalar=ALPHA, in1=res[:, :], op0=ALU.mult, op1=ALU.add)\
                    .then_inc(a3["y_ev"], 1)
                dve.wait_ge(a3["y_ev"], t + 1)
                for b in range(2):
                    ins = dve.bn_stats(s_[:, 6 * b:6 * b + 6], res[:, b * 512:(b + 1) * 512])
                ch.link(ins)
                ch.link(dve.bn_aggr(s_[:, 12:14], s_[:, 0:12]))
                dve.tensor_scalar(s_[:, 13:14], s_[:, 13:14], EPS, None, ALU.add).then_inc(a3["ln_sq"], 1)
                if t:
                    shift_h(t - 1)
                dve.wait_ge(a3["ln_rt"], t + 1)
                ch.link(dve.reciprocal(s_[:, 15:16], s_[:, 14:15]))
                ch.link(dve.tensor_scalar(res[:, :], res[:, :], s_[:, 12:13], s_[:, 15:16], ALU.subtract, ALU.mult))
                if t >= 2:
                    dve.wait_ge(a3[f"x1_out{t % 2}"], 16 * (t // 2))
                    dve.wait_ge(a3["h_mul"], t - 1)
                dve.tensor_tensor(x1[:, t % 2, :], res[:, :], ln1[:, 0, :], ALU.mult).then_inc(a3["x1g"], 1)
                dve.wait_ge(a3["x1g"], t + 1)
            shift_h(ST - 1)

            def v(i, pat="p (t e) -> p t e", **k):
                return rt[:, i, :].rearrange(pat, **(k or dict(t=ST)))

            TG = ST * G
            dve.wait_ge(a3["lg_mm"], ST)
            lg = ps[:, 4, 0:ST * E].rearrange("p (t e) -> p t e", t=ST)
            ch.link(dve.tensor_reduce(rsm[:, 0, :], lg, AX.X, ALU.max))
            dve.tensor_tensor(v(0), lg, rsm[:, 0, :].unsqueeze(2).broadcast_to([P, ST, E]), ALU.subtract).then_inc(a3["sm_in"], 1)
            dve.wait_ge(a3["sm_ex"], 1)
            ch.link(dve.tensor_reduce(rsm[:, 1, :], v(1), AX.X, ALU.add))
            ch.link(dve.reciprocal(rsm[:, 2, :], rsm[:, 1, :]))
            ch.link(dve.tensor_tensor(v(1), v(1), rsm[:, 2, :].unsqueeze(2).broadcast_to([P, ST, E]), ALU.mult))
            ch.link(dve.tensor_tensor(v(2), v(1), rb[:, :].unsqueeze(1).broadcast_to([P, ST, E]), ALU.add))

            def ranks(score, rank, tmp, n, w):
                for i in range(w):
                    ins = dve.memset(rank[:, :, i:i + 1], float(w - 1 - i))
                ch.link(ins)
                for d in range(1, w):
                    t_ = tmp[:, :, 0:w - d]
                    ch.link(dve.tensor_tensor(t_, score[:, :, 0:w - d], score[:, :, d:w], ALU.is_ge))
                    ch.link(dve.tensor_tensor(rank[:, :, d:w], rank[:, :, d:w], t_, ALU.add))
                    ch.link(dve.tensor_tensor(rank[:, :, 0:w - d], rank[:, :, 0:w - d], t_, ALU.subtract))

            g4 = lambda i: rt[:, i, :].rearrange("p (g c) -> p g c", c=EG)
            ranks(g4(2), g4(3), g4(4), TG, EG)
            ch.link(dve.tensor_scalar(rt[:, 3, :], rt[:, 3, :], 1.5, None, ALU.is_lt))
            ch.link(dve.tensor_tensor(rt[:, 4, :], rt[:, 2, :], rt[:, 3, :], ALU.mult))
            ch.link(dve.tensor_reduce(rt[:, 5, 0:TG], g4(4), AX.X, ALU.add))
            gg = lambda i: rt[:, i, 0:TG].rearrange("p (t g) -> p t g", g=G)
            ranks(gg(5), gg(6), gg(7), ST, G)
            ch.link(dve.tensor_scalar(rt[:, 6, 0:TG], rt[:, 6, 0:TG], 0.5, None, ALU.is_lt))
            dve.tensor_tensor(g4(3), g4(3), rt[:, 6, 0:TG].unsqueeze(2).broadcast_to([P, TG, EG]), ALU.mult).then_inc(a3["mask_d"], 1)
            dve.wait_ge(a3["mask_d"], 1)
            ch.link(dve.tensor_tensor(rt[:, 1, :], rt[:, 1, :], rt[:, 3, :], ALU.mult))
            ch.link(dve.tensor_reduce(rsm[:, 3, :], v(1), AX.X, ALU.add))
            ch.link(dve.reciprocal(rsm[:, 4, :], rsm[:, 3, :]))
            ch.link(dve.tensor_tensor(v(1), v(1), rsm[:, 4, :].unsqueeze(2).broadcast_to([P, ST, E]), ALU.mult))
            dve.wait_ge(a3["cnt_mm"], 1)
            ch.link(dve.tensor_copy(rt[:, 8, :], ps[:, 6, 0:ST * E]))
            ch.link(dve.memset(rt[:, 9, 0:E], 0.0))
            for t in range(ST):
                dst = rt[:, 9, (t + 1) * E:(t + 2) * E] if t + 1 < ST else rt[:, 10, 0:E]
                ch.link(dve.tensor_tensor(dst, rt[:, 9, t * E:(t + 1) * E], rt[:, 8, t * E:(t + 1) * E], ALU.add))
            ch.link(dve.tensor_tensor(ecmp[:, 0:E * 8].rearrange("p (e j) -> p e j", j=8), rt[:, 10, 0:E].unsqueeze(2).broadcast_to([P, E, 8]),
                                      kc[:, 0:8].unsqueeze(1).broadcast_to([P, E, 8]), ALU.is_gt))
            ch.link(dve.tensor_reduce(rt[:, 10, 16:32], ecmp[:, 0:E * 8].rearrange("p (e j) -> p e j", j=8), AX.X, ALU.add))
            ch.link(dve.memset(rt[:, 10, 32:48], 1.0))
            ch.link(dve.tensor_tensor_scan(rt[:, 10, 48:64], rt[:, 10, 32:48], rt[:, 10, 16:32], 0.0, ALU.mult, ALU.add))
            ch.link(dve.tensor_tensor(rt[:, 10, 64:80], rt[:, 10, 48:64], rt[:, 10, 16:32], ALU.subtract))
            ch.link(dve.tensor_scalar(rt[:, 10, 64:80], rt[:, 10, 64:80], float(BLK), None, ALU.mult))
            nb = NBLK + 2
            ch.link(dve.tensor_tensor(ecmp[:, 0:nb * E].rearrange("p (b e) -> p b e", e=E), rt[:, 10, 48:64].unsqueeze(1).broadcast_to([P, nb, E]),
                                      kc[:, 8:8 + nb].unsqueeze(2).broadcast_to([P, nb, E]), ALU.is_le))
            ch.link(dve.tensor_reduce(rt[:, 11, 0:nb], ecmp[:, 0:nb * E].rearrange("p (b e) -> p b e", e=E), AX.X, ALU.add))
            ch.link(dve.tensor_scalar(rt[:, 11, 0:nb], rt[:, 11, 0:nb], float(E - 1), None, ALU.min))
            ch.link(dve.tensor_copy(blk_tab[:, 0:nb], rt[:, 11, 0:nb]))
            ch.link(dve.tensor_copy(blk_tab[:, nb:nb + 1], rt[:, 10, 63:64]))
            ch.link(dve.tensor_tensor(v(9), v(9), rt[:, 10, 64:80].unsqueeze(1).broadcast_to([P, ST, E]), ALU.add))
            dve.wait_ge(a3["cnt_mm"], 2)
            ch.link(dve.tensor_tensor(rt[:, 9, :], rt[:, 9, :], ps[:, 7, 0:ST * E], ALU.add))
            ch.link(dve.tensor_tensor(rt[:, 9, :], rt[:, 9, :], rt[:, 3, :], ALU.mult))
            ch.link(dve.tensor_reduce(rsm[:, 5, :], v(9), AX.X, ALU.max))
            ch.link(dve.tensor_reduce(rsm[:, 6, :], v(9), AX.X, ALU.add))
            ch.link(dve.tensor_tensor(rsm[:, 6, :], rsm[:, 6, :], rsm[:, 5, :], ALU.subtract))
            ch.link(dve.tensor_tensor(v(8), v(9), rsm[:, 5, :].unsqueeze(2).broadcast_to([P, ST, E]), ALU.is_equal))
            ch.link(dve.tensor_tensor(rt[:, 8, :], rt[:, 8, :], rt[:, 1, :], ALU.mult))
            ch.link(dve.tensor_reduce(gates[:, 0, :], v(8), AX.X, ALU.add))
            ch.link(dve.tensor_tensor(rt[:, 1, :], rt[:, 1, :], rt[:, 8, :], ALU.subtract))
            ch.link(dve.tensor_reduce(gates[:, 1, :], v(1), AX.X, ALU.add))
            ch.link(dve.tensor_copy(dest[:, 0, :], rsm[:, 5, :]))
            dve.tensor_copy(dest[:, 1, :], rsm[:, 6, :]).then_inc(a3["dest_d"], 1)

        @block.tensor
        def _(pe):
            def turn_y(t):
                if t:
                    pe.wait_ge(a3["yt_lo"], t)
                for j in range(KD - LF):
                    mm = pe.transpose(ps[:, j // 4, (j % 4) * P:(j % 4 + 1) * P], ysm[:, t, j * P:(j + 1) * P], ident[:, :])
                mm.then_inc(a3["yt_mm"], 1)

            def project(t):
                pe.wait_ge(a3["yt_lo"], t + 1)
                pe.wait_ge(a3["ya_lo"], t + 1)
                if t:
                    pe.wait_ge(a3["y_ev"], t)
                for b in range(2):
                    cols = slice(b * 512, (b + 1) * 512)
                    for k in range(KD):
                        for j, (x, y) in enumerate(((yTh, woh), (yTl, woh), (yTh, wol))):
                            mm = pe.matmul(ps[:, 2 + b, :], x[:, t % 2, k, :], y[:, k, cols], start=(k == 0 and j == 0), stop=(k == KD - 1 and j == 2))
                mm.then_inc(a3["y_mm"], 1)

            def turn_h(t):
                pe.wait_ge(a3["h_done"], t + 1)
                if t:
                    pe.wait_ge(a3["ht_cp"], t)
                for k in range(KD):
                    mm = pe.transpose(ps[:, 6 + k // 4, (k % 4) * P:(k % 4 + 1) * P], hh[:, t % 2, k * P:(k + 1) * P], ident[:, :])
                mm.then_inc(a3["ht_mm"], 1)

            def route(t):
                pe.wait_ge(a3["ht_cp"], t + 1)
                pe.wait_ge(a3["c3_in"], 16 * 5)
                for k in range(KD):
                    mm = pe.matmul(ps[:, 4, t * E:(t + 1) * E], hT[:, k, :], rw[:, k, :], start=(k == 0), stop=(k == KD - 1))
                mm.then_inc(a3["lg_mm"], 1)

            turn_y(0)
            for t in range(ST):
                if t + 1 < ST:
                    turn_y(t + 1)
                project(t)
                if t:
                    turn_h(t - 1)
                    route(t - 1)
            turn_h(ST - 1)
            route(ST - 1)
            pe.wait_ge(a3["mask_d"], 1)
            for j, b in ((1, 6), (0, 7)):
                pe.matmul(ps[:, b, 0:ST * E], tri[:, j, :], rt[:, 3, :], start=True, stop=True).then_inc(a3["cnt_mm"], 1)
        blk.close()
        attn.close()

        p4 = ExitStack()
        wraw4 = sb("wraw4", [P, NUNIT, D], F32, p4)
        whi4 = sb("whi4", [P, NUNIT, D], F32R, p4)
        wlo4 = sb("wlo4", [P, NUNIT, D], F32R, p4)
        xg = sb("xg", [P, D], F32, p4)
        xTh = sb("xTh", [P, KD, P], F32R, p4)
        xTl = sb("xTl", [P, KD, P], F32R, p4)
        hs = sb("hs", [P, FF], F32, p4)
        hTh = sb("hTh", [P, FK, P], F32R, p4)
        hTl = sb("hTl", [P, FK, P], F32R, p4)
        ys = sb("ys", [P, D], F32, p4)
        row_all = sb("row_all", [P, NBLK + 1], I32, p4)
        row_ix = sb("row_ix", [P, 2], I32, p4)
        tok4 = sb("tok4", [P, 2], F32, p4)
        p4.close()
        a4 = {n: sem(n) for n in (
            *(f"raw{p}" for p in range(NUNIT // 2)), "rows_in", "whi_d", "wlo_d", "wlo_p", "used", "xg_in", "ix_d", "xt_mm", "xt_hi", "xt_lo",
            "silu_d", "mul_d", "ht_mm4", "ht_hi4", "ht_lo4", "y_ev4", "y_free")}
        block = blk.enter_context(nc.Block())
        POOL_UNITS = (1, 4, 7, 10)
        DVE_UNITS = tuple(u for u in range(NUNIT) if u not in POOL_UNITS)

        def lo_ready(eng, b, u, apart=False):
            name, mine = ("wlo_p", POOL_UNITS) if u in POOL_UNITS else ("wlo_d", DVE_UNITS)
            count = b * len(mine) + (mine.index(u) + 1)
            if apart:
                wait_apart(eng, a4[name], count, passed)
            else:
                eng.wait_ge(a4[name], count)

        def block_count(eng):
            return eng.value_load(blk_tab[0:1, NBLK + 2:NBLK + 3], min_val=1, max_val=NBLK)

        def lo_unit(eng, name, b, u):
            eng.wait_ge(a4["whi_d"], b * NUNIT + (u + 1))
            eng.tensor_tensor(wlo4[:, u, :], wraw4[:, u, :], whi4[:, u, :].bitcast(F32), ALU.subtract).then_inc(a4[name], 1)

        @block.sync
        def _(sp):
            def load(b, p):
                e = sp.value_load(blk_tab[0:1, bass.ds(b, 1)], min_val=0, max_val=E - 1)
                sp.dma_start(wraw4[:, 2 * p:2 * p + 2, :], A["wexp"][bass.ds(e, 1), :, 2 * p:2 * p + 2, :].rearrange("o p u n -> p (o u) n"))\
                    .then_inc(a4[f"raw{p}"], 16)

            sp.dma_start(row_all[:, :], rows_dram.rearrange("(b p) o -> p (b o)", p=P), allow_slow_non_contiguous=True).then_inc(a4["rows_in"], 16)
            for p in range(NUNIT // 2):
                load(0, p)
            for p in range(NUNIT // 2):
                lo_ready(sp, 0, 2 * p)
                lo_ready(sp, 0, 2 * p + 1)
                load(1, p)
            nb = block_count(sp)
            with sp.Fori(0, NBLK) as b:
                with sp.If(b < nb):
                    for p in range(NUNIT // 2):
                        lo_ready(sp, b + 1, 2 * p, apart=True)
                        lo_ready(sp, b + 1, 2 * p + 1, apart=True)
                        load(b + 2, p)
                    sp.wait_ge(a4["y_ev4"], b + 2)
                    sp.dma_start(y_dram[bass.ds(b * BLK, BLK), :], ys[:, :]).then_inc(a4["y_free"], 16)
            wait_apart(sp, a4["y_free"], nb * 16 + 16, passed)
            for p in range(NUNIT // 2):
                wait_apart(sp, a4[f"raw{p}"], nb * 16 + 32, passed)

        @block.gpsimd
        def _(pool):
            def gather(b, col):
                pool.tensor_copy(row_ix[:, 0:1], col).then_inc(a4["ix_d"], 1)
                wait_apart(pool, a4["ix_d"], b + 1, passed)
                pool.indirect_dma_start(xg[:, :], None, h_dram, bass.IndirectOffsetOnAxis(ap=row_ix[:, 0:1], axis=0)).then_inc(a4["xg_in"], 16)

            pool.wait_ge(a4["rows_in"], 16)
            gather(0, row_all[:, 0:1])
            for u in POOL_UNITS:
                lo_unit(pool, "wlo_p", 0, u)
            nb = block_count(pool)
            with pool.Fori(0, NBLK) as b:
                with pool.If(b < nb):
                    wait_apart(pool, a4["xt_mm"], b + 1, passed)
                    gather(b + 1, row_all[:, bass.ds(b + 1, 1)])
                    for u in POOL_UNITS:
                        lo_unit(pool, "wlo_p", b + 1, u)

        @block.scalar
        def _(act):
            def hi_unit(b, u, first=False):
                act.wait_ge(a4[f"raw{u // 2}"], b * 16 + 16)
                if not first:
                    act.wait_ge(a4["used"], (b - 1) * NUNIT + (u + 1))
                act.activation(whi4[:, u, :], wraw4[:, u, :], ACT.Copy).then_inc(a4["whi_d"], 1)

            def xt_hi(b):
                act.wait_ge(a4["xt_mm"], b + 1)
                act.activation(xTh[:, :, :].rearrange("p k m -> p (k m)"), ps[:, 2:4, :].rearrange("p a b -> p (a b)"), ACT.Copy)\
                    .then_inc(a4["xt_hi"], 1)

            for u in range(NUNIT):
                hi_unit(0, u, first=True)
                if u == 3:
                    xt_hi(0)
            nb = block_count(act)
            with act.Fori(0, NBLK) as b:
                with act.If(b < nb):
                    for u in range(KD - 1):
                        hi_unit(b + 1, u)
                    act.wait_ge(a4["used"], b * NUNIT + KD)
                    act.activation(hs[:, :], ps[:, 0, :], ACT.Silu).then_inc(a4["silu_d"], 1)
                    hi_unit(b + 1, KD - 1)
                    act.wait_ge(a4["ht_mm4"], b + 1)
                    act.activation(hTh[:, :, :].rearrange("p k m -> p (k m)"), ps[:, 4, :], ACT.Copy).then_inc(a4["ht_hi4"], 1)
                    xt_hi(b + 1)
                    for u in range(KD, NUNIT):
                        hi_unit(b + 1, u)

        @block.vector
        def _(dve):
            def xt_lo(b):
                dve.wait_ge(a4["xt_hi"], b + 1)
                dve.tensor_tensor(xTl[:, :, :].rearrange("p k m -> p (k m)"), ps[:, 2:4, :].rearrange("p a b -> p (a b)"),
                                  xTh[:, :, :].rearrange("p k m -> p (k m)").bitcast(F32), ALU.subtract).then_inc(a4["xt_lo"], 1)

            dve.memset(tok4[:, 0:1], 0.0).then_inc(a4["y_ev4"], 1)
            dve.memset(tok4[:, 1:2], 0.0).then_inc(a4["y_free"], 16)
            for u in DVE_UNITS:
                lo_unit(dve, "wlo_d", 0, u)
                if u == 3:
                    xt_lo(0)
            nb = block_count(dve)
            with dve.Fori(0, NBLK) as b:
                with dve.If(b < nb):
                    for u in DVE_UNITS:
                        if u == KD:
                            dve.wait_ge(a4["silu_d"], b + 1)
                            dve.tensor_tensor(hs[:, :], hs[:, :], ps[:, 1, :], ALU.mult).then_inc(a4["mul_d"], 1)
                            dve.wait_ge(a4["ht_hi4"], b + 1)
                            dve.tensor_tensor(hTl[:, :, :].rearrange("p k m -> p (k m)"), ps[:, 4, :],
                                              hTh[:, :, :].rearrange("p k m -> p (k m)").bitcast(F32), ALU.subtract).then_inc(a4["ht_lo4"], 1)
                            xt_lo(b + 1)
                        lo_unit(dve, "wlo_d", b + 1, u)
                    dve.wait_ge(a4["used"], b * NUNIT + NUNIT)
                    dve.wait_ge(a4["y_free"], b * 16 + 16)
                    dve.tensor_copy(ys[:, :].rearrange("p (a b) -> p a b", a=2), ps[:, 5:7, :]).then_inc(a4["y_ev4"], 1)

        @block.tensor
        def _(pe):
            def turn_x(b, first=False):
                pe.wait_ge(a4["xg_in"], b * 16 + 16)
                if not first:
                    pe.wait_ge(a4["xt_lo"], b)
                for k in range(KD):
                    mm = pe.transpose(ps[:, 2 + k // 4, (k % 4) * P:(k % 4 + 1) * P], xg[:, k * P:(k + 1) * P], ident[:, :])
                mm.then_inc(a4["xt_mm"], 1)

            def product(b, u, lhs_hi, lhs_lo, bank, first, last):
                lo_ready(pe, b, u)
                for half in range(2):
                    cols = slice(half * 512, (half + 1) * 512)
                    for j, (x, y) in enumerate(((lhs_hi, whi4), (lhs_lo, whi4), (lhs_hi, wlo4))):
                        mm = pe.matmul(ps[:, bank + half, :], x, y[:, u, cols], start=first and j == 0, stop=last and j == 2)
                mm.then_inc(a4["used"], 1)

            turn_x(0, first=True)
            nb = block_count(pe)
            with pe.Fori(0, NBLK) as b:
                with pe.If(b < nb):
                    pe.wait_ge(a4["xt_lo"], b + 1)
                    for k in range(KD):
                        product(b, k, xTh[:, k, :], xTl[:, k, :], 0, k == 0, k == KD - 1)
                    turn_x(b + 1)
                    pe.wait_ge(a4["mul_d"], b + 1)
                    for k in range(FK):
                        mm = pe.transpose(ps[:, 4, k * P:(k + 1) * P], hs[:, k * P:(k + 1) * P], ident[:, :])
                    mm.then_inc(a4["ht_mm4"], 1)
                    pe.wait_ge(a4["ht_lo4"], b + 1)
                    pe.wait_ge(a4["y_ev4"], b + 1)
                    for k in range(FK):
                        product(b, KD + k, hTh[:, k, :], hTl[:, k, :], 5, k == 0, k == FK - 1)
        blk.close()

        p5 = ExitStack()
        yg = sb("yg", [P, 3, 2, D], F32, p5)
        x1t = sb("x1t", [P, 3, D], F32, p5)
        r5 = sb("r5", [P, 2, D], F32, p5)
        o5 = sb("o5", [P, 2, D], F32, p5)
        g2row = sb("g2row", [P, D], F32, p5)
        ln2 = sb("ln2", [P, 2, D], F32, p5)
        st5 = sb("st5", [P, 2, 16], F32, p5)
        p5.close()
        a5 = {n: sem(n) for n in ("c5_in", "yg0", "yg1", "yg2", "x1t0", "x1t1", "x1t2", "y_sum", "var_d", "root_d", "norm_d", "gain_d", "fin_d",
                                  "fin_out0", "fin_out1", "dve5_c")}
        block = blk.enter_context(nc.Block())

        @block.sync
        def _(sp):
            sp.dma_start(g2row[:, :], g2_dram).then_inc(a5["c5_in"], 16)
            sp.dma_start(ln2[:, :, :], A["ln2"]).then_inc(a5["c5_in"], 16)

            def load_x1(t):
                sp.dma_start(x1t[:, t % 3, :], x1_dram[t * P:(t + 1) * P, :]).then_inc(a5[f"x1t{t % 3}"], 16)

            for t in range(3):
                load_x1(t)
            for t in range(ST):
                if t + 3 < ST:
                    sp.wait_ge(a5["y_sum"], t + 1)
                    load_x1(t + 3)
                sp.wait_ge(a5["fin_d"], t + 1)
                sp.dma_start(out[0, t * P:(t + 1) * P, :], o5[:, t % 2, :]).then_inc(a5[f"fin_out{t % 2}"], 16)
            for b in range(2):
                sp.wait_ge(a5[f"fin_out{b}"], 16 * (ST // 2))

        @block.gpsimd
        def _(pool):
            def gather(t):
                if t >= 3:
                    pool.wait_ge(a5["y_sum"], t - 2)
                for c in range(2):
                    pool.indirect_dma_start(yg[:, t % 3, c, :], None, y_dram, bass.IndirectOffsetOnAxis(ap=dest[:, c, t:t + 1], axis=0))\
                        .then_inc(a5[f"yg{t % 3}"], 16)

            for t in range(2):
                gather(t)
            pool.wait_ge(a5["c5_in"], 32)
            for t in range(ST):
                if t + 2 < ST:
                    gather(t + 2)
                pool.wait_ge(a5["norm_d"], t + 1)
                if t >= 2:
                    pool.wait_ge(a5[f"fin_out{t % 2}"], 16 * (t // 2))
                pool.tensor_tensor(o5[:, t % 2, :], r5[:, t % 2, :], ln2[:, 0, :], ALU.mult).then_inc(a5["gain_d"], 1)

        @block.scalar
        def _(act):
            for t in range(ST):
                act.wait_ge(a5["var_d"], t + 1)
                act.activation(st5[:, t % 2, 14:15], st5[:, t % 2, 13:14], ACT.Sqrt).then_inc(a5["root_d"], 1)

        @block.vector
        def _(dve):
            ch = Chain(dve, a5["dve5_c"])
            dve.wait_ge(a5["c5_in"], 32)

            def shift(t):
                dve.wait_ge(a5["gain_d"], t + 1)
                dve.tensor_tensor(o5[:, t % 2, :], o5[:, t % 2, :], ln2[:, 1, :], ALU.add).then_inc(a5["fin_d"], 1)

            for t in range(ST):
                s_, r = st5[:, t % 2, :], r5[:, t % 2, :]
                dve.wait_ge(a5[f"yg{t % 3}"], 32 * (t // 3 + 1))
                if t >= 2:
                    dve.wait_ge(a5["gain_d"], t - 1)
                ch.link(dve.tensor_scalar(r, yg[:, t % 3, 0, :], gates[:, 0, t:t + 1], None, ALU.mult))
                ch.link(dve.scalar_tensor_tensor(out=r, in0=yg[:, t % 3, 1, :], scalar=gates[:, 1, t:t + 1], in1=r, op0=ALU.mult, op1=ALU.add))
                ch.link(dve.tensor_tensor(r, r, g2row[:, :], ALU.mult))
                dve.wait_ge(a5[f"x1t{t % 3}"], 16 * (t // 3 + 1))
                dve.scalar_tensor_tensor(out=r, in0=x1t[:, t % 3, :], scalar=ALPHA, in1=r, op0=ALU.mult, op1=ALU.add).then_inc(a5["y_sum"], 1)
                dve.wait_ge(a5["y_sum"], t + 1)
                for b in range(2):
                    ins = dve.bn_stats(s_[:, 6 * b:6 * b + 6], r5[:, t % 2, b * 512:(b + 1) * 512])
                ch.link(ins)
                ch.link(dve.bn_aggr(s_[:, 12:14], s_[:, 0:12]))
                dve.tensor_scalar(s_[:, 13:14], s_[:, 13:14], EPS, None, ALU.add).then_inc(a5["var_d"], 1)
                if t:
                    shift(t - 1)
                dve.wait_ge(a5["root_d"], t + 1)
                ch.link(dve.reciprocal(s_[:, 15:16], s_[:, 14:15]))
                dve.tensor_scalar(r, r, s_[:, 12:13], s_[:, 15:16], ALU.subtract, ALU.mult).then_inc(a5["norm_d"], 1)
            shift(ST - 1)
        blk.close()


def layouts(inputs):
    import numpy as np
    a = {k: np.asarray(v) for k, v in inputs.items()}
    o = {}
    o["xT"] = np.concatenate([a["x"][0], a["ctx"][0]], 0).T
    o["x"] = a["x"][0]
    o["cvec"] = np.stack([a["c"][0], a["c_ctx"]], -1).reshape(KD, P, 2).transpose(1, 0, 2)
    o["ada_w"] = a["ada_w"][0]
    o["adab_cols"] = a["ada_b"][0][0:2048].reshape(16, P).T
    o["adab_rows"] = np.broadcast_to(a["ada_b"][0][2048:], (P, 4096)).reshape(P, 4, D)
    w = a["w_in"][0]
    ax_, ag, gq, gk, gv, dq, dk, dv = np.split(w, np.cumsum([256, 256, 512, 128, 128, 256, 256]).tolist(), axis=1)
    o["w_in"] = np.concatenate([ax_, ag, gq, gv, gk, dk, dv, dq], 1)
    o["ident"] = np.eye(P, dtype=np.float32)

    def rope(dim):
        t = np.arange(S)
        n = dim // 4
        inv = np.float32(10000.0) ** (-np.arange(n, dtype=np.float32) / np.float32(n))
        ang = np.concatenate([(t // 64).astype(np.float32)[:, None] * inv, (t % 64).astype(np.float32)[:, None] * inv], -1)
        c, s_ = np.cos(ang), np.sin(ang)
        tab = np.stack([np.stack([c, c], -1).reshape(S, dim), np.stack([-s_, s_], -1).reshape(S, dim)], 1)
        return tab.reshape(ST, P, 2, dim).transpose(1, 0, 2, 3).astype(np.float32)

    o["rope_g"], o["rope_d"] = rope(GD), rope(DQ)
    swap = np.arange(GD).reshape(-1, 2)[:, ::-1].reshape(-1)
    o["gvec"] = np.broadcast_to(np.stack([np.stack([g[0], g[0][swap]]) for g in (a["q_norm_g"], a["k_norm_g"])]), (P, 2, 2, GD))
    o["lvec"] = np.broadcast_to(a["diff_lambda"][0], (P, 4, DQ))
    cols = [a["conv_w"][0][k] for k in range(4)] + [a["conv_b"][0]] + [a[n][0][d] for n in ("rg_ba", "rg_bx", "rg_lam") for d in range(2)]
    cols += [cols[0]] * 5
    o["lruc"] = np.stack(cols, -1).reshape(LF, P, 16).transpose(1, 0, 2)
    g = np.stack([a["rg_wa"][0], a["rg_wx"][0]], 1)
    g = g.reshape(2, 2, LF, 2, 64, 64)
    o["wg"] = g.transpose(3, 4, 2, 0, 1, 5).reshape(2, 64, 8, 64)
    o["subg"] = np.broadcast_to(a["diff_subln_g"][0], (P, DV))
    o["w_out"] = a["w_out"][0]
    o["ln1"] = np.broadcast_to(np.stack([a["ln1_g"][0], a["ln1_b"][0]]), (P, 2, D))
    o["rw"] = a["router_w"].reshape(KD, P, E).transpose(1, 0, 2)
    o["rb"] = np.broadcast_to(a["router_b"], (P, E))
    o["tri"] = np.stack([np.triu(np.ones((P, P), np.float32), 1), np.ones((P, P), np.float32)], 1)
    o["kc"] = np.broadcast_to(np.concatenate([np.arange(8) * BLK, np.arange(NBLK + 2)]).astype(np.float32), (P, 8 + NBLK + 2))
    gu = np.concatenate([a["exp_w_gate"][0], a["exp_w_up"][0]], -1).reshape(E, KD, P, D)
    o["wexp"] = np.concatenate([gu, a["exp_w_down"][0].reshape(E, FK, P, D)], 1).transpose(0, 2, 1, 3)
    o["ln2"] = np.broadcast_to(np.stack([a["ln2_g"][0], a["ln2_b"][0]]), (P, 2, D))
    return {k: np.ascontiguousarray(v) for k, v in o.items()}


def kernel(**inputs):
    import concourse.bacc as bacc
    from concourse.bass_utils import run_bass_kernel_spmd
    nc = bacc.Bacc("TRN2", target_bir_lowering=False, num_devices=1)
    arrays = layouts(inputs)
    A = {n: nc.dram_tensor(f"in_{n}", v.shape, mybir.dt.from_np(v.dtype), kind="ExternalInput").ap() for n, v in arrays.items()}
    out = nc.dram_tensor("out", (1, S, D), F32, kind="ExternalOutput").ap()
    build(nc, A, out)
    r = run_bass_kernel_spmd(nc, [{f"in_{n}": v for n, v in arrays.items()}], core_ids=[0])
    return r.results[0]["out"]
```

```python
from contextlib import ExitStack

import concourse.bass as bass
from concourse import mybir

F32 = mybir.dt.float32
F32R = mybir.dt.float32r
I32 = mybir.dt.int32
ALU = mybir.AluOpType
ACT = mybir.ActivationFunctionType
AX = mybir.AxisListType

P = 128
D = 1024
KD = D // P
S = 1024
C = 256
T = S + C
ST, CT = S // P, C // P
TT = ST + CT
LRU = 256
LF = LRU // P
GH, GKV, GD = 8, 2, 64
DH, DQ, DV = 4, 32, 64
LAM_INIT = 0.8 - 0.6
EPS = 1e-6
RG_C = 8.0
ALPHA = 2.0 ** 0.25
CONV = 4
PADL = 1 + S + 3 + C + 2
UL = PADL - (CONV - 1)
UC = S + 3
E, G, EG, FF = 16, 4, 4, 512
FK = FF // P
NUNIT = KD + FK
BLK = P
NBLK = 2 * S // BLK + E - 1
MINBLK = 2 * S // BLK
ROWS = (NBLK + 1) * BLK


class Chain:

    def __init__(self, engine, sem, before):
        self.engine, self.sem, self.n = engine, sem, before[-1].n if before else 0
        before.append(self)

    def mark(self, ins):
        self.n += 1
        ins.then_inc(self.sem, 1)

    def link(self, ins):
        self.mark(ins)
        self.engine.wait_ge(self.sem, self.n)


def wait_apart(engine, sem, value, passed):
    engine.wait_ge(sem, value)
    engine.sem_inc(passed, 1)


def build(nc, A, out):
    def dram(name, shape, dt=F32):
        return nc.dram_tensor(name, shape, dt, kind="Internal").ap()

    q_dram = dram("q_dram", (S, GH * GD))
    k_dram = dram("k_dram", (T, GKV * GD + DH * 2 * DQ))
    dq_dram = dram("dq_dram", (S, DH * 2 * DQ))
    x1_dram, h_dram = dram("x1_dram", (S, D)), dram("h_dram", (S, D))
    g2_dram = dram("g2_dram", (P, D))
    rows_dram = dram("rows_dram", (ROWS, 1), I32)
    y_dram = dram("y_dram", (ROWS, D))

    with ExitStack() as whole:
        def sb(name, shape, dt=F32, at=whole):
            return at.enter_context(nc.sbuf_tensor(name, shape, dt))

        def sem(name):
            return whole.enter_context(nc.semaphore(name))

        ps = whole.enter_context(nc.psum_tensor("ps", [P, 8, 512], F32))
        ident = sb("ident", [P, P])
        dest = sb("dest", [P, 2, ST], I32)
        gates = sb("gates", [P, 2, ST])
        blk_tab = sb("blk_tab", [P, NBLK + 3], I32)
        attn = ExitStack()
        V = sb("V", [P, TT, GKV, GD + 1], F32, attn)
        DVt = sb("DVt", [P, TT, DH, DV + 1], F32, attn)
        ya = sb("ya", [P, LF, S], F32, attn)
        lam = sb("lam", [P, 8], F32, attn)
        silu_c = sb("silu_c", [P, KD, 2], F32, attn)

        p1 = ExitStack()
        cvec = sb("cvec", [P, KD, 2], F32, p1)
        pm = ExitStack()
        adar = sb("adar", [P, KD, 2048], F32, pm)
        modr = sb("modr", [2, 2048], F32, pm)
        pm.close()
        xhi = sb("xhi", [P, KD, T], F32R, p1)
        xlo = sb("xlo", [P, KD, T], F32R, p1)
        whi = sb("whi", [P, KD, 512], F32R, p1)
        wlo = sb("wlo", [P, KD, 512], F32R, p1)
        NWR = 4
        wraw = sb("wraw", [P, NWR, 512], F32, p1)
        ax = sb("ax", [P, LF, PADL], F32, p1)
        rope_q = sb("rope_q", [P, ST, 2, GD], F32, p1)
        rope_k = sb("rope_k", [P, ST, 2, GD], F32, p1)
        rope_d = sb("rope_d", [P, ST, 2, DQ], F32, p1)
        gvec = sb("gvec", [P, 2, 2, GD], F32, p1)
        lvec = sb("lvec", [P, 4, DQ], F32, p1)
        modc = sb("modc", [P, 16, 2], F32, p1)
        adab = sb("adab", [P, 16], F32, p1)
        lruc = sb("lruc", [P, LF, 16], F32, p1)
        nsp = sb("nsp", [P, LF, 2, 2], F32, p1)
        stat = sb("stat", [P, 2, 3, 8], F32, p1)
        wg = sb("wg", [P, 8, P], F32, p1)
        pa = ExitStack()
        xraw = sb("xraw", [P, 6, T], F32, pa)
        pa.close()
        pl = ExitStack()
        U = sb("U", [P, LF, UL], F32, pl)
        TH = sb("TH", [P, UL], F32, pl)
        SQ = sb("SQ", [P, UL], F32, pl)
        H = sb("H", [P, S], F32, pl)
        zst = sb("zst", [P, 2, 512], F32, pl)
        zo = sb("zo", [P, 2, 512], F32, pl)
        pl.close()
        p1.close()
        R = ax[:, 0, 0:UL]
        I = ax[:, 1, 0:UL]

        dve_links = []
        passed = sem("passed")
        s = {n: sem(n) for n in (
            "consts", "c_in", "silu", "adar0", "adar1", "adar2", "ada_used", "modr_d",
            "xraw0", "xraw1", "xraw2", "x_mod", "x_hi", "x_lo",
            "wraw0", "wraw1", "wraw2", "wraw3", "w_hi", "w_lo", "w_used",
            "proj_done", "proj_out", "prep", "wg_load", "z_sq", "z_rt", "z_fin", "zo_out0", "zo_out1",
            "u_ready", "gate_mm", "gate_sig", "a_rdy", "m_neg", "m_rt",
            "lru_done", "dve_c", "act_c", "sp_rdy", "nsp_rdy")}
        blk = ExitStack()
        block = blk.enter_context(nc.Block())

        units = [("L", f, o, n) for f in range(LF) for o, n in ((0, 512), (512, 512), (S, C))] + \
                [("L", LF + f, o, 512) for f in range(LF) for o in (0, 512)]
        NL = len(units)
        units += [("Q", t) for t in range(ST)] + [("K", t) for t in range(TT)] + [("E", t) for t in range(TT)]
        group = {"L": 0, "Q": 1, "K": 2, "E": 3}
        last_of = [max(i for i, u in enumerate(units) if group[u[0]] == g) for g in range(4)]
        z_units = [i for i, u in enumerate(units) if u[0] in "QK" or (u[0] == "E" and u[1] < ST)]
        z_of = {u: n for n, u in enumerate(z_units)}
        NU, RING = len(units), 4
        combos = [(f, d) for f in range(LF) for d in range(2)]
        gate_at = {NL + 1 + 3 * c + g: (c, g) for c in range(4) for g in range(2)}
        CONSTS = 16 * 6

        def w_free(eng, c):
            g, k = divmod(c, KD)
            if g and k < KD - 1:
                eng.wait_ge(s["w_used"], (g - 1) * (KD - 1) + k + 1)
            elif g:
                eng.wait_ge(s["proj_done"], last_of[g - 1] + 1)

        @block.sync
        def _(sp):
            sp.dma_start(cvec[:, :, :], A["cvec"]).then_inc(s["c_in"], 16)
            sp.dma_start(ident[:, :], A["ident"]).then_inc(s["c_in"], 16)
            sp.dma_start(adab[:, :], A["adab_cols"]).then_inc(s["c_in"], 16)
            for p, (k0, k1) in enumerate(((0, 2), (2, 5), (5, KD))):
                sp.dma_start(adar[:, k0:k1, :], A["ada_w"][k0 * P:k1 * P, 0:2048].rearrange("(k p) n -> p k n", p=P)).then_inc(s[f"adar{p}"], 16)

            def load_w(c):
                g, k = divmod(c, KD)
                if c >= NWR:
                    sp.wait_ge(s["w_lo"], c - NWR + 1)
                sp.dma_start(wraw[:, c % NWR, :], A["w_in"][k * P:(k + 1) * P, g * 512:(g + 1) * 512])\
                    .then_inc(s[f"wraw{c % NWR}"], 16)

            for p in range(KD // 2):
                if p >= 3:
                    sp.wait_ge(s["x_lo"], 2 * (p - 3) + 2)
                slot = 2 * (p % 3)
                sp.dma_start(xraw[:, slot:slot + 2, :], A["xT"][2 * p * P:(2 * p + 2) * P, :].rearrange("(k p) n -> p k n", p=P))\
                    .then_inc(s[f"xraw{p % 3}"], 16)
                if p < 2:
                    load_w(2 * p)
                    load_w(2 * p + 1)
            for k in range(4, KD):
                load_w(k)
            for dst, name in ((rope_q[:, :, :, :], "rope_g"), (rope_k[:, :, :, :], "rope_g"),
                              (rope_d[:, :, :, :], "rope_d"), (gvec[:, :, :, :], "gvec"), (lvec[:, :, :], "lvec"),
                              (lruc[:, :, :], "lruc")):
                sp.dma_start(dst, A[name]).then_inc(s["consts"], 16)
            sp.wait_ge(s["prep"], 2)
            for b in range(2):
                sp.dma_start(wg[b * 64:(b + 1) * 64, :, b * 64:(b + 1) * 64], A["wg"][b]).then_inc(s["wg_load"], 16)

            def store_z(i):
                n, (kind, t) = z_of[i], units[i]
                rows = slice(t * P, (t + 1) * P)
                dst, lo = {"Q": (q_dram, 0), "K": (k_dram, 128), "E": (dq_dram, 256)}[kind]
                sp.wait_ge(s["z_fin"], n + 1)
                sp.dma_start(dst[rows, :], zo[:, n % 2, lo:512]).then_inc(s[f"zo_out{n % 2}"], 16)

            for c in range(KD, 2 * KD):
                load_w(c)
            for g in range(1, 4):
                mine = [i for i in z_units if group[units[i][0]] == g]
                for c in range((g + 1) * KD, (g + 1) * KD + NWR if g < 3 else 0):
                    load_w(c)
                for i in mine[:-1]:
                    store_z(i)
                for c in range((g + 1) * KD + NWR, (g + 2) * KD if g < 3 else 0):
                    load_w(c)
                store_z(mine[-1])
            for b in range(2):
                sp.wait_ge(s[f"zo_out{b}"], 16 * len(z_units[b::2]))

        @block.gpsimd
        def _(pool):
            pool.memset(V[:, :, :, GD:GD + 1], 1.0)
            pool.memset(DVt[:, :, :, DV:DV + 1], 1.0)
            pool.memset(ax[:, :, :], 0.0).then_inc(s["prep"], 1)
            pool.memset(wg[:, :, :], 0.0).then_inc(s["prep"], 1)
            for c in range(4 * KD):
                pool.wait_ge(s["w_hi"], c + 1)
                pool.tensor_tensor(wlo[:, c % KD, :], wraw[:, c % NWR, :], whi[:, c % KD, :].bitcast(F32), ALU.subtract)\
                    .then_inc(s["w_lo"], 1)

        @block.scalar
        def _(act):
            ch = Chain(act, s["act_c"], [])
            act.wait_ge(s["c_in"], 48)
            act.activation(silu_c[:, :, :], cvec[:, :, :], ACT.Silu).then_inc(s["silu"], 1)

            def w_hi(c):
                act.wait_ge(s[f"wraw{c % NWR}"], 16 * (c // NWR + 1))
                w_free(act, c)
                act.activation(whi[:, c % KD, :], wraw[:, c % NWR, :], ACT.Copy).then_inc(s["w_hi"], 1)

            for k in range(KD):
                act.wait_ge(s["x_mod"], k + 1)
                act.activation(xhi[:, k, :], xraw[:, k % 6, :], ACT.Copy).then_inc(s["x_hi"], 1)
                w_hi(k)

            def sqrt_rms(i):
                n, nh = z_of[i], {"Q": GH, "K": GKV}[units[i][0]]
                act.wait_ge(s["z_sq"], n + 1)
                act.activation(stat[:, n % 2, 1, 0:nh], stat[:, n % 2, 0, 0:nh], ACT.Sqrt).then_inc(s["z_rt"], 1)

            def lru_gate(c, g):
                f, d = combos[c]
                act.wait_ge(s["gate_mm"], 2 * c + g + 1)
                if g == 0 and c:
                    act.wait_ge(s["lru_done"], c)
                act.activation(R if g == 0 else I, ps[:, 0:3, :].rearrange("p a b -> p (a b)")[:, 0:UL], ACT.Sigmoid,
                               bias=lruc[:, f, 5 + 2 * g + d:6 + 2 * g + d]).then_inc(s["gate_sig"], 1)
                if g == 1:
                    act.wait_ge(s["gate_sig"], 2 * c + 2)
                    act.wait_ge(s["nsp_rdy"], 1)
                    ch.link(act.activation(TH[:, :], R, ACT.Tanh, scale=nsp[:, f, d:d + 1, 0]))
                    act.activation(R, R, ACT.Exp, scale=nsp[:, f, d:d + 1, 0]).then_inc(s["a_rdy"], 1)

            def lru_root(c):
                act.wait_ge(s["m_neg"], c + 1)
                act.activation(TH[:, :], TH[:, :], ACT.Sqrt, scale=-1.0).then_inc(s["m_rt"], 1)

            for i, u in enumerate(units):
                if i in last_of and i != NU - 1:
                    for k in range(KD):
                        w_hi((group[u[0]] + 1) * KD + k)
                act.wait_ge(s["proj_done"], i + 1)
                src = ps[:, 4 + i % RING, :]
                if i == 0:
                    act.wait_ge(s["prep"], 1)
                if i == NL:
                    act.wait_ge(s["consts"], CONSTS)
                    for f in range(LF):
                        ch.link(act.activation(nsp[:, f, :, 1], lruc[:, f, 9:11], ACT.Exp, scale=-1.0))
                        ins = act.activation(nsp[:, f, :, 0], nsp[:, f, :, 1], ACT.Ln, bias=1.0)
                    ins.then_inc(s["sp_rdy"], 1)
                if u[0] == "L":
                    _, f, o, n = u
                    if f < LF:
                        at = 1 + o if o < S else UC + 1
                        last = act.activation(ax[:, f, at:at + n], src[:, 0:n], ACT.Copy)
                    else:
                        last = act.activation(ya[:, f - LF, o:o + n], src[:, 0:n], ACT.Gelu_apprx_tanh)
                else:
                    t, n = u[1], z_of.get(i)
                    if n is not None and n >= 2:
                        act.wait_ge(s["z_fin"], n - 1)
                    if u[0] == "K":
                        act.activation(V[:, t, :, 0:GD], src[:, 0:128].rearrange("p (h d) -> p h d", h=GKV), ACT.Copy)
                    if u[0] == "E":
                        last = act.activation(DVt[:, t, :, 0:DV], src[:, 0:256].rearrange("p (h d) -> p h d", h=DH), ACT.Copy)
                    lo = {"Q": 0, "K": 128, "E": 256}[u[0]]
                    if n is not None:
                        last = act.activation(zst[:, n % 2, lo:512], src[:, lo:512], ACT.Copy)
                last.then_inc(s["proj_out"], 1)
                if u[0] in "QK":
                    sqrt_rms(i)
                if i - 1 in gate_at and gate_at[i - 1][1] == 1:
                    lru_root(gate_at[i - 1][0])
                if i in gate_at:
                    lru_gate(*gate_at[i])

        @block.vector
        def _(dve):
            ch = Chain(dve, s["dve_c"], dve_links)
            dve.wait_ge(s["ada_used"], 1)
            dve.tensor_copy(modr[:, :].rearrange("p (a b) -> p a b", a=4), ps[0:2, 4:8, :]).then_inc(s["modr_d"], 1)
            dve.wait_ge(s["ada_used"], 2)
            dve.wait_ge(s["c_in"], 48)
            for j in range(2):
                ins = dve.tensor_tensor(modc[:, :, j], ps[:, 0, 0:32].rearrange("p (n j) -> p n j", j=2)[:, :, j],
                                        adab[:, :], ALU.add)
            ch.link(ins)
            ch.link(dve.tensor_scalar(modc[:, 8:16, :], modc[:, 8:16, :], 1.0, None, ALU.add))

            def modulate(k):
                dve.wait_ge(s[f"xraw{k // 2 % 3}"], 16 * (k // 6 + 1))
                x = xraw[:, k % 6, :]
                dve.tensor_scalar(x[:, 0:S], x[:, 0:S], modc[:, 8 + k, 0:1], modc[:, k, 0:1], ALU.mult, ALU.add)
                dve.tensor_scalar(x[:, S:T], x[:, S:T], modc[:, 8 + k, 1:2], modc[:, k, 1:2], ALU.mult, ALU.add)\
                    .then_inc(s["x_mod"], 1)

            modulate(0)
            for k in range(KD):
                if k + 1 < KD:
                    modulate(k + 1)
                dve.wait_ge(s["x_hi"], k + 1)
                dve.tensor_tensor(xlo[:, k, :], xraw[:, k % 6, :], xhi[:, k, :].bitcast(F32), ALU.subtract)\
                    .then_inc(s["x_lo"], 1)

            dve.wait_ge(s["consts"], CONSTS)
            for tab, j in ((rope_q, 0), (rope_k, 1)):
                for h in range(2):
                    dve.tensor_tensor(tab[:, :, h, :], tab[:, :, h, :],
                                      gvec[:, j, h, :].unsqueeze(1).broadcast_to([P, ST, GD]), ALU.mult)
            for j in range(2):
                ch.link(dve.tensor_tensor(lvec[:, 2 * j, :], lvec[:, 2 * j, :], lvec[:, 2 * j + 1, :], ALU.mult))
                ch.link(dve.tensor_reduce(lam[:, j:j + 1], lvec[:, 2 * j, :], AX.X, ALU.add))

            dve.wait_ge(s["proj_out"], 3 * LF)
            for f in range(LF):
                ch.link(dve.tensor_scalar(U[:, f, :], ax[:, f, 0:UL], lruc[:, f, 0:1], lruc[:, f, 4:5], ALU.mult, ALU.add))
                for k in range(1, CONV):
                    ins = dve.scalar_tensor_tensor(out=U[:, f, :], in0=ax[:, f, k:k + UL], scalar=lruc[:, f, k:k + 1],
                                                   in1=U[:, f, :], op0=ALU.mult, op1=ALU.add)
                    if f == LF - 1 and k == CONV - 1:
                        ins.then_inc(s["u_ready"], 1)
                    else:
                        ch.link(ins)
            dve.wait_ge(s["sp_rdy"], 1)
            dve.tensor_scalar(nsp[:, :, :, 0], nsp[:, :, :, 0], -RG_C, None, ALU.mult).then_inc(s["nsp_rdy"], 1)

            def rms(n, lo, nh, w):
                z = zst[:, n % 2, lo:lo + nh * w].rearrange("p (h d) -> p h d", h=nh)
                o = zo[:, n % 2, lo:lo + nh * w].rearrange("p (h d) -> p h d", h=nh)
                st = stat[:, n % 2]
                ch.link(dve.tensor_tensor(o, z, z, ALU.mult))
                ch.link(dve.tensor_reduce(st[:, 0, 0:nh], o, AX.X, ALU.add))
                dve.tensor_scalar(st[:, 0, 0:nh], st[:, 0, 0:nh], 1.0 / w, EPS, ALU.mult, ALU.add).then_inc(s["z_sq"], 1)
                dve.wait_ge(s["z_rt"], n + 1)
                ch.link(dve.reciprocal(st[:, 2, 0:nh], st[:, 1, 0:nh]))
                ch.link(dve.tensor_tensor(z, z, st[:, 2, 0:nh].unsqueeze(2).broadcast_to([P, nh, w]), ALU.mult))

            def rotate(n, lo, tab, t, nh, w):
                z, o = zst[:, n % 2, lo:lo + nh * w], zo[:, n % 2, lo:lo + nh * w]
                swapped = z.rearrange("p (h c two) -> p h c two", h=nh, two=2)[:, :, :, ::-1]
                sines = tab[:, t, 1, :].rearrange("p (c two) -> p c two", two=2).unsqueeze(1).broadcast_to([P, nh, w // 2, 2])
                zh = z.rearrange("p (h d) -> p h d", h=nh)
                ch.link(dve.tensor_tensor(o.rearrange("p (h c two) -> p h c two", h=nh, two=2), swapped, sines, ALU.mult))
                ch.link(dve.tensor_tensor(zh, zh, tab[:, t, 0, :].unsqueeze(1).broadcast_to([P, nh, w]), ALU.mult))
                return dve.tensor_tensor(o, o, z, ALU.add)

            def heads(i):
                (kind, t), n = units[i], z_of[i]
                dve.wait_ge(s["proj_out"], i + 1)
                if n >= 2:
                    dve.wait_ge(s[f"zo_out{n % 2}"], 16 * (n // 2))
                if kind == "Q":
                    rms(n, 0, GH, GD)
                    last = rotate(n, 0, rope_q, t, GH, GD)
                elif kind == "E":
                    last = rotate(n, 256, rope_d, t, 2 * DH, DQ)
                else:
                    rms(n, 128, GKV, GD)
                    if t < ST:
                        ch.mark(rotate(n, 128, rope_k, t, GKV, GD))
                        last = rotate(n, 256, rope_d, t, 2 * DH, DQ)
                    else:
                        dve.tensor_tensor(zo[:, n % 2, 128:256].rearrange("p (h d) -> p h d", h=GKV),
                                          zst[:, n % 2, 128:256].rearrange("p (h d) -> p h d", h=GKV),
                                          gvec[:, 1, 0, :].unsqueeze(1).broadcast_to([P, GKV, GD]), ALU.mult)
                        last = dve.tensor_copy(zo[:, n % 2, 256:512], zst[:, n % 2, 256:512])
                last.then_inc(s["z_fin"], 1)

            def lru_mult(c):
                f, d = combos[c]
                dve.wait_ge(s["gate_sig"], 2 * c + 2)
                dve.tensor_tensor(I, I, U[:, f, :], ALU.mult)
                dve.wait_ge(s["a_rdy"], c + 1)
                ch.link(dve.tensor_tensor(SQ[:, :], R, R, ALU.mult))
                dve.scalar_tensor_tensor(out=TH[:, :], in0=SQ[:, :], scalar=1.0, in1=TH[:, :], op0=ALU.add, op1=ALU.mult)\
                    .then_inc(s["m_neg"], 1)

            def lru_scan(c):
                f, d = combos[c]
                dve.wait_ge(s["m_rt"], c + 1)
                ch.link(dve.tensor_tensor(I, I, TH[:, :], ALU.mult))
                rv = slice(None, None, -1) if d else slice(None)
                cx, lx = slice(UC, UC + C), slice(0, S)
                ch.link(dve.tensor_tensor_scan(I[:, cx][:, rv], R[:, cx][:, rv], I[:, cx][:, rv], 0.0, ALU.mult, ALU.add))
                h0 = I[:, UC:UC + 1] if d else I[:, UC + C - 1:UC + C]
                dst = I[:, lx] if d else H[:, :]
                scan = dve.tensor_tensor_scan(dst[:, rv], R[:, lx][:, rv], I[:, lx][:, rv], h0, ALU.mult, ALU.add)
                if d == 0:
                    scan.then_inc(s["lru_done"], 1)
                else:
                    ch.link(scan)
                    ch.link(dve.tensor_tensor(H[:, :], H[:, :], I[:, lx], ALU.add))
                    dve.wait_ge(s["proj_out"], NL)
                    dve.tensor_tensor(ya[:, f, :], ya[:, f, :], H[:, :], ALU.mult).then_inc(s["lru_done"], 1)

            for i, u in enumerate(units):
                if i in z_of:
                    heads(i)
                if i - 1 in gate_at and gate_at[i - 1][1] == 1:
                    lru_scan(gate_at[i - 1][0])
                if i in gate_at and gate_at[i][1] == 1:
                    lru_mult(gate_at[i][0])

        @block.tensor
        def _(pe):
            pe.wait_ge(s["silu"], 1)
            for k in range(KD):
                pe.wait_ge(s["adar0" if k < 2 else "adar1" if k < 5 else "adar2"], 16)
                for n in range(4):
                    mm = pe.matmul(ps[0:2, 4 + n, :], silu_c[:, k, :], adar[:, k, n * 512:(n + 1) * 512], start=k == 0, stop=k == KD - 1)
            mm.then_inc(s["ada_used"], 1)
            pe.wait_ge(s["modr_d"], 1)
            for n in range(16):
                mm = pe.transpose(ps[:, 0, 2 * n:2 * n + 2], modr[:, n * P:(n + 1) * P], ident[0:2, 0:2])
            mm.then_inc(s["ada_used"], 1)

            def product(dst, a, b, k, n_k):
                for j, (x, y) in enumerate(((a[0], b[0]), (a[1], b[0]), (a[0], b[1]))):
                    mm = pe.matmul(dst, x, y, start=(k == 0 and j == 0), stop=(k == n_k - 1 and j == 2))
                return mm

            def gates(c, g):
                f, d = combos[c]
                pe.wait_ge(s["u_ready"], 1)
                pe.wait_ge(s["wg_load"], 32)
                if 2 * c + g:
                    pe.wait_ge(s["gate_sig"], 2 * c + g)
                for o, n, b in ((0, 512, 0), (512, 512, 1), (1024, UL - 1024, 2)):
                    mm = pe.matmul(ps[:, b, 0:n], wg[:, (f * 2 + d) * 2 + g, :], U[:, f, o:o + n], start=True, stop=True)
                mm.then_inc(s["gate_mm"], 1)

            order = [(i, k) for k in range(KD) for i in range(RING)] + [(i, k) for i in range(RING, NU) for k in range(KD)]
            for i, k in order:
                u = units[i]
                g = group[u[0]]
                if i >= RING and k == 0:
                    pe.wait_ge(s["proj_out"], i - RING + 1)
                pe.wait_ge(s["w_lo"], g * KD + k + 1)
                if g == 0:
                    pe.wait_ge(s["x_lo"], k + 1)
                if u[0] == "L":
                    _, f, o, n = u
                    cols = slice(f * P, (f + 1) * P)
                    a, b = (whi[:, k, cols], wlo[:, k, cols]), (xhi[:, k, o:o + n], xlo[:, k, o:o + n])
                else:
                    n = 256 if u[0] == "E" and u[1] >= ST else 512
                    cols = slice(u[1] * P, (u[1] + 1) * P)
                    a, b = (xhi[:, k, cols], xlo[:, k, cols]), (whi[:, k, 0:n], wlo[:, k, 0:n])
                mm = product(ps[:, 4 + i % RING, 0:n], a, b, k, KD)
                if i in last_of and k < KD - 1:
                    mm.then_inc(s["w_used"], 1)
                if k == KD - 1:
                    mm.then_inc(s["proj_done"], 1)
                    if i in gate_at:
                        gates(*gate_at[i])

        blk.close()

        mrow = sb("mrow", [P, 3, D], F32, attn)
        p2 = ExitStack()
        woh = sb("woh", [P, KD, D], F32R, attn)
        wol = sb("wol", [P, KD, D], F32R, attn)
        pv = ExitStack()
        wring = sb("wring", [P, 2, 2 * D], F32, pv)
        sbc = sb("sbc", [P, KD, P], F32, pv)
        pv.close()
        ysm = sb("ysm", [P, ST, GH * GD + DH * DV], F32, attn)
        pw = ExitStack()
        ring = sb("ring", [P, 2, 2048], F32, pw)
        pw.close()
        py = ExitStack()
        sub = sb("sub", [P, 2, ST * DH * DV], F32, py)
        subg = sb("subg", [P, DV], F32, py)
        rst = sb("rst", [P, 2, ST * DH], F32, py)
        py.close()
        pT = sb("pT", [P, 2, 512], F32, p2)
        pH = sb("pH", [P, 2, 512], F32R, p2)
        pL = sb("pL", [P, 2, 512], F32R, p2)
        OT = sb("OT", [P, S], F32, p2)
        Q1 = sb("Q1", [P, 2, S], F32R, p2)
        Q2 = sb("Q2", [P, 2, S], F32R, p2)
        K1 = sb("K1", [P, 2, T], F32R, p2)
        K2 = sb("K2", [P, 2, T], F32R, p2)
        qr = sb("qr", [P, ST, GD], F32, p2)
        kr = sb("kr", [P, TT, GD], F32, p2)
        qs = sb("qs", [P, ST, P], F32, p2)
        ks = sb("ks", [P, TT, P], F32, p2)
        MX = sb("MX", [P, ST], F32, p2)
        MX3 = sb("MX3", [P, ST, 3], F32, p2)
        MM = sb("MM", [P, ST, 2], F32R, p2)
        rec = sb("rec", [P, ST], F32, p2)
        pz = ExitStack()
        g2t = sb("g2t", [P, D], F32, pz)
        pz.close()
        od = sb("od", [P, 2, ST, DV], F32, p2)
        Vh = sb("Vh", [P, 2, TT, GD + 1], F32R, p2)
        Vl = sb("Vl", [P, 2, TT, GD], F32R, p2)
        p2.close()

        a2 = {n: sem(n) for n in (
            "g2_out", "phi_d", "plo_d", "plo_p", "vh_d", "mrow_in", "ring0", "ring1", "wring0", "wring1", "row_mm", "row_out", "wo_hi", "wo_lo", "bc_rdy", "m_part", "head_d", "rec_d", "subg_in", "lam_e",
            "qr_in", "kr_in", "dup", "tr_mm", "hi_d", "lo_d", "k2_cp", "max_mm", "max_red", "m_rdy", "mt_mm", "mt_cp",
            "s_mm", "exp_d", "pv_mm", "o_out", "acc_free", "ot_mm", "ones_d", "vs_d", "sub_sq", "sub_rt")}
        NROW = 8
        MAPS = GH + 2 * DH
        GROUP_HEADS = GH // GKV
        rounds = [(0, 0, 4), (0, 4, 4), (1, 0, 4), (1, 4, 4), (1, 8, 2)]
        NR = len(rounds)
        NS = 2 * TT
        chunks = [(0, 512), (512, 512), (1024, 256)]
        EARLY, ROW_SLOTS = 2, (1, 3, 5, 7, 9, 11)
        POOL_SOFT = (10, 12, 14, 16, 18)
        DVE_SOFT = tuple(u for u in range(NS) if u not in POOL_SOFT)

        class Kind:
            def __init__(self, w, rep, rows, scale):
                self.w, self.rep, self.rows, self.scale = w, rep, rows, scale

        gqa = Kind(GD, 2, 128, GD ** -0.5)
        dif = Kind(DQ, 3, 96, DQ ** -0.5)

        block = blk.enter_context(nc.Block())

        def soft_lo_ready(eng, G, u):
            name, mine = ("plo_p", POOL_SOFT) if u in POOL_SOFT else ("plo_d", DVE_SOFT)
            eng.wait_ge(a2[name], G * len(mine) + (mine.index(u) + 1))

        def soft_lo(eng, name, G, u):
            eng.wait_ge(a2["phi_d"], G * NS + (u + 1))
            eng.tensor_tensor(pL[:, u % 2, :], pT[:, u % 2, :], pH[:, u % 2, :].bitcast(F32), ALU.subtract).then_inc(a2[name], 1)

        @block.sync
        def _(sp):
            for i in range(2 * NROW):
                if i >= 2:
                    sp.wait_ge(a2["row_mm"], i - 1)
                n, kh = divmod(i, 2)
                src = A["ada_w"][kh * 512:(kh + 1) * 512, 2048 + n * 512:2048 + (n + 1) * 512]
                sp.dma_start(ring[:, i % 2, :].rearrange("p (k n) -> p k n", k=4), src.rearrange("(k p) n -> p k n", p=P)).then_inc(a2[f"ring{i % 2}"], 16)
                if i == 1:
                    sp.wait_ge(a2["dup"], 1)
                    sp.dma_start(qr[:, :, :], q_dram.rearrange("(t p) (h d) -> h p t d", p=P, d=GD)[0]).then_inc(a2["qr_in"], 16)
                    sp.dma_start(kr[:, :, :], k_dram.rearrange("(t p) (h d) -> h p t d", p=P, d=GD)[0]).then_inc(a2["kr_in"], 16)
                    sp.dma_start(mrow[:, :, :], A["adab_rows"][:, 0:3, :]).then_inc(a2["mrow_in"], 16)
                    sp.dma_start(g2t[:, :], A["adab_rows"][:, 3, :]).then_inc(a2["mrow_in"], 16)
            sp.wait_ge(a2["row_out"], NROW)
            sp.dma_start(g2_dram, g2t[:, :]).then_inc(a2["g2_out"], 16)

            def load(G, q_src, k_src):
                sp.wait_ge(a2["dup"], 2 * G + 1)
                sp.dma_start(qr[:, :, :], q_src).then_inc(a2["qr_in"], 16)
                sp.dma_start(kr[:, :, :], k_src).then_inc(a2["kr_in"], 16)

            q_v = q_dram.rearrange("(t p) (h d) -> h p t d", p=P, d=GD)
            k_v = k_dram.rearrange("(t p) (h d) -> h p t d", p=P, d=GD)
            dq_v = dq_dram.rearrange("(t p) (h d) -> h p t d", p=P, d=GD)
            one = lambda v, i: v[bass.ds(i, 1)].rearrange("o p t d -> (o p) t d")
            with sp.Fori(1, GH) as h:
                load(h, one(q_v, h), one(k_v, h // GROUP_HEADS))
            with sp.Fori(0, DH) as h:
                for m in range(2):
                    load(GH + 2 * h + m, one(dq_v, h), one(k_v, GKV + h))
            sp.wait_ge(a2["head_d"], DH)
            sp.dma_start(subg[:, :], A["subg"]).then_inc(a2["subg_in"], 16)

        @block.gpsimd
        def _(pool):
            pool.memset(K2[64:66, :, :].bitcast(F32), 1.0).then_inc(a2["dup"], 1)
            pool.wait_ge(a2["dup"], 1)
            def repeat(kind, G, m, first=False):
                if not first:
                    if kind is gqa:
                        wait_apart(pool, a2["k2_cp"], G * 3, passed)
                    wait_apart(pool, a2["lo_d"], G * NR, passed)
                for raw, dst, n, got in ((qr, qs, ST, "qr_in"), (kr, ks, TT, "kr_in")):
                    wait_apart(pool, a2[got], G * 16 + 16, passed)
                    pool.tensor_copy(dst[:, :, 0:kind.rep * kind.w].rearrange("p t (r w) -> p t r w", w=kind.w),
                                     raw[:, :, m * kind.w:(m + 1) * kind.w].unsqueeze(2).broadcast_to([P, n, kind.rep, kind.w]))\
                        .then_inc(a2["dup"], 1)

            def split_values(kind, G, par, vh, ones=False):
                wait_apart(pool, a2["tr_mm"], G * NR + 1, passed)
                src = (V if kind is gqa else DVt)[:, :, bass.ds(vh, 1), :].rearrange("p t o d -> p (t o) d")
                pool.tensor_copy(Vh[:, par, :, :], src).then_inc(a2["vh_d"], 1)
                wait_apart(pool, a2["vh_d"], G + 1, passed)
                pool.tensor_tensor(Vl[:, par, :, :], src[:, :, 0:GD], Vh[:, par, :, 0:GD].bitcast(F32), ALU.subtract).then_inc(a2["vs_d"], 1)
                if kind is gqa:
                    for r, (is_k, t0, nt) in enumerate(rounds):
                        if is_k:
                            if r == 2:
                                wait_apart(pool, a2["vs_d"], G + 1, passed)
                            else:
                                wait_apart(pool, a2["k2_cp"], G * 3 + r - 2, passed)
                            wait_apart(pool, a2["hi_d"], G * NR + r + 1, passed)
                            cols = slice(t0 * P, (t0 + nt) * P)
                            pool.tensor_copy(K2[0:64, par, cols], K1[0:64, par, cols].bitcast(F32)).then_inc(a2["k2_cp"], 1)
                if ones:
                    wait_apart(pool, a2["vs_d"], G + 1, passed)
                    pool.memset(K1[96:98, par, :].bitcast(F32), 1.0).then_inc(a2["ones_d"], 1)
                    pool.wait_ge(a2["ones_d"], par + 1)

            def soft_parts(G):
                for u in POOL_SOFT:
                    soft_lo(pool, "plo_p", G, u)

            repeat(gqa, 0, 0, first=True)
            split_values(gqa, 0, 0, 0)
            repeat(gqa, 1, 0)
            with pool.Fori(0, 3) as it:
                for par in range(2):
                    G = it * 2 + par
                    split_values(gqa, G + 1, 1 - par, (it + par) // 2)
                    repeat(gqa, G + 2, 0)
                    soft_parts(G)
            split_values(gqa, 7, 1, 1)
            pool.wait_ge(a2["k2_cp"], GH * 3)
            repeat(dif, GH, 0)
            soft_parts(6)
            split_values(dif, GH, 0, 0, ones=True)
            repeat(dif, GH + 1, 1)
            soft_parts(7)
            split_values(dif, GH + 1, 1, 0, ones=True)
            repeat(dif, GH + 2, 0)
            soft_parts(GH)
            split_values(dif, GH + 2, 0, 1)
            repeat(dif, GH + 3, 1)
            soft_parts(GH + 1)
            with pool.Fori(1, 3) as it:
                for par in range(2):
                    G = it * 2 + (GH + par)
                    split_values(dif, G + 1, 1 - par, it + par)
                    repeat(dif, G + 2, par)
                    soft_parts(G)
            split_values(dif, MAPS - 1, 1, DH - 1)
            soft_parts(MAPS - 2)
            soft_parts(MAPS - 1)

        @block.scalar
        def _(act):
            act.activation(lam[:, 2:4], lam[:, 0:2], ACT.Exp).then_inc(a2["lam_e"], 1)

            def load_wo(j):
                if j >= 2:
                    act.wait_ge(a2["wo_lo"], 2 * (j - 1))
                act.dma_start(wring[:, j % 2, :].rearrange("p (k n) -> p k n", k=2), A["w_out"][j * 256:(j + 1) * 256, :].rearrange("(k p) n -> p k n", p=P))\
                    .then_inc(a2[f"wring{j % 2}"], 16)

            load_wo(0)
            load_wo(1)
            for k in range(KD):
                act.wait_ge(a2[f"wring{k // 2 % 2}"], 16 * (k // 4 + 1))
                act.activation(woh[:, k, :], wring[:, k // 2 % 2, (k % 2) * D:(k % 2 + 1) * D], ACT.Copy).then_inc(a2["wo_hi"], 1)
                if k in (2, 4):
                    load_wo(k // 2 + 1)

            def hi(kind, G, par, r):
                is_k, t0, nt = rounds[r]
                dst = (K1 if is_k else Q1)[0:kind.rows, par, t0 * P:(t0 + nt) * P]
                act.wait_ge(a2["tr_mm"], G * NR + r + 1)
                act.activation(dst, ps[0:kind.rows, 4 + r % 3, 0:nt * P], ACT.Copy).then_inc(a2["hi_d"], 1)

            def soft(kind, G, nxt, Gn, par, first=False):
                for u in range(NS):
                    act.wait_ge(a2["s_mm"], G * NS + u + 1)
                    if u >= 2 or not first:
                        soft_lo_ready(act, G if u >= 2 else G - 1, (u - 2) % NS)
                    act.activation(pT[:, u % 2, :], ps[:, u % 2, :], ACT.Exp, scale=kind.scale).then_inc(a2["exp_d"], 1)
                    if nxt and 1 <= u <= NR:
                        hi(nxt, Gn, 1 - par, u - 1)
                    act.wait_ge(a2["exp_d"], G * NS + (u + 1))
                    if u >= 2 or not first:
                        act.wait_ge(a2["pv_mm"], G * NS + (u - 1))
                    act.activation(pH[:, u % 2, :], pT[:, u % 2, :], ACT.Copy).then_inc(a2["phi_d"], 1)

            for r in range(NR):
                hi(gqa, 0, 0, r)
            for kind, G0, after in ((gqa, 0, dif), (dif, GH, None)):
                for par in range(2):
                    soft(kind, G0 + par, kind, G0 + par + 1, par, first=(G0 + par == 0))
                with act.Fori(1, 3) as it:
                    for par in range(2):
                        soft(kind, it * 2 + (G0 + par), kind, it * 2 + (G0 + par + 1), par)
                soft(kind, G0 + 6, kind, G0 + 7, 0)
                soft(kind, G0 + 7, after, G0 + 8, 1)
            act.wait_ge(a2["sub_sq"], 1)
            act.activation(rst[:, 1, :], rst[:, 0, :], ACT.Sqrt).then_inc(a2["sub_rt"], 1)

        @block.vector
        def _(dve):
            ch = Chain(dve, s["dve_c"], dve_links)
            for k in range(KD):
                ins = dve.tensor_copy(sbc[:, k, :], silu_c[:, k, 0:1].broadcast_to([P, P]))
            ins.then_inc(a2["bc_rdy"], 1)
            dve.wait_ge(a2["lam_e"], 1)
            ch.link(dve.tensor_tensor(lam[:, 4:5], lam[:, 3:4], lam[:, 2:3], ALU.subtract))
            dve.tensor_scalar(lam[:, 5:6], lam[:, 4:5], LAM_INIT, None, ALU.subtract).then_inc(a2["o_out"], 1)
            dve.wait_ge(a2["mrow_in"], 32)
            def row(n):
                dve.wait_ge(a2["row_mm"], 2 * n + 2)
                m = (mrow[:, n // 2, :] if n < 6 else g2t[:, :])[:, (n % 2) * 512:(n % 2 + 1) * 512]
                dve.tensor_tensor(m, m, ps[:, n % 2, :], ALU.add).then_inc(a2["row_out"], 1)

            for k in range(KD):
                dve.wait_ge(a2["wo_hi"], k + 1)
                dve.tensor_tensor(wol[:, k, :], wring[:, k // 2 % 2, (k % 2) * D:(k % 2 + 1) * D], woh[:, k, :].bitcast(F32), ALU.subtract)\
                    .then_inc(a2["wo_lo"], 1)
                if k % (KD // EARLY) == KD // EARLY - 1:
                    row(k // (KD // EARLY))

            def lo(kind, G, par, r):
                is_k, t0, nt = rounds[r]
                cols = slice(t0 * P, (t0 + nt) * P)
                dve.wait_ge(a2["hi_d"], G * NR + r + 1)
                if kind is gqa:
                    rows = slice(64, 128) if is_k else slice(0, 64)
                    hi_part = (K1 if is_k else Q1)[rows, par, cols]
                    dst = (K1 if is_k else Q2)[rows, par, cols]
                else:
                    rows = slice(32, 64) if is_k else slice(64, 96)
                    hi_part = dst = (K1 if is_k else Q1)[rows, par, cols]
                dve.tensor_tensor(dst, ps[rows, 4 + r % 3, 0:nt * P], hi_part.bitcast(F32), ALU.subtract).then_inc(a2["lo_d"], 1)

            def maxima(G, j):
                for b, (o, n) in enumerate(chunks):
                    dve.wait_ge(a2["max_mm"], G * (3 * ST) + (3 * j + b + 1))
                    dve.tensor_reduce(MX3[:, j, b:b + 1], ps[:, 4 + b, 0:n], AX.X, ALU.max, negate=True).then_inc(a2["max_red"], 1)

            def max_parts(G):
                dve.wait_ge(a2["max_red"], G * (3 * ST) + 3 * ST)
                dve.tensor_reduce(MX[:, :], MX3[:, :, :], AX.X, ALU.min).then_inc(a2["m_part"], 1)
                dve.wait_ge(a2["m_part"], 2 * G + 1)
                dve.tensor_copy(MM[:, :, 0], MX[:, :]).then_inc(a2["m_part"], 1)
                dve.wait_ge(a2["m_part"], 2 * G + 2)
                dve.tensor_tensor(MM[:, :, 1], MX[:, :], MM[:, :, 0].bitcast(F32), ALU.subtract).then_inc(a2["m_rdy"], 1)

            def max_rows(kind, G, par, b):
                dve.wait_ge(a2["mt_mm"], G * 2 + b + 1)
                dst = Q2[64:66, par, b * 512:(b + 1) * 512] if kind is gqa else Q1[96:98, par, b * 512:(b + 1) * 512]
                dve.tensor_copy(dst, ps[0:2, 7, :]).then_inc(a2["mt_cp"], 1)

            def take(G, b):
                dve.wait_ge(a2["pv_mm"], G * NS + (NS - 1 + b))
                dve.tensor_copy(OT[0:GD + 1, b * 512:(b + 1) * 512], ps[0:GD + 1, 2 + b, :]).then_inc(a2["acc_free"], 1)

            def output(kind, G, par, col, b):
                acc = ps[:, 7, 0:4 * (GD + 1)].rearrange("p (j d) -> p j d", j=4)
                js = slice(4 * b, 4 * b + 4)
                dve.wait_ge(a2["ot_mm"], 2 * G + b + 1)
                dve.reciprocal(rec[:, js], acc[:, :, GD]).then_inc(a2["rec_d"], 1)
                dve.wait_ge(a2["rec_d"], 2 * G + b + 1)
                dst = ysm[:, js, bass.ds(col, GD)] if kind is gqa else od[:, par, js, :]
                dve.tensor_tensor(dst, acc[:, :, 0:GD], rec[:, js].unsqueeze(2).broadcast_to([P, 4, GD]), ALU.mult)\
                    .then_inc(a2["o_out"], 1)
                if kind is dif and par and b:
                    dve.wait_ge(a2["o_out"], 2 * G + 3)
                    dve.scalar_tensor_tensor(out=ysm[:, :, bass.ds(col, DV)], in0=od[:, 1, :, :], scalar=lam[:, 5:6], in1=od[:, 0, :, :],
                                             op0=ALU.mult, op1=ALU.add).then_inc(a2["head_d"], 1)

            def ahead(kind, G, par, u):
                if 1 <= u <= NR:
                    lo(kind, G, par, u - 1)
                elif NR < u <= NR + ST:
                    maxima(G, u - NR - 1)
                    if u == NR + ST:
                        max_parts(G)
                elif NR + ST + 2 <= u < NR + ST + 4:
                    max_rows(kind, G, par, u - NR - ST - 2)

            def step(kind, G, par, nxt, Gn, prev, prev_col):
                for u in range(NS):
                    if u in DVE_SOFT:
                        soft_lo(dve, "plo_d", G, u)
                    if nxt:
                        ahead(nxt, Gn, 1 - par, u)
                    if prev and u in (1, 3):
                        output(prev, G - 1, 1 - par, prev_col, u // 2)
                for b in range(2):
                    take(G, b)

            for u in range(NS):
                ahead(gqa, 0, 0, u)
                if u in ROW_SLOTS:
                    row(EARLY + ROW_SLOTS.index(u))
            dve.wait_ge(a2["row_out"], NROW)
            dve.tensor_scalar(mrow[:, 2, :], mrow[:, 2, :], 1.0, None, ALU.add).then_inc(a2["acc_free"], 2)
            dve.wait_ge(a2["g2_out"], 16)
            for kind, G0, before, after in ((gqa, 0, None, dif), (dif, GH, gqa, None)):
                wide = 2 * GD if kind is gqa else DV
                base = 0 if kind is gqa else GH * GD
                back = GD if kind is gqa else DV
                step(kind, G0, 0, kind, G0 + 1, before, (GH - 1) * GD)
                step(kind, G0 + 1, 1, kind, G0 + 2, kind, base)
                with dve.Fori(1, 3) as it:
                    for par in range(2):
                        step(kind, it * 2 + (G0 + par), par, kind, it * 2 + (G0 + par + 1), kind, it * wide + (base if par else base - back))
                step(kind, G0 + 6, 0, kind, G0 + 7, kind, 3 * wide + base - back)
                step(kind, G0 + 7, 1, after, G0 + 8, kind, 3 * wide + base)
            for b in range(2):
                output(dif, MAPS - 1, 1, GH * GD + (DH - 1) * DV, b)

            dve.wait_ge(a2["subg_in"], 16)
            dve.wait_ge(a2["head_d"], DH)
            sq = sub[:, 0, :].rearrange("p (t h d) -> p (t h) d", t=ST, h=DH)
            y3 = ysm[:, :, GH * GD:GH * GD + DH * DV]
            ch.link(dve.tensor_copy(sub[:, 0, :].rearrange("p (t c) -> p t c", t=ST), y3))
            ch.link(dve.tensor_tensor(sub[:, 1, :], sub[:, 0, :], sub[:, 0, :], ALU.mult))
            ch.link(dve.tensor_reduce(rst[:, 0, :], sub[:, 1, :].rearrange("p (g d) -> p g d", d=DV), AX.X, ALU.add))
            dve.tensor_scalar(rst[:, 0, :], rst[:, 0, :], 1.0 / DV, EPS, ALU.mult, ALU.add).then_inc(a2["sub_sq"], 1)
            dve.wait_ge(a2["sub_rt"], 1)
            ch.link(dve.reciprocal(rst[:, 0, :], rst[:, 1, :]))
            ch.link(dve.tensor_scalar(rst[:, 0, :], rst[:, 0, :], 1.0 - LAM_INIT, None, ALU.mult))
            ch.link(dve.tensor_tensor(sq, sq, rst[:, 0, :].unsqueeze(2).broadcast_to([P, ST * DH, DV]), ALU.mult))
            ch.link(dve.tensor_tensor(sq, sq, subg[:, :].unsqueeze(1).broadcast_to([P, ST * DH, DV]), ALU.mult))
            ch.link(dve.tensor_copy(y3, sub[:, 0, :].rearrange("p (t c) -> p t c", t=ST)))

        @block.tensor
        def _(pe):
            pe.wait_ge(a2["bc_rdy"], 1)

            def row(n):
                if n >= 2:
                    pe.wait_ge(a2["row_out"], n - 1)
                for k in range(KD):
                    i = 2 * n + k // 4
                    if k % 4 == 0:
                        pe.wait_ge(a2[f"ring{i % 2}"], 16 * (i // 2 + 1))
                    mm = pe.matmul(ps[:, n % 2, :], sbc[:, k, :], ring[:, i % 2, (k % 4) * 512:(k % 4 + 1) * 512],
                                   start=(k == 0), stop=(k == KD - 1))
                    if k % 4 == 3:
                        mm.then_inc(a2["row_mm"], 1)

            def transposes(kind, G, r):
                is_k, t0, nt = rounds[r]
                src = ks if is_k else qs
                if r == 0:
                    pe.wait_ge(a2["dup"], G * 2 + 2)
                if r == 2:
                    pe.wait_ge(a2["dup"], G * 2 + 3)
                if r >= 3:
                    pe.wait_ge(a2["lo_d"], G * NR + r - 2)
                for j in range(nt):
                    mm = pe.transpose(ps[0:kind.rows, 4 + r % 3, j * P:(j + 1) * P], src[:, t0 + j, 0:kind.rows], ident[:, :])
                mm.then_inc(a2["tr_mm"], 1)

            def max_tile(kind, G, par, j):
                if j == 0:
                    pe.wait_ge(a2["lo_d"], G * NR + NR)
                    if kind is gqa:
                        pe.wait_ge(a2["k2_cp"], G * 3 + 3)
                cols = slice(j * P, (j + 1) * P)
                for b, (o, n) in enumerate(chunks):
                    if j:
                        pe.wait_ge(a2["max_red"], G * (3 * ST) + (3 * j - 2 + b))
                    mm = pe.matmul(ps[:, 4 + b, 0:n], Q1[0:kind.rows, par, cols], K1[0:kind.rows, par, o:o + n],
                                   start=True, stop=kind is dif)
                    if kind is gqa:
                        mm = pe.matmul(ps[:, 4 + b, 0:n], Q2[0:64, par, cols], K2[0:64, par, o:o + n], start=False, stop=True)
                    mm.then_inc(a2["max_mm"], 1)

            def max_turn(G, b, first):
                if b == 0:
                    pe.wait_ge(a2["m_rdy"], G + 1)
                    if not first:
                        pe.wait_ge(a2["o_out"], G * 2 - 1)
                else:
                    pe.wait_ge(a2["mt_cp"], G * 2 + 1)
                for j in range(4):
                    mm = pe.transpose(ps[0:2, 7, j * P:(j + 1) * P], MM[:, b * 4 + j, :].bitcast(F32), ident[:, :])
                mm.then_inc(a2["mt_mm"], 1)

            def scores(kind, G, par, u, first=False):
                kt, qh = divmod(u, 2)
                if u == 0:
                    pe.wait_ge(a2["mt_cp"], G * 2 + 2)
                    if kind is dif:
                        pe.wait_ge(a2["ones_d"], par + 1)
                if u >= 2 or not first:
                    pe.wait_ge(a2["exp_d"], G * NS + (u - 1))
                keys, qrs = slice(kt * P, (kt + 1) * P), slice(qh * 512, (qh + 1) * 512)
                rows = 128 if kind is gqa else 98
                mm = pe.matmul(ps[:, u % 2, :], K1[0:rows, par, keys], Q1[0:rows, par, qrs], start=True, stop=kind is dif)
                if kind is gqa:
                    mm = pe.matmul(ps[:, u % 2, :], K2[0:66, par, keys], Q2[0:66, par, qrs], start=False, stop=True)
                mm.then_inc(a2["s_mm"], 1)

            def values(G, par, u, part):
                kt, qh = divmod(u, 2)
                if part == 0:
                    if u == 0:
                        pe.wait_ge(a2["vs_d"], G + 1)
                    if u < 2:
                        pe.wait_ge(a2["acc_free"], 2 * G + (1 + u))
                    pe.wait_ge(a2["phi_d"], G * NS + (u + 1))
                    pe.matmul(ps[0:GD + 1, 2 + qh, :], Vh[:, par, kt, :], pH[:, u % 2, :], start=kt == 0, stop=False)
                    pe.matmul(ps[0:GD, 2 + qh, :], Vl[:, par, kt, :], pH[:, u % 2, :], start=False, stop=False)
                else:
                    soft_lo_ready(pe, G, u)
                    pe.matmul(ps[0:GD + 1, 2 + qh, :], Vh[:, par, kt, :], pL[:, u % 2, :], start=False, stop=kt == TT - 1).then_inc(a2["pv_mm"], 1)

            def turn_back(G, b):
                pe.wait_ge(a2["acc_free"], 2 * G + (3 + b))
                if b == 1:
                    pe.wait_ge(a2["o_out"], 2 * G + 2)
                for j in range(4):
                    mm = pe.transpose(ps[:, 7, j * (GD + 1):(j + 1) * (GD + 1)], OT[0:GD + 1, (4 * b + j) * P:(4 * b + j + 1) * P],
                                      ident[0:GD + 1, 0:GD + 1])
                mm.then_inc(a2["ot_mm"], 1)

            def ahead(kind, G, par, u, first=False):
                if u < NR:
                    transposes(kind, G, u)
                elif NR < u <= NR + ST:
                    max_tile(kind, G, par, u - NR - 1)
                elif NR + ST + 2 <= u < NR + ST + 4:
                    max_turn(G, u - NR - ST - 2, first)

            def step(kind, G, par, nxt, Gn, prev):
                for u in range(NS):
                    if u:
                        values(G, par, u - 1, 1)
                    elif prev:
                        values(G - 1, 1 - par, NS - 1, 1)
                    if u + 2 < NS:
                        scores(kind, G, par, u + 2)
                    elif nxt:
                        scores(nxt, Gn, 1 - par, u + 2 - NS)
                    if nxt:
                        ahead(nxt, Gn, 1 - par, u)
                    values(G, par, u, 0)
                    if prev and u in (1, 3):
                        turn_back(G - 1, u // 2)

            for n in range(EARLY):
                row(n)
            for u in range(NS):
                ahead(gqa, 0, 0, u, first=True)
                if u in ROW_SLOTS:
                    row(EARLY + ROW_SLOTS.index(u))
            pe.wait_ge(a2["acc_free"], 2)
            for u in range(2):
                scores(gqa, 0, 0, u, first=True)
            for kind, G0, after in ((gqa, 0, dif), (dif, GH, None)):
                for par in range(2):
                    step(kind, G0 + par, par, kind, G0 + par + 1, G0 + par > 0)
                with pe.Fori(1, 3) as it:
                    for par in range(2):
                        step(kind, it * 2 + (G0 + par), par, kind, it * 2 + (G0 + par + 1), True)
                step(kind, G0 + 6, 0, kind, G0 + 7, True)
                step(kind, G0 + 7, 1, after, G0 + 8, True)
            values(MAPS - 1, 1, NS - 1, 1)
            for b in range(2):
                turn_back(MAPS - 1, b)
        blk.close()

        p3 = ExitStack()
        yTh = sb("yTh", [P, 2, KD, P], F32R, p3)
        yTl = sb("yTl", [P, 2, KD, P], F32R, p3)
        xt = sb("xt", [P, 2, D], F32, p3)
        ln1 = sb("ln1", [P, 2, D], F32, p3)
        res = sb("res", [P, D], F32, p3)
        x1 = sb("x1", [P, 2, D], F32, p3)
        hh = sb("hh", [P, 2, D], F32, p3)
        hT = sb("hT", [P, KD, P], F32, p3)
        rw = sb("rw", [P, KD, E], F32, p3)
        rb = sb("rb", [P, E], F32, p3)
        st3 = sb("st3", [P, 2, 16], F32, p3)
        tri = sb("tri", [P, 2, P], F32, p3)
        kc = sb("kc", [P, 8 + NBLK + 2], F32, p3)
        rt = sb("rt", [P, 12, ST * E], F32, p3)
        rsm = sb("rsm", [P, 16, ST], F32, p3)
        ecmp = sb("ecmp", [P, E * (NBLK + 2)], F32, p3)
        zrow = sb("zrow", [P, (NBLK + 1)], I32, p3)
        zeros = sb("zeros", [P, D], F32, p3)
        tokid = sb("tokid", [P, ST], I32, p3)
        p3.close()

        a3 = {n: sem(n) for n in (
            "c3_in", "y_zero", "xt0", "xt1", "yt_mm", "yt_hi", "yt_lo", "ya_lo", "y_mm", "y_ev", "ln_sq", "ln_rt", "x1g", "x1_done",
            "h_mul", "h_done", "x1_out0", "x1_out1", "h_out0", "h_out1", "ht_mm", "ht_cp", "lg_mm", "sm_in",
            "sm_ex", "mask_d", "cnt_mm", "z_in", "z_out", "dest_d", "scat")}
        block = blk.enter_context(nc.Block())

        @block.sync
        def _(sp):
            for dst, name in ((ln1[:, :, :], "ln1"), (rw[:, :, :], "rw"), (rb[:, :], "rb"), (tri[:, :, :], "tri"), (kc[:, :], "kc")):
                sp.dma_start(dst, A[name]).then_inc(a3["c3_in"], 16)
            def load_x(t):
                sp.dma_start(xt[:, t % 2, :], A["x"][t * P:(t + 1) * P, :]).then_inc(a3[f"xt{t % 2}"], 16)

            load_x(0)
            load_x(1)
            sp.wait_ge(a3["z_in"], 1)
            sp.dma_start(rows_dram.rearrange("(p n) o -> p (n o)", p=P), zrow[:, :]).then_inc(a3["z_out"], 16)
            for t in range(ST):
                if t + 2 < ST:
                    sp.wait_ge(a3["y_ev"], t + 1)
                    load_x(t + 2)
                for b in range(MINBLK + 2 * t, min(MINBLK + 2 * t + 2, NBLK + 1)):
                    sp.dma_start(y_dram[b * BLK:(b + 1) * BLK, :], zeros[:, :]).then_inc(a3["y_zero"], 16)
                sp.wait_ge(a3["x1_done"], t + 1)
                sp.dma_start(x1_dram[t * P:(t + 1) * P, :], x1[:, t % 2, :]).then_inc(a3[f"x1_out{t % 2}"], 16)
                sp.wait_ge(a3["h_done"], t + 1)
                sp.dma_start(h_dram[t * P:(t + 1) * P, :], hh[:, t % 2, :]).then_inc(a3[f"h_out{t % 2}"], 16)
            sp.wait_ge(a3["y_zero"], 16 * (NBLK + 1 - MINBLK))
            for b in range(2):
                sp.wait_ge(a3[f"x1_out{b}"], 16 * ST // 2)
                sp.wait_ge(a3[f"h_out{b}"], 16 * ST // 2)

        @block.gpsimd
        def _(pool):
            pool.memset(zrow[:, :], 0)
            pool.memset(zeros[:, :], 0.0).then_inc(a3["z_in"], 1)
            pool.iota(tokid[:, :], [[P, ST]], base=0, channel_multiplier=1).then_inc(a3["z_in"], 1)
            pool.wait_ge(a3["c3_in"], 16 * 5)

            def ya_part(t):
                pool.wait_ge(a3["yt_hi"], t + 1)
                if t >= 2:
                    pool.wait_ge(a3["y_mm"], t - 1)
                pool.tensor_tensor(yTl[:, t % 2, 0:LF, :], ya[:, :, t * P:(t + 1) * P], yTh[:, t % 2, 0:LF, :].bitcast(F32), ALU.subtract)\
                    .then_inc(a3["ya_lo"], 1)

            ya_part(0)
            for t in range(ST):
                if t + 1 < ST:
                    ya_part(t + 1)
                pool.wait_ge(a3["x1g"], t + 1)
                pool.tensor_tensor(x1[:, t % 2, :], x1[:, t % 2, :], ln1[:, 1, :], ALU.add).then_inc(a3["x1_done"], 1)
                pool.wait_ge(a3["x1_done"], t + 1)
                if t >= 2:
                    pool.wait_ge(a3[f"h_out{t % 2}"], 16 * (t // 2))
                    pool.wait_ge(a3["ht_mm"], t - 1)
                pool.tensor_tensor(hh[:, t % 2, :], x1[:, t % 2, :], mrow[:, 2, :], ALU.mult).then_inc(a3["h_mul"], 1)
            pool.wait_ge(a3["z_out"], 16)
            pool.wait_ge(a3["dest_d"], 1)
            pool.wait_ge(a3["z_in"], 2)
            for t in range(ST):
                for c in range(2):
                    pool.indirect_dma_start(rows_dram, bass.IndirectOffsetOnAxis(ap=dest[:, c, t:t + 1], axis=0), tokid[:, t:t + 1], None)\
                        .then_inc(a3["scat"], 16)
            pool.wait_ge(a3["scat"], 16 * 2 * ST)

        @block.scalar
        def _(act):
            def hi_parts(t):
                act.wait_ge(a3["yt_mm"], t + 1)
                if t >= 2:
                    act.wait_ge(a3["y_mm"], t - 1)
                act.activation(yTh[:, t % 2, LF:KD, :].rearrange("p k m -> p (k m)"), ps[:, 0:2, :].rearrange("p a b -> p (a b)")[:, 0:(KD - LF) * P], ACT.Copy)
                act.activation(yTh[:, t % 2, 0:LF, :], ya[:, :, t * P:(t + 1) * P], ACT.Copy).then_inc(a3["yt_hi"], 1)

            def h_copy(t):
                act.wait_ge(a3["ht_mm"], t + 1)
                if t >= 1:
                    act.wait_ge(a3["lg_mm"], t)
                act.activation(hT[:, :, :].rearrange("p k m -> p (k m)"), ps[:, 6:8, :].rearrange("p a b -> p (a b)"), ACT.Copy).then_inc(a3["ht_cp"], 1)

            hi_parts(0)
            for t in range(ST):
                if t + 1 < ST:
                    hi_parts(t + 1)
                if t:
                    h_copy(t - 1)
                act.wait_ge(a3["ln_sq"], t + 1)
                act.activation(st3[:, t % 2, 14:15], st3[:, t % 2, 13:14], ACT.Sqrt).then_inc(a3["ln_rt"], 1)
            h_copy(ST - 1)
            act.wait_ge(a3["sm_in"], 1)
            act.activation(rt[:, 1, :], rt[:, 0, :], ACT.Exp).then_inc(a3["sm_ex"], 1)

        @block.vector
        def _(dve):
            ch = Chain(dve, s["dve_c"], dve_links)
            dve.wait_ge(a3["c3_in"], 16 * 5)

            def lo_part(t):
                dve.wait_ge(a3["yt_hi"], t + 1)
                dve.tensor_tensor(yTl[:, t % 2, LF:KD, :].rearrange("p k m -> p (k m)"), ps[:, 0:2, :].rearrange("p a b -> p (a b)")[:, 0:(KD - LF) * P],
                                  yTh[:, t % 2, LF:KD, :].rearrange("p k m -> p (k m)").bitcast(F32), ALU.subtract).then_inc(a3["yt_lo"], 1)

            def shift_h(t):
                dve.wait_ge(a3["h_mul"], t + 1)
                dve.tensor_tensor(hh[:, t % 2, :], hh[:, t % 2, :], mrow[:, 1, :], ALU.add).then_inc(a3["h_done"], 1)

            lo_part(0)
            for t in range(ST):
                if t + 1 < ST:
                    lo_part(t + 1)
                if t:
                    shift_h(t - 1)
                s_ = st3[:, t % 2, :]
                dve.wait_ge(a3["y_mm"], t + 1)
                ch.link(dve.tensor_tensor(res[:, :].rearrange("p (a b) -> p a b", a=2), ps[:, 2:4, :],
                                          mrow[:, 0, :].rearrange("p (a b) -> p a b", a=2), ALU.mult))
                dve.wait_ge(a3[f"xt{t % 2}"], 16 * (t // 2 + 1))
                dve.scalar_tensor_tensor(out=res[:, :], in0=xt[:, t % 2, :], scalar=ALPHA, in1=res[:, :], op0=ALU.mult, op1=ALU.add)\
                    .then_inc(a3["y_ev"], 1)
                dve.wait_ge(a3["y_ev"], t + 1)
                for b in range(2):
                    ins = dve.bn_stats(s_[:, 6 * b:6 * b + 6], res[:, b * 512:(b + 1) * 512])
                ch.link(ins)
                ch.link(dve.bn_aggr(s_[:, 12:14], s_[:, 0:12]))
                dve.tensor_scalar(s_[:, 13:14], s_[:, 13:14], EPS, None, ALU.add).then_inc(a3["ln_sq"], 1)
                dve.wait_ge(a3["ln_rt"], t + 1)
                ch.link(dve.reciprocal(s_[:, 15:16], s_[:, 14:15]))
                ch.link(dve.tensor_scalar(res[:, :], res[:, :], s_[:, 12:13], s_[:, 15:16], ALU.subtract, ALU.mult))
                if t >= 2:
                    dve.wait_ge(a3[f"x1_out{t % 2}"], 16 * (t // 2))
                    dve.wait_ge(a3["h_mul"], t - 1)
                dve.tensor_tensor(x1[:, t % 2, :], res[:, :], ln1[:, 0, :], ALU.mult).then_inc(a3["x1g"], 1)
                dve.wait_ge(a3["x1g"], t + 1)
            shift_h(ST - 1)

            def v(i, pat="p (t e) -> p t e", **k):
                return rt[:, i, :].rearrange(pat, **(k or dict(t=ST)))

            TG = ST * G
            dve.wait_ge(a3["lg_mm"], ST)
            lg = ps[:, 4, 0:ST * E].rearrange("p (t e) -> p t e", t=ST)
            ch.link(dve.tensor_reduce(rsm[:, 0, :], lg, AX.X, ALU.max))
            dve.tensor_tensor(v(0), lg, rsm[:, 0, :].unsqueeze(2).broadcast_to([P, ST, E]), ALU.subtract).then_inc(a3["sm_in"], 1)
            dve.wait_ge(a3["sm_ex"], 1)
            ch.link(dve.tensor_reduce(rsm[:, 1, :], v(1), AX.X, ALU.add))
            ch.link(dve.reciprocal(rsm[:, 2, :], rsm[:, 1, :]))
            ch.link(dve.tensor_tensor(v(1), v(1), rsm[:, 2, :].unsqueeze(2).broadcast_to([P, ST, E]), ALU.mult))
            ch.link(dve.tensor_tensor(v(2), v(1), rb[:, :].unsqueeze(1).broadcast_to([P, ST, E]), ALU.add))

            def ranks(score, rank, tmp, n, w):
                for i in range(w):
                    ins = dve.memset(rank[:, :, i:i + 1], float(w - 1 - i))
                ch.link(ins)
                for d in range(1, w):
                    t_ = tmp[:, :, 0:w - d]
                    ch.link(dve.tensor_tensor(t_, score[:, :, 0:w - d], score[:, :, d:w], ALU.is_ge))
                    ch.link(dve.tensor_tensor(rank[:, :, d:w], rank[:, :, d:w], t_, ALU.add))
                    ch.link(dve.tensor_tensor(rank[:, :, 0:w - d], rank[:, :, 0:w - d], t_, ALU.subtract))

            g4 = lambda i: rt[:, i, :].rearrange("p (g c) -> p g c", c=EG)
            ranks(g4(2), g4(3), g4(4), TG, EG)
            ch.link(dve.tensor_scalar(rt[:, 3, :], rt[:, 3, :], 1.5, None, ALU.is_lt))
            ch.link(dve.tensor_tensor(rt[:, 4, :], rt[:, 2, :], rt[:, 3, :], ALU.mult))
            ch.link(dve.tensor_reduce(rt[:, 5, 0:TG], g4(4), AX.X, ALU.add))
            gg = lambda i: rt[:, i, 0:TG].rearrange("p (t g) -> p t g", g=G)
            ranks(gg(5), gg(6), gg(7), ST, G)
            ch.link(dve.tensor_scalar(rt[:, 6, 0:TG], rt[:, 6, 0:TG], 0.5, None, ALU.is_lt))
            dve.tensor_tensor(g4(3), g4(3), rt[:, 6, 0:TG].unsqueeze(2).broadcast_to([P, TG, EG]), ALU.mult).then_inc(a3["mask_d"], 1)
            dve.wait_ge(a3["mask_d"], 1)
            ch.link(dve.tensor_tensor(rt[:, 1, :], rt[:, 1, :], rt[:, 3, :], ALU.mult))
            ch.link(dve.tensor_reduce(rsm[:, 3, :], v(1), AX.X, ALU.add))
            ch.link(dve.reciprocal(rsm[:, 4, :], rsm[:, 3, :]))
            ch.link(dve.tensor_tensor(v(1), v(1), rsm[:, 4, :].unsqueeze(2).broadcast_to([P, ST, E]), ALU.mult))
            dve.wait_ge(a3["cnt_mm"], 1)
            ch.link(dve.tensor_copy(rt[:, 8, :], ps[:, 6, 0:ST * E]))
            ch.link(dve.memset(rt[:, 9, 0:E], 0.0))
            for t in range(ST):
                dst = rt[:, 9, (t + 1) * E:(t + 2) * E] if t + 1 < ST else rt[:, 10, 0:E]
                ch.link(dve.tensor_tensor(dst, rt[:, 9, t * E:(t + 1) * E], rt[:, 8, t * E:(t + 1) * E], ALU.add))
            ch.link(dve.tensor_tensor(ecmp[:, 0:E * 8].rearrange("p (e j) -> p e j", j=8), rt[:, 10, 0:E].unsqueeze(2).broadcast_to([P, E, 8]),
                                      kc[:, 0:8].unsqueeze(1).broadcast_to([P, E, 8]), ALU.is_gt))
            ch.link(dve.tensor_reduce(rt[:, 10, 16:32], ecmp[:, 0:E * 8].rearrange("p (e j) -> p e j", j=8), AX.X, ALU.add))
            ch.link(dve.memset(rt[:, 10, 32:48], 1.0))
            ch.link(dve.tensor_tensor_scan(rt[:, 10, 48:64], rt[:, 10, 32:48], rt[:, 10, 16:32], 0.0, ALU.mult, ALU.add))
            ch.link(dve.tensor_tensor(rt[:, 10, 64:80], rt[:, 10, 48:64], rt[:, 10, 16:32], ALU.subtract))
            ch.link(dve.tensor_scalar(rt[:, 10, 64:80], rt[:, 10, 64:80], float(BLK), None, ALU.mult))
            nb = NBLK + 2
            ch.link(dve.tensor_tensor(ecmp[:, 0:nb * E].rearrange("p (b e) -> p b e", e=E), rt[:, 10, 48:64].unsqueeze(1).broadcast_to([P, nb, E]),
                                      kc[:, 8:8 + nb].unsqueeze(2).broadcast_to([P, nb, E]), ALU.is_le))
            ch.link(dve.tensor_reduce(rt[:, 11, 0:nb], ecmp[:, 0:nb * E].rearrange("p (b e) -> p b e", e=E), AX.X, ALU.add))
            ch.link(dve.tensor_scalar(rt[:, 11, 0:nb], rt[:, 11, 0:nb], float(E - 1), None, ALU.min))
            ch.link(dve.tensor_copy(blk_tab[:, 0:nb], rt[:, 11, 0:nb]))
            ch.link(dve.tensor_copy(blk_tab[:, nb:nb + 1], rt[:, 10, 63:64]))
            ch.link(dve.tensor_tensor(v(9), v(9), rt[:, 10, 64:80].unsqueeze(1).broadcast_to([P, ST, E]), ALU.add))
            dve.wait_ge(a3["cnt_mm"], 2)
            ch.link(dve.tensor_tensor(rt[:, 9, :], rt[:, 9, :], ps[:, 7, 0:ST * E], ALU.add))
            ch.link(dve.tensor_tensor(rt[:, 9, :], rt[:, 9, :], rt[:, 3, :], ALU.mult))
            ch.link(dve.tensor_reduce(rsm[:, 5, :], v(9), AX.X, ALU.max))
            ch.link(dve.tensor_reduce(rsm[:, 6, :], v(9), AX.X, ALU.add))
            ch.link(dve.tensor_tensor(rsm[:, 6, :], rsm[:, 6, :], rsm[:, 5, :], ALU.subtract))
            ch.link(dve.tensor_tensor(v(8), v(9), rsm[:, 5, :].unsqueeze(2).broadcast_to([P, ST, E]), ALU.is_equal))
            ch.link(dve.tensor_tensor(rt[:, 8, :], rt[:, 8, :], rt[:, 1, :], ALU.mult))
            ch.link(dve.tensor_reduce(gates[:, 0, :], v(8), AX.X, ALU.add))
            ch.link(dve.tensor_tensor(rt[:, 1, :], rt[:, 1, :], rt[:, 8, :], ALU.subtract))
            ch.link(dve.tensor_reduce(gates[:, 1, :], v(1), AX.X, ALU.add))
            ch.link(dve.tensor_copy(dest[:, 0, :], rsm[:, 5, :]))
            dve.tensor_copy(dest[:, 1, :], rsm[:, 6, :]).then_inc(a3["dest_d"], 1)

        @block.tensor
        def _(pe):
            def turn_y(t):
                if t:
                    pe.wait_ge(a3["yt_lo"], t)
                for j in range(KD - LF):
                    mm = pe.transpose(ps[:, j // 4, (j % 4) * P:(j % 4 + 1) * P], ysm[:, t, j * P:(j + 1) * P], ident[:, :])
                mm.then_inc(a3["yt_mm"], 1)

            def project(t):
                pe.wait_ge(a3["yt_lo"], t + 1)
                pe.wait_ge(a3["ya_lo"], t + 1)
                if t:
                    pe.wait_ge(a3["y_ev"], t)
                for b in range(2):
                    cols = slice(b * 512, (b + 1) * 512)
                    for k in range(KD):
                        for j, (x, y) in enumerate(((yTh, woh), (yTl, woh), (yTh, wol))):
                            mm = pe.matmul(ps[:, 2 + b, :], x[:, t % 2, k, :], y[:, k, cols], start=(k == 0 and j == 0), stop=(k == KD - 1 and j == 2))
                mm.then_inc(a3["y_mm"], 1)

            def turn_h(t):
                pe.wait_ge(a3["h_done"], t + 1)
                if t:
                    pe.wait_ge(a3["ht_cp"], t)
                for k in range(KD):
                    mm = pe.transpose(ps[:, 6 + k // 4, (k % 4) * P:(k % 4 + 1) * P], hh[:, t % 2, k * P:(k + 1) * P], ident[:, :])
                mm.then_inc(a3["ht_mm"], 1)

            def route(t):
                pe.wait_ge(a3["ht_cp"], t + 1)
                pe.wait_ge(a3["c3_in"], 16 * 5)
                for k in range(KD):
                    mm = pe.matmul(ps[:, 4, t * E:(t + 1) * E], hT[:, k, :], rw[:, k, :], start=(k == 0), stop=(k == KD - 1))
                mm.then_inc(a3["lg_mm"], 1)

            turn_y(0)
            for t in range(ST):
                if t + 1 < ST:
                    turn_y(t + 1)
                project(t)
                if t:
                    turn_h(t - 1)
                    route(t - 1)
            turn_h(ST - 1)
            route(ST - 1)
            pe.wait_ge(a3["mask_d"], 1)
            for j, b in ((1, 6), (0, 7)):
                pe.matmul(ps[:, b, 0:ST * E], tri[:, j, :], rt[:, 3, :], start=True, stop=True).then_inc(a3["cnt_mm"], 1)
        blk.close()
        attn.close()

        p4 = ExitStack()
        wraw4 = sb("wraw4", [P, NUNIT, D], F32, p4)
        whi4 = sb("whi4", [P, NUNIT, D], F32R, p4)
        wlo4 = sb("wlo4", [P, NUNIT, D], F32R, p4)
        xg = sb("xg", [P, D], F32, p4)
        xTh = sb("xTh", [P, KD, P], F32R, p4)
        xTl = sb("xTl", [P, KD, P], F32R, p4)
        hs = sb("hs", [P, FF], F32, p4)
        hTh = sb("hTh", [P, FK, P], F32R, p4)
        hTl = sb("hTl", [P, FK, P], F32R, p4)
        ys = sb("ys", [P, D], F32, p4)
        g2row = sb("g2row", [P, D], F32, p4)
        row_all = sb("row_all", [P, NBLK + 1], I32, p4)
        row_ix = sb("row_ix", [P, 2], I32, p4)
        tok4 = sb("tok4", [P, 2], F32, p4)
        p4.close()
        a4 = {n: sem(n) for n in (
            *(f"raw{p}" for p in range(NUNIT // 2)), "rows_in", "g2_in", "gu_mm", "whi_d", "wlo_d", "wlo_p", "used", "xg_in", "ix_d", "xt_mm", "xt_hi", "xt_lo",
            "silu_d", "mul_d", "ht_mm4", "ht_hi4", "ht_lo4", "y_ev4", "y_free")}
        block = blk.enter_context(nc.Block())
        POOL_UNITS = (1, 4, 7, 10)
        DVE_UNITS = tuple(u for u in range(NUNIT) if u not in POOL_UNITS)

        def ht_bank(half):
            return ps[:, 0 if half else 4, 0:2 * P]

        def ht_part(t, half):
            return t[:, 2 * half:2 * half + 2, :].rearrange("p k m -> p (k m)")

        def lo_ready(eng, b, u, apart=False):
            name, mine = ("wlo_p", POOL_UNITS) if u in POOL_UNITS else ("wlo_d", DVE_UNITS)
            count = b * len(mine) + (mine.index(u) + 1)
            if apart:
                wait_apart(eng, a4[name], count, passed)
            else:
                eng.wait_ge(a4[name], count)

        def expert(eng, b):
            return eng.value_load(blk_tab[0:1, bass.ds(b, 1)], min_val=0, max_val=E - 1)

        def keep(eng, name, b, n):
            wait_apart(eng, a4[name], b * n, passed)
            eng.sem_inc(a4[name], n)

        def block_count(eng):
            return eng.value_load(blk_tab[0:1, NBLK + 2:NBLK + 3], min_val=1, max_val=NBLK)

        def lo_unit(eng, name, b, u):
            eng.wait_ge(a4["whi_d"], b * NUNIT + (u + 1))
            eng.tensor_tensor(wlo4[:, u, :], wraw4[:, u, :], whi4[:, u, :].bitcast(F32), ALU.subtract).then_inc(a4[name], 1)

        @block.sync
        def _(sp):
            def load(b, p):
                e = expert(sp, b)
                sp.dma_start(wraw4[:, 2 * p:2 * p + 2, :], A["wexp"][bass.ds(e, 1), :, 2 * p:2 * p + 2, :].rearrange("o p u n -> p (o u) n"))\
                    .then_inc(a4[f"raw{p}"], 16)

            sp.dma_start(row_all[:, :], rows_dram.rearrange("(b p) o -> p (b o)", p=P), allow_slow_non_contiguous=True).then_inc(a4["rows_in"], 16)
            for p in range(NUNIT // 2):
                load(0, p)
            sp.dma_start(g2row[:, :], g2_dram).then_inc(a4["g2_in"], 16)
            e0, e1 = (sp.value_load(blk_tab[0:1, b:b + 1], min_val=0, max_val=E - 1) for b in range(2))
            with sp.If(e0 != e1):
                for p in range(NUNIT // 2):
                    lo_ready(sp, 0, 2 * p)
                    lo_ready(sp, 0, 2 * p + 1)
                    load(1, p)
            with sp.Else():
                for p in range(NUNIT // 2):
                    sp.wait_ge(a4[f"raw{p}"], 16)
                    sp.sem_inc(a4[f"raw{p}"], 16)
            nb = block_count(sp)
            with sp.Fori(0, NBLK) as b:
                with sp.If(b < nb):
                    now, then = expert(sp, b + 1), expert(sp, b + 2)
                    with sp.If(now != then):
                        for p in range(NUNIT // 2):
                            lo_ready(sp, b + 1, 2 * p, apart=True)
                            lo_ready(sp, b + 1, 2 * p + 1, apart=True)
                            load(b + 2, p)
                    with sp.Else():
                        for p in range(NUNIT // 2):
                            wait_apart(sp, a4[f"raw{p}"], b * 16 + 32, passed)
                            sp.sem_inc(a4[f"raw{p}"], 16)
                    sp.wait_ge(a4["y_ev4"], b + 2)
                    sp.dma_start(y_dram[bass.ds(b * BLK, BLK), :], ys[:, :]).then_inc(a4["y_free"], 16)
            wait_apart(sp, a4["y_free"], nb * 16 + 16, passed)
            for p in range(NUNIT // 2):
                wait_apart(sp, a4[f"raw{p}"], nb * 16 + 32, passed)

        @block.gpsimd
        def _(pool):
            def gather(b, col):
                pool.tensor_copy(row_ix[:, 0:1], col).then_inc(a4["ix_d"], 1)
                wait_apart(pool, a4["ix_d"], b + 1, passed)
                pool.indirect_dma_start(xg[:, :], None, h_dram, bass.IndirectOffsetOnAxis(ap=row_ix[:, 0:1], axis=0)).then_inc(a4["xg_in"], 16)

            pool.wait_ge(a4["rows_in"], 16)
            gather(0, row_all[:, 0:1])
            for u in POOL_UNITS:
                lo_unit(pool, "wlo_p", 0, u)
            nb = block_count(pool)
            with pool.Fori(0, NBLK) as b:
                with pool.If(b < nb):
                    wait_apart(pool, a4["xt_mm"], b + 1, passed)
                    gather(b + 1, row_all[:, bass.ds(b + 1, 1)])
                    now, then = expert(pool, b), expert(pool, b + 1)
                    with pool.If(now != then):
                        for u in POOL_UNITS:
                            lo_unit(pool, "wlo_p", b + 1, u)
                    with pool.Else():
                        keep(pool, "wlo_p", b + 1, len(POOL_UNITS))

        @block.scalar
        def _(act):
            def hi_unit(b, u, first=False):
                act.wait_ge(a4[f"raw{u // 2}"], b * 16 + 16)
                if not first and u == KD - 1:
                    act.wait_ge(a4["gu_mm"], (b - 1) * 3 + 3)
                elif not first:
                    act.wait_ge(a4["used"], (b - 1) * (NUNIT - 1) + (u + (1 if u < KD else 0)))
                act.activation(whi4[:, u, :], wraw4[:, u, :], ACT.Copy).then_inc(a4["whi_d"], 1)

            def xt_hi(b):
                act.wait_ge(a4["xt_mm"], b + 1)
                act.activation(xTh[:, :, :].rearrange("p k m -> p (k m)"), ps[:, 2:4, :].rearrange("p a b -> p (a b)"), ACT.Copy)\
                    .then_inc(a4["xt_hi"], 1)

            act.wait_ge(a4["y_ev4"], 1)
            act.activation(tok4[:, 0:1], tok4[:, 0:1], ACT.Silu)
            for u in range(NUNIT):
                hi_unit(0, u, first=True)
                if u == 3:
                    xt_hi(0)
            nb = block_count(act)
            with act.Fori(0, NBLK) as b:
                with act.If(b < nb):
                    def body(fresh):
                        act.wait_ge(a4["gu_mm"], b * 3 + 1)
                        act.activation(hs[:, :], ps[:, 0, :], ACT.Silu).then_inc(a4["silu_d"], 1)
                        for u in range(NUNIT if fresh else 4):
                            if u in (2, 3):
                                act.wait_ge(a4["ht_mm4"], b * 2 + (u - 1))
                                act.activation(ht_part(hTh, u - 2), ht_bank(u - 2), ACT.Copy).then_inc(a4["ht_hi4"], 1)
                            if u == 3:
                                xt_hi(b + 1)
                            if fresh:
                                hi_unit(b + 1, u)

                    now, then = expert(act, b), expert(act, b + 1)
                    with act.If(now != then):
                        body(True)
                    with act.Else():
                        body(False)
                        keep(act, "whi_d", b + 1, NUNIT)

        @block.vector
        def _(dve):
            def xt_lo(b):
                dve.wait_ge(a4["xt_hi"], b + 1)
                dve.tensor_tensor(xTl[:, :, :].rearrange("p k m -> p (k m)"), ps[:, 2:4, :].rearrange("p a b -> p (a b)"),
                                  xTh[:, :, :].rearrange("p k m -> p (k m)").bitcast(F32), ALU.subtract).then_inc(a4["xt_lo"], 1)

            dve.memset(tok4[:, 0:1], 0.0).then_inc(a4["y_ev4"], 1)
            dve.memset(tok4[:, 1:2], 0.0).then_inc(a4["y_free"], 16)
            for u in DVE_UNITS:
                lo_unit(dve, "wlo_d", 0, u)
                if u == 3:
                    xt_lo(0)
            dve.wait_ge(a4["g2_in"], 16)
            nb = block_count(dve)
            with dve.Fori(0, NBLK) as b:
                with dve.If(b < nb):
                    def body(fresh):
                        def mul(half):
                            cols = slice(half * 256, half * 256 + 256)
                            dve.wait_ge(a4["gu_mm"], b * 3 + (2 + half))
                            dve.tensor_tensor(hs[:, cols], hs[:, cols], ps[:, 7 if half else 1, 0:256], ALU.mult).then_inc(a4["mul_d"], 1)

                        dve.wait_ge(a4["silu_d"], b + 1)
                        mul(0)
                        for u in DVE_UNITS if fresh else (2,):
                            if u == 2:
                                mul(1)
                                for half in range(2):
                                    dve.wait_ge(a4["ht_hi4"], b * 2 + (half + 1))
                                    dve.tensor_tensor(ht_part(hTl, half), ht_bank(half), ht_part(hTh, half).bitcast(F32), ALU.subtract)\
                                        .then_inc(a4["ht_lo4"], 1)
                                xt_lo(b + 1)
                            if fresh:
                                lo_unit(dve, "wlo_d", b + 1, u)

                    now, then = expert(dve, b), expert(dve, b + 1)
                    with dve.If(now != then):
                        body(True)
                    with dve.Else():
                        body(False)
                        keep(dve, "wlo_d", b + 1, len(DVE_UNITS))
                    dve.wait_ge(a4["used"], b * (NUNIT - 1) + (NUNIT - 1))
                    dve.wait_ge(a4["y_free"], b * 16 + 16)
                    dve.tensor_tensor(ys[:, :].rearrange("p (a b) -> p a b", a=2), ps[:, 5:7, :], g2row[:, :].rearrange("p (a b) -> p a b", a=2), ALU.mult)\
                        .then_inc(a4["y_ev4"], 1)

        @block.tensor
        def _(pe):
            def turn_x(b, first=False):
                pe.wait_ge(a4["xg_in"], b * 16 + 16)
                if not first:
                    pe.wait_ge(a4["xt_lo"], b)
                for k in range(KD):
                    mm = pe.transpose(ps[:, 2 + k // 4, (k % 4) * P:(k % 4 + 1) * P], xg[:, k * P:(k + 1) * P], ident[:, :])
                mm.then_inc(a4["xt_mm"], 1)

            def product(b, u, lhs_hi, lhs_lo, dst, cols, first, last):
                for j, (x, y) in enumerate(((lhs_hi, whi4), (lhs_lo, whi4), (lhs_hi, wlo4))):
                    mm = pe.matmul(dst, x, y[:, u, cols], start=first and j == 0, stop=last and j == 2)
                return mm

            turn_x(0, first=True)
            nb = block_count(pe)
            with pe.Fori(0, NBLK) as b:
                with pe.If(b < nb):
                    pe.wait_ge(a4["xt_lo"], b + 1)
                    for part, (bank, cols) in enumerate(((0, slice(0, FF)), (1, slice(FF, FF + 256)), (7, slice(FF + 256, 2 * FF)))):
                        for k in range(KD):
                            if part == 0:
                                lo_ready(pe, b, k)
                            mm = product(b, k, xTh[:, k, :], xTl[:, k, :], ps[:, bank, 0:cols.stop - cols.start], cols, k == 0, k == KD - 1)
                            if part == 2 and k < KD - 1:
                                mm.then_inc(a4["used"], 1)
                        mm.then_inc(a4["gu_mm"], 1)

                    def turn_h(half):
                        pe.wait_ge(a4["mul_d"], b * 2 + (half + 1))
                        for j in range(2):
                            k = 2 * half + j
                            mm = pe.transpose(ht_bank(half)[:, j * P:(j + 1) * P], hs[:, k * P:(k + 1) * P], ident[:, :])
                        mm.then_inc(a4["ht_mm4"], 1)

                    turn_h(0)
                    turn_x(b + 1)
                    turn_h(1)
                    pe.wait_ge(a4["y_ev4"], b + 1)
                    for k in range(FK):
                        if k % 2 == 0:
                            pe.wait_ge(a4["ht_lo4"], b * 2 + (k // 2 + 1))
                        lo_ready(pe, b, KD + k)
                        for half in range(2):
                            mm = product(b, KD + k, hTh[:, k, :], hTl[:, k, :], ps[:, 5 + half, :], slice(half * 512, half * 512 + 512), k == 0, k == FK - 1)
                        mm.then_inc(a4["used"], 1)
        blk.close()

        p5 = ExitStack()
        yg = sb("yg", [P, 3, 2, D], F32, p5)
        x1t = sb("x1t", [P, 3, D], F32, p5)
        r5 = sb("r5", [P, 2, D], F32, p5)
        o5 = sb("o5", [P, 2, D], F32, p5)
        ln2 = sb("ln2", [P, 2, D], F32, p5)
        st5 = sb("st5", [P, 2, 16], F32, p5)
        p5.close()
        a5 = {n: sem(n) for n in ("c5_in", "yg0", "yg1", "yg2", "x1t0", "x1t1", "x1t2", "y_sum", "row_d", "neg_d", "var_d", "root_d", "norm_d", "gain_d", "fin_d",
                                  "fin_out0", "fin_out1")}
        block = blk.enter_context(nc.Block())

        @block.sync
        def _(sp):
            sp.dma_start(ln2[:, :, :], A["ln2"]).then_inc(a5["c5_in"], 16)

            def load_x1(t):
                sp.dma_start(x1t[:, t % 3, :], x1_dram[t * P:(t + 1) * P, :]).then_inc(a5[f"x1t{t % 3}"], 16)

            for t in range(3):
                load_x1(t)
            for t in range(ST):
                if t + 3 < ST:
                    sp.wait_ge(a5["y_sum"], t + 1)
                    load_x1(t + 3)
                sp.wait_ge(a5["fin_d"], t + 1)
                sp.dma_start(out[0, t * P:(t + 1) * P, :], o5[:, t % 2, :]).then_inc(a5[f"fin_out{t % 2}"], 16)
            for b in range(2):
                sp.wait_ge(a5[f"fin_out{b}"], 16 * (ST // 2))

        @block.gpsimd
        def _(pool):
            def gather(t):
                if t >= 3:
                    pool.wait_ge(a5["y_sum"], t - 2)
                for c in range(2):
                    pool.indirect_dma_start(yg[:, t % 3, c, :], None, y_dram, bass.IndirectOffsetOnAxis(ap=dest[:, c, t:t + 1], axis=0))\
                        .then_inc(a5[f"yg{t % 3}"], 16)

            for t in range(3):
                gather(t)
            pool.wait_ge(a5["c5_in"], 16)
            for t in range(ST):
                pool.wait_ge(a5["norm_d"], t + 1)
                if t >= 2:
                    pool.wait_ge(a5[f"fin_out{t % 2}"], 16 * (t // 2))
                pool.tensor_tensor(o5[:, t % 2, :], r5[:, t % 2, :], ln2[:, 0, :], ALU.mult).then_inc(a5["gain_d"], 1)
                if t + 3 < ST:
                    gather(t + 3)

        @block.scalar
        def _(act):
            def first_row(t):
                act.wait_ge(a5[f"yg{t % 3}"], 32 * (t // 3 + 1))
                if t >= 2:
                    act.wait_ge(a5["gain_d"], t - 1)
                act.activation(r5[:, t % 2, :], yg[:, t % 3, 0, :], ACT.Copy, scale=gates[:, 0, t:t + 1]).then_inc(a5["row_d"], 1)

            first_row(0)
            for t in range(ST):
                s_ = st5[:, t % 2, :]
                if t + 1 < ST:
                    first_row(t + 1)
                act.wait_ge(a5["var_d"], t + 1)
                act.activation(s_[:, 14:15], s_[:, 13:14], ACT.Sqrt).then_inc(a5["root_d"], 1)
                act.wait_ge(a5["neg_d"], t + 1)
                act.activation(r5[:, t % 2, :], r5[:, t % 2, :], ACT.Identity, bias=s_[:, 12:13], scale=s_[:, 15:16]).then_inc(a5["norm_d"], 1)

        @block.vector
        def _(dve):
            ch = Chain(dve, s["dve_c"], dve_links)
            dve.wait_ge(a5["c5_in"], 16)

            def shift(t):
                dve.wait_ge(a5["gain_d"], t + 1)
                dve.tensor_tensor(o5[:, t % 2, :], o5[:, t % 2, :], ln2[:, 1, :], ALU.add).then_inc(a5["fin_d"], 1)

            for t in range(ST):
                s_, r = st5[:, t % 2, :], r5[:, t % 2, :]
                dve.wait_ge(a5["row_d"], t + 1)
                ch.link(dve.scalar_tensor_tensor(out=r, in0=yg[:, t % 3, 1, :], scalar=gates[:, 1, t:t + 1], in1=r, op0=ALU.mult, op1=ALU.add))
                dve.wait_ge(a5[f"x1t{t % 3}"], 16 * (t // 3 + 1))
                dve.scalar_tensor_tensor(out=r, in0=x1t[:, t % 3, :], scalar=ALPHA, in1=r, op0=ALU.mult, op1=ALU.add).then_inc(a5["y_sum"], 1)
                dve.wait_ge(a5["y_sum"], t + 1)
                for b in range(2):
                    ins = dve.bn_stats(s_[:, 6 * b:6 * b + 6], r5[:, t % 2, b * 512:(b + 1) * 512])
                ch.link(ins)
                ch.link(dve.bn_aggr(s_[:, 12:14], s_[:, 0:12]))
                dve.tensor_scalar(s_[:, 13:14], s_[:, 13:14], EPS, None, ALU.add).then_inc(a5["var_d"], 1)
                if t:
                    shift(t - 1)
                dve.wait_ge(a5["root_d"], t + 1)
                ch.link(dve.reciprocal(s_[:, 15:16], s_[:, 14:15]))
                dve.tensor_scalar(s_[:, 12:13], s_[:, 12:13], s_[:, 15:16], -1.0, ALU.mult, ALU.mult).then_inc(a5["neg_d"], 1)
            shift(ST - 1)
        blk.close()


def layouts(inputs):
    import numpy as np
    a = {k: np.asarray(v) for k, v in inputs.items()}
    o = {}
    o["xT"] = np.concatenate([a["x"][0], a["ctx"][0]], 0).T
    o["x"] = a["x"][0]
    o["cvec"] = np.stack([a["c"][0], a["c_ctx"]], -1).reshape(KD, P, 2).transpose(1, 0, 2)
    o["ada_w"] = a["ada_w"][0]
    o["adab_cols"] = a["ada_b"][0][0:2048].reshape(16, P).T
    o["adab_rows"] = np.broadcast_to(a["ada_b"][0][2048:], (P, 4096)).reshape(P, 4, D)
    w = a["w_in"][0]
    ax_, ag, gq, gk, gv, dq, dk, dv = np.split(w, np.cumsum([256, 256, 512, 128, 128, 256, 256]).tolist(), axis=1)
    o["w_in"] = np.concatenate([ax_, ag, gq, gv, gk, dk, dv, dq], 1)
    o["ident"] = np.eye(P, dtype=np.float32)

    def rope(dim):
        t = np.arange(S)
        n = dim // 4
        inv = np.float32(10000.0) ** (-np.arange(n, dtype=np.float32) / np.float32(n))
        ang = np.concatenate([(t // 64).astype(np.float32)[:, None] * inv, (t % 64).astype(np.float32)[:, None] * inv], -1)
        c, s_ = np.cos(ang), np.sin(ang)
        tab = np.stack([np.stack([c, c], -1).reshape(S, dim), np.stack([-s_, s_], -1).reshape(S, dim)], 1)
        return tab.reshape(ST, P, 2, dim).transpose(1, 0, 2, 3).astype(np.float32)

    o["rope_g"], o["rope_d"] = rope(GD), rope(DQ)
    swap = np.arange(GD).reshape(-1, 2)[:, ::-1].reshape(-1)
    o["gvec"] = np.broadcast_to(np.stack([np.stack([g[0], g[0][swap]]) for g in (a["q_norm_g"], a["k_norm_g"])]), (P, 2, 2, GD))
    o["lvec"] = np.broadcast_to(a["diff_lambda"][0], (P, 4, DQ))
    cols = [a["conv_w"][0][k] for k in range(4)] + [a["conv_b"][0]] + [a[n][0][d] for n in ("rg_ba", "rg_bx", "rg_lam") for d in range(2)]
    cols += [cols[0]] * 5
    o["lruc"] = np.stack(cols, -1).reshape(LF, P, 16).transpose(1, 0, 2)
    g = np.stack([a["rg_wa"][0], a["rg_wx"][0]], 1)
    g = g.reshape(2, 2, LF, 2, 64, 64)
    o["wg"] = g.transpose(3, 4, 2, 0, 1, 5).reshape(2, 64, 8, 64)
    o["subg"] = np.broadcast_to(a["diff_subln_g"][0], (P, DV))
    o["w_out"] = a["w_out"][0]
    o["ln1"] = np.broadcast_to(np.stack([a["ln1_g"][0], a["ln1_b"][0]]), (P, 2, D))
    o["rw"] = a["router_w"].reshape(KD, P, E).transpose(1, 0, 2)
    o["rb"] = np.broadcast_to(a["router_b"], (P, E))
    o["tri"] = np.stack([np.triu(np.ones((P, P), np.float32), 1), np.ones((P, P), np.float32)], 1)
    o["kc"] = np.broadcast_to(np.concatenate([np.arange(8) * BLK, np.arange(NBLK + 2)]).astype(np.float32), (P, 8 + NBLK + 2))
    gu = np.concatenate([a["exp_w_gate"][0], a["exp_w_up"][0]], -1).reshape(E, KD, P, D)
    o["wexp"] = np.concatenate([gu, a["exp_w_down"][0].reshape(E, FK, P, D)], 1).transpose(0, 2, 1, 3)
    o["ln2"] = np.broadcast_to(np.stack([a["ln2_g"][0], a["ln2_b"][0]]), (P, 2, D))
    return {k: np.ascontiguousarray(v) for k, v in o.items()}


def kernel(**inputs):
    import concourse.bacc as bacc
    from concourse.bass_utils import run_bass_kernel_spmd
    nc = bacc.Bacc("TRN2", target_bir_lowering=False, num_devices=1)
    arrays = layouts(inputs)
    A = {n: nc.dram_tensor(f"in_{n}", v.shape, mybir.dt.from_np(v.dtype), kind="ExternalInput").ap() for n, v in arrays.items()}
    out = nc.dram_tensor("out", (1, S, D), F32, kind="ExternalOutput").ap()
    build(nc, A, out)
    r = run_bass_kernel_spmd(nc, [{f"in_{n}": v for n, v in arrays.items()}], core_ids=[0])
    return r.results[0]["out"]
```
